# Optimizing a Trainium2 kernel written in Bass

```python
import math
import jax, jax.numpy as jnp
from jax import lax
import numpy as np

D_MODEL = 1024
BATCH = 1
SEQ = 256
DEPTH = 2

GRID_W = 64
CTX_LEN = 256
HEAD_DIM = 64
A_HEADS = 8
A_KV_HEADS = 2
B_HEADS = 8
NB_KH_MAX = 8
NB_KW = 16
C_HEADS = 16
C_KV_HEADS = 2
C_WINDOW = 128
Q_BLOCK = 128
D_FF = 2816
CONV_W = 3
ROPE_THETA = 10000.0
LN_EPS = 1e-5
RMS_EPS = 1e-6
NEG = -1e30
DN_ALPHA = (2 * DEPTH) ** 0.25
DN_BETA = (8 * DEPTH) ** -0.25
N_EVEN = (DEPTH + 1) // 2
N_ODD = DEPTH // 2
A_Q = A_HEADS * HEAD_DIM
A_KV = A_KV_HEADS * HEAD_DIM
B_W = B_HEADS * HEAD_DIM
EVEN_IN = A_Q + 2 * A_KV + 3 * B_W
EVEN_MIX = A_Q + B_W
C_Q = C_HEADS * HEAD_DIM
C_KV = C_KV_HEADS * HEAD_DIM
ODD_IN = C_Q + 2 * C_KV
ODD_MIX = C_Q


def layer_norm(x, g, b):
    xf = x.astype(jnp.float32)
    mu = jnp.mean(xf, -1, keepdims=True)
    var = jnp.mean(jnp.square(xf - mu), -1, keepdims=True)
    return ((xf - mu) * lax.rsqrt(var + LN_EPS) * g + b).astype(x.dtype)

def rms_norm(x, g):
    xf = x.astype(jnp.float32)
    return (xf * lax.rsqrt(jnp.mean(xf * xf, -1, keepdims=True) + RMS_EPS) * g).astype(x.dtype)

def axial_rope_tables(n_tokens):
    t = jnp.arange(n_tokens, dtype=jnp.int32)
    row = (t // GRID_W).astype(jnp.float32)
    col = (t % GRID_W).astype(jnp.float32)
    half = HEAD_DIM // 2
    inv_freq = ROPE_THETA ** (-jnp.arange(0, half, 2, dtype=jnp.float32) / half)
    ang_r = row[:, None] * inv_freq
    ang_c = col[:, None] * inv_freq
    ang = jnp.concatenate([ang_r, ang_r, ang_c, ang_c], -1)
    return jnp.cos(ang), jnp.sin(ang)

def apply_rope(x, cos, sin):
    x1, x2, x3, x4 = jnp.split(x, 4, axis=-1)
    rot = jnp.concatenate([-x2, x1, -x4, x3], -1)
    return (x * cos[None, :, None, :] + rot * sin[None, :, None, :]).astype(x.dtype)

def heads(z, n):
    return z.reshape(z.shape[0], z.shape[1], n, HEAD_DIM)

def modulate(x, shift, scale):
    return x * (1 + scale) + shift

def gqa_scores(q, k):
    return jnp.einsum('bqkgd,btkd->bkgqt', q, k).astype(jnp.float32)

def gqa_out(p, v):
    return jnp.einsum('bkgqt,btkd->bqkgd', p.astype(v.dtype), v)

def global_gqa(q_lat, k_lat, v_lat, q_ctx, k_ctx, v_ctx, ctx_out):
    B, S, H, d = q_lat.shape
    KV = k_lat.shape[2]
    G = H // KV
    scale = d ** -0.5
    k_all = jnp.concatenate([k_ctx, k_lat], 1)
    v_all = jnp.concatenate([v_ctx, v_lat], 1)
    qb = (q_lat * scale).reshape(B, S // Q_BLOCK, Q_BLOCK, KV, G, d).swapaxes(0, 1)

    def block(q):
        p = jax.nn.softmax(gqa_scores(q, k_all), axis=-1)
        return gqa_out(p, v_all)

    o = lax.map(block, qb)
    y_lat = o.swapaxes(0, 1).reshape(B, S, H * d)
    y_ctx = None
    if ctx_out:
        qc = (q_ctx * scale).reshape(B, q_ctx.shape[1], KV, G, d)
        p = jax.nn.softmax(gqa_scores(qc, k_ctx), axis=-1)
        y_ctx = gqa_out(p, v_ctx).reshape(B, q_ctx.shape[1], H * d)
    return y_lat, y_ctx

def neighbourhood_attention(q_lat, k_lat, v_lat, q_ctx, k_ctx, v_ctx, rpb, ctx_out):
    B, S, H, d = q_lat.shape
    rows = S // GRID_W
    kh = min(NB_KH_MAX, rows)
    rb = Q_BLOCK // GRID_W
    scale = d ** -0.5
    col = jnp.arange(GRID_W)
    cs = jnp.clip(col - NB_KW // 2, 0, GRID_W - NB_KW)
    kcol = cs[:, None] + jnp.arange(NB_KW)
    dcol = kcol - col[:, None]
    qb = (q_lat * scale).reshape(B, rows // rb, rb, GRID_W, H, d).swapaxes(0, 1)
    n_nb = kh * NB_KW

    def block(args):
        qblk, blk = args
        row = blk * rb + jnp.arange(rb)
        rs = jnp.clip(row - kh // 2, 0, rows - kh)
        krow = rs[:, None] + jnp.arange(kh)
        drow = krow - row[:, None]
        idx = krow[:, None, :, None] * GRID_W + kcol[None, :, None, :]
        kn = k_lat[:, idx]
        vn = v_lat[:, idx]
        bias = rpb[:, drow[:, None, :, None] + NB_KH_MAX - 1, dcol[None, :, None, :] + NB_KW - 1]
        s_nb = jnp.einsum('brwhd,brwyxhd->bhrwyx', qblk, kn).astype(jnp.float32) + bias[None]
        s_nb = s_nb.reshape(B, H, rb, GRID_W, n_nb)
        s_ctx = jnp.einsum('brwhd,bthd->bhrwt', qblk, k_ctx).astype(jnp.float32)
        p = jax.nn.softmax(jnp.concatenate([s_nb, s_ctx], -1), axis=-1)
        p_nb = p[..., :n_nb].reshape(B, H, rb, GRID_W, kh, NB_KW).astype(vn.dtype)
        p_ctx = p[..., n_nb:].astype(v_ctx.dtype)
        return (jnp.einsum('bhrwyx,brwyxhd->brwhd', p_nb, vn)
                + jnp.einsum('bhrwt,bthd->brwhd', p_ctx, v_ctx))

    o = lax.map(block, (qb, jnp.arange(rows // rb)))
    y_lat = o.swapaxes(0, 1).reshape(B, S, H * d)
    y_ctx = None
    if ctx_out:
        s = jnp.einsum('bqhd,bthd->bhqt', q_ctx * scale, k_ctx).astype(jnp.float32)
        p = jax.nn.softmax(s, axis=-1).astype(v_ctx.dtype)
        y_ctx = jnp.einsum('bhqt,bthd->bqhd', p, v_ctx).reshape(B, q_ctx.shape[1], H * d)
    return y_lat, y_ctx

def window_gqa_sink(q_lat, k_lat, v_lat, q_ctx, k_ctx, v_ctx, sink, ctx_out):
    B, S, H, d = q_lat.shape
    KV = k_lat.shape[2]
    G = H // KV
    C = k_ctx.shape[1]
    scale = d ** -0.5
    span = Q_BLOCK + 2 * C_WINDOW
    pad = ((0, 0), (C_WINDOW, C_WINDOW), (0, 0), (0, 0))
    kp = jnp.pad(k_lat, pad)
    vp = jnp.pad(v_lat, pad)
    sink5 = sink.astype(jnp.float32).reshape(1, KV, G, 1, 1)
    qb = (q_lat * scale).reshape(B, S // Q_BLOCK, Q_BLOCK, KV, G, d).swapaxes(0, 1)
    qpos = jnp.arange(Q_BLOCK)
    kpos = jnp.arange(span) - C_WINDOW
    sink_q = jnp.broadcast_to(sink5, (B, KV, G, Q_BLOCK, 1))

    def block(args):
        q, blk = args
        start = blk * Q_BLOCK
        kb = lax.dynamic_slice_in_dim(kp, start, span, axis=1)
        vb = lax.dynamic_slice_in_dim(vp, start, span, axis=1)
        abs_k = start + kpos
        valid = ((jnp.abs(kpos[None, :] - qpos[:, None]) <= C_WINDOW)
                 & ((abs_k >= 0) & (abs_k < S))[None, :])
        s_loc = jnp.where(valid, gqa_scores(q, kb), NEG)
        s_ctx = gqa_scores(q, k_ctx)
        p = jax.nn.softmax(jnp.concatenate([s_loc, s_ctx, sink_q], -1), axis=-1)
        return gqa_out(p[..., :span], vb) + gqa_out(p[..., span:span + C], v_ctx)

    o = lax.map(block, (qb, jnp.arange(S // Q_BLOCK)))
    y_lat = o.swapaxes(0, 1).reshape(B, S, H * d)
    y_ctx = None
    if ctx_out:
        qc = (q_ctx * scale).reshape(B, C, KV, G, d)
        s = jnp.concatenate([gqa_scores(qc, k_ctx), jnp.broadcast_to(sink5, (B, KV, G, C, 1))], -1)
        p = jax.nn.softmax(s, axis=-1)
        y_ctx = gqa_out(p[..., :C], v_ctx).reshape(B, C, H * d)
    return y_lat, y_ctx

def even_project(h, w_in, q_gain, k_gain):
    qa, ka, va, qb, kb, vb = jnp.split(
        h @ w_in, [A_Q, A_Q + A_KV, A_Q + 2 * A_KV, A_Q + 2 * A_KV + B_W, A_Q + 2 * A_KV + 2 * B_W], axis=-1)
    return (rms_norm(heads(qa, A_HEADS), q_gain), rms_norm(heads(ka, A_KV_HEADS), k_gain),
            heads(va, A_KV_HEADS), heads(qb, B_HEADS), heads(kb, B_HEADS), heads(vb, B_HEADS))

def even_mixer(h_lat, h_ctx, w_in, w_out, q_gain, k_gain, rpb, cos, sin, ctx_out):
    qa, ka, va, qb, kb, vb = even_project(h_lat, w_in, q_gain, k_gain)
    qa_c, ka_c, va_c, qb_c, kb_c, vb_c = even_project(h_ctx, w_in, q_gain, k_gain)
    qa = apply_rope(qa, cos, sin)
    ka = apply_rope(ka, cos, sin)
    ya, ya_c = global_gqa(qa, ka, va, qa_c, ka_c, va_c, ctx_out)
    yb, yb_c = neighbourhood_attention(qb, kb, vb, qb_c, kb_c, vb_c, rpb, ctx_out)
    y_lat = jnp.concatenate([ya, yb], -1) @ w_out
    y_ctx = (jnp.concatenate([ya_c, yb_c], -1) @ w_out) if ctx_out else None
    return y_lat, y_ctx

def odd_project(h, w_in):
    q, k, v = jnp.split(h @ w_in, [C_Q, C_Q + C_KV], axis=-1)
    return heads(q, C_HEADS), heads(k, C_KV_HEADS), heads(v, C_KV_HEADS)

def odd_mixer(h_lat, h_ctx, w_in, w_out, sink, cos, sin, ctx_out):
    q, k, v = odd_project(h_lat, w_in)
    qc, kc, vc = odd_project(h_ctx, w_in)
    q = apply_rope(q, cos, sin)
    k = apply_rope(k, cos, sin)
    y, yc = window_gqa_sink(q, k, v, qc, kc, vc, sink, ctx_out)
    return y @ w_out, ((yc @ w_out) if ctx_out else None)

def conv_ffn(h, w_up, conv_w, conv_b, w_down):
    u = h @ w_up
    L = u.shape[1]
    r = CONV_W // 2
    up = jnp.pad(u, ((0, 0), (r, r), (0, 0)))
    acc = conv_b
    for j in range(CONV_W):
        acc = acc + up[:, j:j + L] * conv_w[j]
    a, g = jnp.split(acc, 2, axis=-1)
    return (jax.nn.silu(g) * a) @ w_down

def first_inputs(seed: int = 0) -> dict:
    key = jax.random.key(seed)
    ks = jax.random.split(key, 24)
    nrm = jax.random.normal
    f32 = jnp.float32
    return {
        'x': nrm(ks[0], (BATCH, SEQ, D_MODEL), f32),
        'c': nrm(ks[1], (BATCH, D_MODEL), f32),
        'ctx': nrm(ks[2], (BATCH, CTX_LEN, D_MODEL), f32),
        'c_ctx': nrm(ks[3], (D_MODEL,), f32),
        'ada_w': nrm(ks[4], (DEPTH, D_MODEL, 6 * D_MODEL), f32) * (0.5 * D_MODEL ** -0.5),
        'ada_b': nrm(ks[5], (DEPTH, 6 * D_MODEL), f32) * 0.02,
        'ln_g': 1.0 + 0.02 * nrm(ks[6], (DEPTH, 2, D_MODEL), f32),
        'ln_b': 0.02 * nrm(ks[7], (DEPTH, 2, D_MODEL), f32),
        'ev_w_in': nrm(ks[8], (N_EVEN, D_MODEL, EVEN_IN), f32) * D_MODEL ** -0.5,
        'ev_w_out': nrm(ks[9], (N_EVEN, EVEN_MIX, D_MODEL), f32) * (EVEN_MIX ** -0.5 * DN_BETA),
        'ev_q_gain': 1.0 + 0.02 * nrm(ks[10], (N_EVEN, HEAD_DIM), f32),
        'ev_k_gain': 1.0 + 0.02 * nrm(ks[11], (N_EVEN, HEAD_DIM), f32),
        'ev_rpb': 0.5 * nrm(ks[12], (N_EVEN, B_HEADS, 2 * NB_KH_MAX - 1, 2 * NB_KW - 1), f32),
        'od_w_in': nrm(ks[13], (N_ODD, D_MODEL, ODD_IN), f32) * D_MODEL ** -0.5,
        'od_w_out': nrm(ks[14], (N_ODD, ODD_MIX, D_MODEL), f32) * (ODD_MIX ** -0.5 * DN_BETA),
        'od_sink': nrm(ks[15], (N_ODD, C_HEADS), f32),
        'ffn_w_up': nrm(ks[16], (DEPTH, D_MODEL, 2 * D_FF), f32) * D_MODEL ** -0.5,
        'ffn_conv_w': nrm(ks[17], (DEPTH, CONV_W, 2 * D_FF), f32) * CONV_W ** -0.5,
        'ffn_conv_b': 0.02 * nrm(ks[18], (DEPTH, 2 * D_FF), f32),
        'ffn_w_down': nrm(ks[19], (DEPTH, D_FF, D_MODEL), f32) * (D_FF ** -0.5 * DN_BETA),
    }

def first_block(x, c, ctx, c_ctx, ada_w, ada_b, ln_g, ln_b, ev_w_in, ev_w_out, ev_q_gain, ev_k_gain, ev_rpb,
              od_w_in, od_w_out, od_sink, ffn_w_up, ffn_conv_w, ffn_conv_b, ffn_w_down):
    S = x.shape[1]
    cos, sin = axial_rope_tables(S)
    x_lat, x_ctx = x, ctx
    for l in range(DEPTH):
        ctx_out = l < DEPTH - 1
        i = l // 2
        m_lat = [m[:, None, :] for m in jnp.split(jax.nn.silu(c) @ ada_w[l] + ada_b[l], 6, axis=-1)]
        m_ctx = jnp.split(jax.nn.silu(c_ctx) @ ada_w[l] + ada_b[l], 6, axis=-1)
        h_lat = modulate(x_lat, m_lat[0], m_lat[1])
        h_ctx = modulate(x_ctx, m_ctx[0], m_ctx[1])
        if l % 2 == 0:
            y_lat, y_ctx = even_mixer(h_lat, h_ctx, ev_w_in[i], ev_w_out[i], ev_q_gain[i], ev_k_gain[i],
                                      ev_rpb[i], cos, sin, ctx_out)
        else:
            y_lat, y_ctx = odd_mixer(h_lat, h_ctx, od_w_in[i], od_w_out[i], od_sink[i], cos, sin, ctx_out)
        x_lat = layer_norm(DN_ALPHA * x_lat + m_lat[2] * y_lat, ln_g[l, 0], ln_b[l, 0])
        f_lat = conv_ffn(modulate(x_lat, m_lat[3], m_lat[4]), ffn_w_up[l], ffn_conv_w[l], ffn_conv_b[l], ffn_w_down[l])
        x_lat = layer_norm(DN_ALPHA * x_lat + m_lat[5] * f_lat, ln_g[l, 1], ln_b[l, 1])
        if ctx_out:
            x_ctx = layer_norm(DN_ALPHA * x_ctx + m_ctx[2] * y_ctx, ln_g[l, 0], ln_b[l, 0])
            f_ctx = conv_ffn(modulate(x_ctx, m_ctx[3], m_ctx[4]), ffn_w_up[l], ffn_conv_w[l], ffn_conv_b[l], ffn_w_down[l])
            x_ctx = layer_norm(DN_ALPHA * x_ctx + m_ctx[5] * f_ctx, ln_g[l, 1], ln_b[l, 1])
    return x_lat


EPS = 1e-6
CONV_CH = 512
CONV_WIDTH = 31
N_HEADS = 8
V_DIM = 2 * HEAD_DIM
QK_W = N_HEADS * 2 * HEAD_DIM
ATTN_W = N_HEADS * V_DIM
ROPE_BASE = 10000.0
POOL_CH = 512
POOL_WINDOWS = (2, 4, 8, 16)
POOL_GROUP = POOL_CH // len(POOL_WINDOWS)
N_BRANCH = 3
D_FF_2 = -(-(8 * D_MODEL) // (3 * 256)) * 256
N_MOD = 6
COL_A = 0
COL_Q = COL_A + 2 * CONV_CH
COL_K = COL_Q + QK_W
COL_V = COL_K + QK_W
COL_P = COL_V + ATTN_W
COL_G = COL_P + POOL_CH
IN_W = COL_G + N_BRANCH * D_MODEL


def rms_norm_2(x, g):
    x32 = x.astype(jnp.float32)
    y = x32 * lax.rsqrt(jnp.mean(x32 * x32, axis=-1, keepdims=True) + EPS)
    return (y * g.astype(jnp.float32)).astype(x.dtype)

def layer_norm_2(x, g, b):
    x32 = x.astype(jnp.float32)
    mu = jnp.mean(x32, axis=-1, keepdims=True)
    var = jnp.mean(jnp.square(x32 - mu), axis=-1, keepdims=True)
    y = (x32 - mu) * lax.rsqrt(var + EPS) * g.astype(jnp.float32) + b.astype(jnp.float32)
    return y.astype(x.dtype)

def axial_rope_tables_2(n_tokens):
    rows = n_tokens // GRID_W
    row = jnp.repeat(jnp.arange(rows), GRID_W).astype(jnp.float32)
    col = jnp.tile(jnp.arange(GRID_W), rows).astype(jnp.float32)
    half = HEAD_DIM // 2
    inv = ROPE_BASE ** (-jnp.arange(0, half, 2, dtype=jnp.float32) / half)
    ang_r = row[:, None] * inv[None, :]
    ang_c = col[:, None] * inv[None, :]
    return (jnp.cos(ang_r), jnp.sin(ang_r), jnp.cos(ang_c), jnp.sin(ang_c))

def _rotate(x, cos, sin):
    n = x.shape[-1] // 2
    x1, x2 = x[..., :n], x[..., n:]
    cos = cos.astype(x.dtype)
    sin = sin.astype(x.dtype)
    return jnp.concatenate([x1 * cos - x2 * sin, x2 * cos + x1 * sin], axis=-1)

def apply_axial_rope(x, rope):
    cos_r, sin_r, cos_c, sin_c = rope
    half = HEAD_DIM // 2
    return jnp.concatenate([_rotate(x[..., :half], cos_r, sin_r),
                            _rotate(x[..., half:], cos_c, sin_c)], axis=-1)

def depthwise_conv(u, w, b):
    k, ch = w.shape
    out = lax.conv_general_dilated(u, w[:, None, :].astype(u.dtype), window_strides=(1,),
                                   padding=[(k // 2, k // 2)],
                                   dimension_numbers=('NWC', 'WIO', 'NWC'),
                                   feature_group_count=ch)
    return out + b.astype(u.dtype)

def conformer_conv(h, w_glu, conv_w, conv_b, ln_g, ln_b, w_proj):
    u = h @ w_glu
    u = u[..., :CONV_CH] * jax.nn.sigmoid(u[..., CONV_CH:])
    u = depthwise_conv(u, conv_w, conv_b)
    u = layer_norm_2(u, ln_g, ln_b)
    return jax.nn.silu(u) @ w_proj

def multiscale_pool(h, w_p, w_group, scale, w_proj):
    p = h @ w_p
    b_, l_ = p.shape[0], p.shape[1]
    cs = jnp.cumsum(p.astype(jnp.float32), axis=1)
    cs = jnp.pad(cs, ((0, 0), (1, 0), (0, 0)))
    t = jnp.arange(l_)
    outs = []
    for gi, w in enumerate(POOL_WINDOWS):
        lo = jnp.clip(t - w // 2, 0, l_)
        hi = jnp.clip(t + w // 2, 0, l_)
        csg = cs[..., gi * POOL_GROUP:(gi + 1) * POOL_GROUP]
        s = jnp.take(csg, hi, axis=1) - jnp.take(csg, lo, axis=1)
        outs.append(s / (hi - lo).astype(jnp.float32)[None, :, None])
    pooled = jnp.concatenate(outs, axis=-1).astype(p.dtype) - p
    pooled = pooled.reshape(b_, l_, len(POOL_WINDOWS), POOL_GROUP)
    mixed = jnp.einsum('blgc,gcd->blgd', pooled, w_group).reshape(b_, l_, POOL_CH)
    return (mixed * scale) @ w_proj

def diff_qkv(h, w_q, w_k, w_v):
    b_, l_ = h.shape[0], h.shape[1]
    q = (h @ w_q).reshape(b_, l_, N_HEADS, 2, HEAD_DIM).transpose(0, 2, 3, 1, 4)
    k = (h @ w_k).reshape(b_, l_, N_HEADS, 2, HEAD_DIM).transpose(0, 2, 3, 1, 4)
    v = (h @ w_v).reshape(b_, l_, N_HEADS, V_DIM).transpose(0, 2, 1, 3)
    return q, k, v

def diff_attend(q, k, v, lam):
    s = jnp.einsum('bhiqd,bhikd->bhiqk', q, k).astype(jnp.float32) * (HEAD_DIM ** -0.5)
    p = jax.nn.softmax(s, axis=-1)
    a = (p[:, :, 0] - lam * p[:, :, 1]).astype(v.dtype)
    return jnp.einsum('bhqk,bhkd->bhqd', a, v)

def diff_finish(o, subln_g, lam_init, w_proj):
    o = rms_norm_2(o, subln_g) * (1.0 - lam_init)
    b_, h_, l_, _ = o.shape
    return o.transpose(0, 2, 1, 3).reshape(b_, l_, ATTN_W) @ w_proj

def gated_merge(h, y_a, y_b, y_c, w_g, b_gate, w_out):
    g = jax.nn.sigmoid(h @ w_g + b_gate)
    m = (g[..., :D_MODEL] * y_a + g[..., D_MODEL:2 * D_MODEL] * y_b
         + g[..., 2 * D_MODEL:] * y_c)
    return m @ w_out

def token_mixer(h, hc, rope, need_ctx, lam_init, w_in, b_gate, conv_w, conv_b, ln_g, ln_b,
                w_conv_out, lam_q1, lam_k1, lam_q2, lam_k2, subln_g, w_attn_out,
                w_pool_group, pool_scale, w_pool_out, w_out):
    w_glu = w_in[:, COL_A:COL_Q]
    w_q = w_in[:, COL_Q:COL_K]
    w_k = w_in[:, COL_K:COL_V]
    w_v = w_in[:, COL_V:COL_P]
    w_p = w_in[:, COL_P:COL_G]
    w_g = w_in[:, COL_G:IN_W]
    lam = (jnp.exp(jnp.sum(lam_q1.astype(jnp.float32) * lam_k1.astype(jnp.float32)))
           - jnp.exp(jnp.sum(lam_q2.astype(jnp.float32) * lam_k2.astype(jnp.float32)))
           + lam_init)

    qc, kc, vc = diff_qkv(hc, w_q, w_k, w_v)
    q, k, v = diff_qkv(h, w_q, w_k, w_v)
    q = apply_axial_rope(q, rope)
    k = apply_axial_rope(k, rope)
    k_all = jnp.concatenate([kc, k], axis=3)
    v_all = jnp.concatenate([vc, v], axis=2)
    b_, h_, _, l_, _ = q.shape
    nb = l_ // Q_BLOCK
    qb = jnp.moveaxis(q.reshape(b_, h_, 2, nb, Q_BLOCK, HEAD_DIM), 3, 0)
    ob = lax.map(lambda qq: diff_attend(qq, k_all, v_all, lam), qb)
    o = jnp.moveaxis(ob, 0, 2).reshape(b_, h_, l_, V_DIM)

    y_a = conformer_conv(h, w_glu, conv_w, conv_b, ln_g, ln_b, w_conv_out)
    y_b = diff_finish(o, subln_g, lam_init, w_attn_out)
    y_c = multiscale_pool(h, w_p, w_pool_group, pool_scale, w_pool_out)
    y = gated_merge(h, y_a, y_b, y_c, w_g, b_gate, w_out)
    if not need_ctx:
        return y, None
    oc = diff_attend(qc, kc, vc, lam)
    yc_a = conformer_conv(hc, w_glu, conv_w, conv_b, ln_g, ln_b, w_conv_out)
    yc_b = diff_finish(oc, subln_g, lam_init, w_attn_out)
    yc_c = multiscale_pool(hc, w_p, w_pool_group, pool_scale, w_pool_out)
    yc = gated_merge(hc, yc_a, yc_b, yc_c, w_g, b_gate, w_out)
    return y, yc

def swiglu(h, w_ffn_in, w_ffn_out):
    u = h @ w_ffn_in
    return (jax.nn.silu(u[..., :D_FF_2]) * u[..., D_FF_2:]) @ w_ffn_out

def second_inputs(seed: int = 0) -> dict:
    key = jax.random.key(seed)
    ks = jax.random.split(key, 32)
    f32 = jnp.float32
    nrm = lambda k, shape, s: jax.random.normal(k, shape, f32) * s
    gain = lambda k, shape: 1.0 + 0.02 * jax.random.normal(k, shape, f32)
    L = DEPTH
    return {
        "x": nrm(ks[0], (BATCH, SEQ, D_MODEL), 1.0),
        "c": nrm(ks[1], (BATCH, D_MODEL), 1.0),
        "ctx": nrm(ks[2], (BATCH, CTX_LEN, D_MODEL), 1.0),
        "c_ctx": nrm(ks[3], (D_MODEL,), 1.0),
        "w_mod": nrm(ks[4], (L, D_MODEL, N_MOD * D_MODEL), 0.5 * D_MODEL ** -0.5),
        "b_mod": nrm(ks[5], (L, N_MOD * D_MODEL), 0.02),
        "g_pre_mix": gain(ks[6], (L, D_MODEL)),
        "g_post_mix": gain(ks[7], (L, D_MODEL)),
        "w_in": nrm(ks[8], (L, D_MODEL, IN_W), D_MODEL ** -0.5),
        "b_gate": nrm(ks[9], (L, N_BRANCH * D_MODEL), 0.02),
        "conv_w": nrm(ks[10], (L, CONV_WIDTH, CONV_CH), CONV_WIDTH ** -0.5),
        "conv_b": nrm(ks[11], (L, CONV_CH), 0.02),
        "conv_ln_g": gain(ks[12], (L, CONV_CH)),
        "conv_ln_b": nrm(ks[13], (L, CONV_CH), 0.02),
        "w_conv_out": nrm(ks[14], (L, CONV_CH, D_MODEL), CONV_CH ** -0.5),
        "lam_q1": nrm(ks[15], (L, HEAD_DIM), 0.1),
        "lam_k1": nrm(ks[16], (L, HEAD_DIM), 0.1),
        "lam_q2": nrm(ks[17], (L, HEAD_DIM), 0.1),
        "lam_k2": nrm(ks[18], (L, HEAD_DIM), 0.1),
        "subln_g": gain(ks[19], (L, V_DIM)),
        "w_attn_out": nrm(ks[20], (L, ATTN_W, D_MODEL), ATTN_W ** -0.5),
        "w_pool_group": nrm(ks[21], (L, len(POOL_WINDOWS), POOL_GROUP, POOL_GROUP), POOL_GROUP ** -0.5),
        "pool_scale": 1.0 + 0.1 * jax.random.normal(ks[22], (L, POOL_CH), f32),
        "w_pool_out": nrm(ks[23], (L, POOL_CH, D_MODEL), POOL_CH ** -0.5),
        "w_out": nrm(ks[24], (L, D_MODEL, D_MODEL), D_MODEL ** -0.5),
        "g_pre_ffn": gain(ks[25], (L, D_MODEL)),
        "g_post_ffn": gain(ks[26], (L, D_MODEL)),
        "w_ffn_in": nrm(ks[27], (L, D_MODEL, 2 * D_FF_2), D_MODEL ** -0.5),
        "w_ffn_out": nrm(ks[28], (L, D_FF_2, D_MODEL), D_FF_2 ** -0.5),
    }

def second_block(x, c, ctx, c_ctx, w_mod, b_mod, g_pre_mix, g_post_mix, w_in, b_gate, conv_w,
              conv_b, conv_ln_g, conv_ln_b, w_conv_out, lam_q1, lam_k1, lam_q2, lam_k2,
              subln_g, w_attn_out, w_pool_group, pool_scale, w_pool_out, w_out, g_pre_ffn,
              g_post_ffn, w_ffn_in, w_ffn_out):
    rope = axial_rope_tables_2(x.shape[1])
    xl, xc = x, ctx
    for l in range(DEPTH):
        need_ctx = l < DEPTH - 1
        lam_init = 0.8 - 0.6 * math.exp(-0.3 * l)
        mod = jax.nn.silu(c) @ w_mod[l] + b_mod[l]
        modc = jax.nn.silu(c_ctx) @ w_mod[l] + b_mod[l]
        sh1, sc1, gt1, sh2, sc2, gt2 = jnp.split(mod[:, None, :], N_MOD, axis=-1)
        csh1, csc1, cgt1, csh2, csc2, cgt2 = jnp.split(modc, N_MOD, axis=-1)

        h = rms_norm_2(xl, g_pre_mix[l]) * (1.0 + sc1) + sh1
        hc = rms_norm_2(xc, g_pre_mix[l]) * (1.0 + csc1) + csh1
        y, yc = token_mixer(h, hc, rope, need_ctx, lam_init, w_in[l], b_gate[l], conv_w[l],
                            conv_b[l], conv_ln_g[l], conv_ln_b[l], w_conv_out[l], lam_q1[l],
                            lam_k1[l], lam_q2[l], lam_k2[l], subln_g[l], w_attn_out[l],
                            w_pool_group[l], pool_scale[l], w_pool_out[l], w_out[l])
        xl = xl + gt1 * rms_norm_2(y, g_post_mix[l])

        h = rms_norm_2(xl, g_pre_ffn[l]) * (1.0 + sc2) + sh2
        xl = xl + gt2 * rms_norm_2(swiglu(h, w_ffn_in[l], w_ffn_out[l]), g_post_ffn[l])

        if need_ctx:
            xc = xc + cgt1 * rms_norm_2(yc, g_post_mix[l])
            hc = rms_norm_2(xc, g_pre_ffn[l]) * (1.0 + csc2) + csh2
            xc = xc + cgt2 * rms_norm_2(swiglu(hc, w_ffn_in[l], w_ffn_out[l]), g_post_ffn[l])
    return xl


def setup_inputs(seed=0):
    out = dict(first_inputs(seed))
    for name, value in second_inputs(seed + 1).items():
        if name != "x":
            out[name + "_2"] = value
    return out


def reference(
    x, c, ctx, c_ctx, ada_w, ada_b, ln_g, ln_b, ev_w_in, ev_w_out, ev_q_gain, ev_k_gain, ev_rpb,
    od_w_in, od_w_out, od_sink, ffn_w_up, ffn_conv_w, ffn_conv_b, ffn_w_down, c_2, ctx_2,
    c_ctx_2, w_mod_2, b_mod_2, g_pre_mix_2, g_post_mix_2, w_in_2, b_gate_2, conv_w_2, conv_b_2,
    conv_ln_g_2, conv_ln_b_2, w_conv_out_2, lam_q1_2, lam_k1_2, lam_q2_2, lam_k2_2, subln_g_2,
    w_attn_out_2, w_pool_group_2, pool_scale_2, w_pool_out_2, w_out_2, g_pre_ffn_2,
    g_post_ffn_2, w_ffn_in_2, w_ffn_out_2,
):
    x = first_block(
        x, c, ctx, c_ctx, ada_w, ada_b, ln_g, ln_b, ev_w_in, ev_w_out, ev_q_gain, ev_k_gain,
        ev_rpb, od_w_in, od_w_out, od_sink, ffn_w_up, ffn_conv_w, ffn_conv_b, ffn_w_down,
    )
    return second_block(
        x, c_2, ctx_2, c_ctx_2, w_mod_2, b_mod_2, g_pre_mix_2, g_post_mix_2, w_in_2, b_gate_2,
        conv_w_2, conv_b_2, conv_ln_g_2, conv_ln_b_2, w_conv_out_2, lam_q1_2, lam_k1_2,
        lam_q2_2, lam_k2_2, subln_g_2, w_attn_out_2, w_pool_group_2, pool_scale_2, w_pool_out_2,
        w_out_2, g_pre_ffn_2, g_post_ffn_2, w_ffn_in_2, w_ffn_out_2,
    )


_drawn_inputs = setup_inputs


def setup_inputs(seed=0):
    import zlib

    import numpy as np

    out = dict(_drawn_inputs(seed))
    spreads = {}
    factors = {'ctx': 4.601,
     'ada_b': 5.574,
     'ev_q_gain': 8.0,
     'ev_k_gain': 8.0,
     'ev_rpb': 8.0,
     'od_sink': 8.0,
     'ffn_conv_b': 8.0,
     'g_pre_mix_2': 6.291,
     'g_post_mix_2': 6.661,
     'b_gate_2': 8.0,
     'conv_b_2': 8.0,
     'conv_ln_g_2': 8.0,
     'conv_ln_b_2': 8.0,
     'lam_q1_2': 8.0,
     'lam_k1_2': 8.0,
     'lam_q2_2': 3.695,
     'lam_k2_2': 4.314,
     'subln_g_2': 8.0,
     'g_pre_ffn_2': 5.025,
     'g_post_ffn_2': 7.005}
    for name, (base, spread) in spreads.items():
        noise = np.random.default_rng([zlib.crc32(name.encode()), seed]).standard_normal(out[name].shape)
        drawn = base * np.exp(spread * noise) if base else spread * noise
        out[name] = __import__('jax').numpy.asarray(drawn.astype(out[name].dtype))
    for name, factor in factors.items():
        out[name] = (out[name] * factor).astype(out[name].dtype)
    return out
```

```python
from contextlib import ExitStack
import math

import numpy as np

import concourse.bass as bass
from concourse import mybir

F32 = mybir.dt.float32
ALU = mybir.AluOpType
ACT = mybir.ActivationFunctionType
AX_X = mybir.AxisListType.X

P = 128
D = 1024
KC = D // P
S = 256
TOK = 2 * S
TT = TOK // P
HD = 64
FF = 2816
FC = FF // P
GRID_W = 64
ALPHA = 4.0 ** 0.25
LN_EPS = 1e-5
RMS_EPS = 1e-6
SCALE = HD ** -0.5
NEG = -1e30
CONV_TAPS = 31
CONV_PAD = CONV_TAPS // 2
POOL_PAD = 8
POOL_WINDOWS = (2, 4, 8, 16)
LAM_INIT = [0.8 - 0.6 * math.exp(-0.3 * l) for l in range(2)]

RING = 6
SLAB = 8
DOWN = [8, 8, 6]

def columns(spec):
    at, out = 0, {}
    for name, n in spec:
        out[name] = at
        at += n
    return out, at


V1, NV1 = columns([("mod_b", 48), ("ln_g", 16), ("ln_b", 16), ("conv_w", 3 * 2 * FC), ("conv_b", 2 * FC),
                   ("q_gain", 1), ("k_gain", 1), ("sink", 16)])
V2, NV2 = columns([("mod_b", 48), ("g_pre_mix", 8), ("g_post_mix", 8), ("g_pre_ffn", 8), ("g_post_ffn", 8),
                   ("b_gate", 24), ("conv_w", 4 * CONV_TAPS), ("conv_b", 4), ("conv_ln_g", 4), ("conv_ln_b", 4),
                   ("subln_g", 1), ("pool_scale", 4)])
NV = max(NV1, NV2)
C_COS, C_SIN, C_ONE, C_ID, C_ROT, C_HEAD, C_EDGE = 0, S, 2 * S, 2 * S + P, 2 * S + 2 * P, 2 * S + 3 * P, 2 * S + 4 * P
NCONST = C_EDGE + 4 * 2 * POOL_PAD


ROOTS, NORMS, X_READS = 4, 4 * KC, 4 * KC


class Linear:

    def __init__(self, name, groups, tiles, n, emptied, kind="features"):
        self.name, self.groups, self.tiles, self.n, self.kind = name, groups, tiles, n, kind
        self.emptied = emptied if isinstance(emptied, tuple) else (emptied, emptied)
        self.per = len(tiles)
        self.step = RING // self.per


def plan_linears():
    plan = []
    for l in range(2):
        n = TOK if l == 0 else S
        plan.append(Linear(f"mod1_{l}", 48, [8], 2, "vector"))
        if l == 0:
            plan += [Linear("ev_qk", 13, [8], TOK, "scalar"), Linear("ev_v", 5, [8], TOK, "scalar", "tokens")]
        else:
            plan += [Linear("od_k", 1, [8], TOK, "scalar"), Linear("od_v", 1, [8], TOK, "scalar", "tokens"),
                     Linear("od_q", 8, [8], S, "scalar")]
        plan += [Linear(f"mix1_{l}", 8, [8], n, "scalar"), Linear(f"up1_{l}", 2 * FC, [8], n, "vector"),
                 Linear(f"down1_{l}", 8, DOWN, n, "scalar")]
    for l in range(2):
        n = TOK if l == 0 else S
        plan += [Linear(f"mod2_{l}", 48, [8], 2, "vector"),
                 Linear(f"glu_{l}", 8, [8], n, ("scalar", "vector")),
                 Linear(f"q_{l}", 8, [8], n, "scalar"), Linear(f"k_{l}", 8, [8], TOK, "scalar"),
                 Linear(f"v_{l}", 8, [8], TOK, "scalar", "tokens"), Linear(f"p_{l}", 4, [8], n, "scalar"),
                 Linear(f"gate_{l}", 24, [8], n, "scalar"), Linear(f"group_{l}", 4, [1], n, "scalar"),
                 Linear(f"merge_{l}", 24, [8], n, "vector"), Linear(f"out_{l}", 8, [8], n, "scalar"),
                 Linear(f"up2_{l}", 2 * FC, [8], n, ("scalar", "vector")),
                 Linear(f"down2_{l}", 8, DOWN, n, "scalar")]
    slab, emptied, last = 0, {"scalar": 0, "vector": 0}, {0: None, 1: None}
    for L in plan:
        L.slab0 = slab
        L.empty0 = dict(emptied)
        L.before = dict(last)
        slab += L.groups * L.per
        for g in range(L.groups):
            emptied[L.emptied[g % 2]] += 1
            last[g % 2] = (L.emptied[g % 2], emptied[L.emptied[g % 2]])
    return {L.name: L for L in plan}, plan


def build(nc, T):
    LIN, ORDER = plan_linears()
    ctx = ExitStack()
    with ctx:
        def sb(name, words):
            return ctx.enter_context(nc.sbuf_tensor(name, [P, words], F32))

        def sem(name):
            return ctx.enter_context(nc.semaphore(name))

        bank = [ctx.enter_context(nc.psum_tensor(f"bank{i}", [P, 512], F32)) for i in range(8)]
        X_ = sb("x", KC * TOK)
        H_ = sb("h", KC * TOK)
        BIG = sb("big", 24 * TOK)
        QK_ = sb("qk", 16 * TOK)
        VT_ = sb("v_tokens", TT * D)
        O_ = sb("attn_out", KC * TOK)
        CV_ = sb("conv_out", 4 * TOK)
        PM_ = sb("pooled", 4 * TOK)
        TMP_ = sb("tmp", 2 * TOK)
        RS_ = sb("rstd", 2 * TOK)
        ring = sb("ring", RING * SLAB * P)
        vec = sb("vec", 2 * NV)
        con = sb("con", NCONST)
        mod = sb("mod", 96)
        mods = sb("mod_derived", 4 * 16)
        cvec = sb("cvec", 32)
        small = sb("small", 16)
        lamv = sb("lam_vectors", 2 * 4 * HD)
        nsink = sb("minus_sink", 16)
        smax = sb("smax", 64)
        ssum = sb("ssum", 64)
        srec = sb("srec", 64)
        ssink = sb("ssink", 64)

        X = X_[:, :].rearrange("p (c n) -> p c n", c=KC)
        H = H_[:, :].rearrange("p (c n) -> p c n", c=KC)
        QK = QK_[:, :].rearrange("p (c n) -> p c n", c=16)
        G = BIG[:, :].rearrange("p (c n) -> p c n", c=24)
        O = O_[:, :].rearrange("p (c n) -> p c n", c=KC)
        CV = CV_[:, :].rearrange("p (c n) -> p c n", c=4)
        PM = PM_[:, :].rearrange("p (c n) -> p c n", c=4)
        TMP = TMP_[:, :].rearrange("p (c n) -> p c n", c=2)
        RS = RS_[:, :].rearrange("p (c n) -> p c n", c=2)
        VT = VT_[:, :].rearrange("p (t d) -> p t d", t=TT)
        MOD = mod[:, :].rearrange("p (j s) -> p j s", s=2)
        MD = mods[:, :].rearrange("p (k c s) -> p k c s", k=4, s=2)
        UW = S + 2 * CONV_PAD
        U = BIG[:, 0:4 * 2 * UW].rearrange("p (c s n) -> p c s n", c=4, s=2)
        PW = S + 2 * POOL_PAD
        PP = O_[:, 0:4 * 2 * PW].rearrange("p (c s n) -> p c s n", c=4, s=2)
        PT0 = O_[:, 8 * PW + 0:8 * PW + 2 * PW].rearrange("p (s n) -> p s n", s=2)
        PT1 = O_[:, 8 * PW + 2 * PW:8 * PW + 4 * PW].rearrange("p (s n) -> p s n", s=2)
        LAM = lamv[:, :].rearrange("p (l j d) -> p l j d", l=2, j=4)
        BIAS = BIG[:, 13 * TOK:13 * TOK + 8 * 2 * S].rearrange("p (h q t) -> p h q t", h=8, q=2)
        MASKB = BIG[:, 22 * TOK:22 * TOK + 2 * S].rearrange("p (q t) -> p q t", q=2)
        MASKC = BIG[:, 23 * TOK:23 * TOK + 2 * S].rearrange("p (q t) -> p q t", q=2)
        COS, SIN = con[:, C_COS:C_COS + S], con[:, C_SIN:C_SIN + S]
        ONES, IDENT = con[:, C_ONE:C_ONE + P], con[:, C_ID:C_ID + P]
        ROT, HEADS = con[:, C_ROT:C_ROT + P], con[:, C_HEAD:C_HEAD + P]
        PROB = [H[:, i, :] for i in range(6)]
        PROBT = [H[:, 6 + i, :] for i in range(2)]
        SCORES = [bank[i] for i in (2, 3, 4, 0)]
        OUTB = [bank[7], bank[1]]

        def vcol(layer, at, n=1):
            return vec[:, bass.ds(at + NV * (layer % 2), n)]

        landed = [sem(f"slab_landed{i}") for i in range(RING)]
        slab_done = sem("slab_done")
        emptied = {"scalar": sem("banks_emptied_by_scalar"), "vector": sem("banks_emptied_by_vector")}
        act_step, dve_step, pool_step = sem("act_step"), sem("dve_step"), sem("pool_step")
        const_in, cvec_in, vec_in, mask_in, x_in, ctx_in = sem("const_in"), sem("cvec_in"), sem("vec_in"), sem("mask_in"), sem("x_in"), sem("ctx_in")
        bias_in, lam_in = sem("bias_in"), sem("lam_in")
        silu_c = sem("silu_c_ready")
        h_ready = sem("h_chunks_ready")
        mod_ready = sem("mod_ready")
        part_ready = sem("scaled_part_ready")
        row_ready = sem("residual_chunk_ready")
        cent_ready = sem("centred_chunk_ready")
        sq_ready = sem("square_chunk_ready")
        stat_done = sem("stat_done")
        root_ready = sem("root_ready")
        norm_ready = sem("normed_chunk_ready")
        x_ready = sem("x_chunk_ready")
        rope_mm = sem("rope_product_done")
        rope_done = sem("rope_chunk_done")
        hsq_ready, hsum_done, hroot_ready, hnorm_done = sem("head_square"), sem("head_sum"), sem("head_root"), sem("head_norm")
        sc_done, nm_ready, ex_ready, pr_ready = sem("scores_done"), sem("max_ready"), sem("exp_ready"), sem("probs_ready")
        tr_done, pt_ready, pv_done, o_ready = sem("probs_turned"), sem("turned_copied"), sem("pv_done"), sem("o_ready")
        sig_ready, tap_ready = sem("sigmoid_ready"), sem("conv_centre_ready")
        hid_ready = sem("hidden_ready")
        conv_ready = sem("conv_ready")
        pad_ready, pool_ready = sem("pads_ready"), sem("pooled_ready")
        bias_ready = sem("bias_ready")
        lam_ready, lam_exp = sem("lam_ready"), sem("lam_exp")
        sub_sq = sem("subln_square")
        out_sem = sem("out_stored")

        act_own, dve_own = sem("act_own"), sem("dve_own")
        tap_left = sem("conv_left_tap_done")
        merge_step = sem("merge_sum_done")
        small_ready = sem("small_ready")

        class Own:

            def __init__(self, eng, s):
                self.eng, self.s, self.n = eng, s, 0

            def inc(self, ins):
                ins.then_inc(self.s, 1)
                self.n += 1
                return self.n

            def wait(self, n):
                self.eng.wait_ge(self.s, n)

            def link(self, ins):
                self.wait(self.inc(ins))

        class Tally(dict):

            def __missing__(self, k):
                return 0

        class At:

            def __init__(self, L, g, u, turn):
                self.L, self.g, self.u, self.turn = L, g, u, turn

            def over(self, k):
                return self.g // k if self.turn is None else self.turn * (self.L.step // k) + self.u // k

            def full(self):
                return self.g * self.L.per + (self.L.per + self.L.slab0)

            def emptied(self, back=0):
                L, who = self.L, self.L.emptied[self.u % 2]
                if L.emptied[0] == L.emptied[1]:
                    return emptied[who], self.g + (L.empty0[who] + 1 - back)
                return emptied[who], self.over(2) + (L.empty0[who] + 1 - back // 2)

        def turns(eng, L, body):
            whole = L.groups // L.step
            whole = whole if whole > 2 else 1
            for g in range(min(L.step, L.groups)):
                body(At(L, g, g, None))
            if whole > 2:
                with eng.Fori(1, whole) as turn:
                    for u in range(L.step):
                        body(At(L, turn * L.step + u, u, turn))
            for g in range(whole * L.step, L.groups):
                body(At(L, g, g % L.step, None))

        def streams(ap, ns):
            return ap.rearrange("p (s n) -> p s n", s=ns)

        def units_pair(qchunk, kchunk, chunk0, vcols, tiles, mask, sink, shared):
            out = []
            for c in range(8 if sink else 4):
                for half in range(2):
                    rows = slice(HD * half, HD * half + HD)
                    for qt in tiles:
                        keys = slice(0, TOK) if qt < 2 else slice(S, TOK)
                        k0 = keys.start // P
                        m = None if qt >= 2 or mask is None else mask(2 * c + half, qt)
                        q = G[rows, qchunk + c, qt * P:(qt + 1) * P]
                        k = G[rows, kchunk + (0 if shared else c), keys]
                        v0 = vcols + (0 if shared else c * P) + HD * half
                        out.append(dict(
                            subs=[(q, k)], T=keys.stop - keys.start, mask=m, diff=False,
                            sink=(c + 8 * half) if sink else None,
                            v=[VT[:, k0 + t, v0:v0 + HD] for t in range((keys.stop - keys.start) // P)],
                            rows=rows, out=O[rows, chunk0 + c, qt * P:(qt + 1) * P]))
            return out

        def units_diff(tiles):
            out = []
            for h in range(8):
                for qt in tiles:
                    keys = slice(0, TOK) if qt < 2 else slice(S, TOK)
                    k0 = keys.start // P
                    subs = [(QK[HD * i:HD * i + HD, h, qt * P:(qt + 1) * P], QK[HD * i:HD * i + HD, 8 + h, keys])
                            for i in range(2)]
                    out.append(dict(subs=subs, T=keys.stop - keys.start, mask=None, diff=True, sink=None,
                                    v=[VT[:, k0 + t, h * P:(h + 1) * P] for t in range((keys.stop - keys.start) // P)],
                                    rows=slice(0, P), out=O[:, h, qt * P:(qt + 1) * P]))
            return out

        ATT = {
            "global": units_pair(0, 4, 0, 0, range(4), None, False, True),
            "near": units_pair(5, 9, 4, P, range(4), lambda h, qt: BIAS[:, h, qt, :], False, False),
            "window": units_pair(1, 0, 0, 0, range(2), lambda h, qt: MASKC[:, qt, :], True, True),
            "diff_0": units_diff(range(4)),
            "diff_1": units_diff(range(2)),
        }
        AHEAD = 2


        def post_stat(pe, L, w):
            for c in range(KC):
                pe.wait_ge(emptied["scalar"], L.empty0["scalar"] + c + 1)
                ins = pe.matmul(bank[3][:, 0:w], ONES, QK[:, 8 + c, 0:w], start=(c == 0), stop=(c == KC - 1))
            ins.then_inc(stat_done, 1)

        block = ctx.enter_context(nc.Block())

        @block.sync
        def _(sp):
            sp.dma_start(cvec[:, :], T["cvecs"]).then_inc(cvec_in, 16)
            for L in ORDER:
                w = T["w_" + L.name]

                def load(at):
                    for j in range(L.per):
                        slot = (L.slab0 + at.u * L.per + j) % RING
                        n = at.g * L.per + (L.slab0 + j)
                        if not (isinstance(n, int) and n < RING):
                            sp.wait_ge(slab_done, n - (RING - 1))
                        words = L.tiles[j] * P
                        if L.name.startswith("merge"):
                            words = (4, 4, 8)[at.u % 3] * P
                        src = w[at.g] if L.per == 1 else w[at.g, :, j * SLAB * P:j * SLAB * P + words]
                        sp.dma_start(ring[:, slot * SLAB * P:slot * SLAB * P + words],
                                     src[:, 0:words]).then_inc(landed[slot], 16)

                turns(sp, L, load)
            sp.wait_ge(x_ready, X_READS + 32)
            sp.dma_start(T["out"], X[:, :, 0:S]).then_inc(out_sem, 16)
            sp.wait_ge(out_sem, 16)

        @block.tensor
        def _(pe):
            n = Tally()

            def linear(name, rhs, waits=()):
                L = LIN[name]
                for s, v in waits:
                    pe.wait_ge(s, v)

                def group(at):
                    b = bank[at.u % 2]
                    if isinstance(at.g, int) and at.g < 2:
                        if L.before[at.u % 2] is not None:
                            who, count = L.before[at.u % 2]
                            pe.wait_ge(emptied[who], count)
                    else:
                        pe.wait_ge(*at.emptied(back=2))
                    first = True
                    kc = 0
                    for j in range(L.per):
                        slot = (L.slab0 + at.u * L.per + j) % RING
                        nth = at.g * L.per + (L.slab0 + j) if at.turn is None else None
                        use = nth // RING if at.turn is None else at.turn + (L.slab0 + at.u * L.per + j) // RING
                        pe.wait_ge(landed[slot], use * 16 + 16)
                        tiles = (4, 4, 8)[at.u % 3] if name.startswith("merge") else L.tiles[j]
                        for i in range(tiles):
                            w = ring[:, (slot * SLAB + i) * P:(slot * SLAB + i + 1) * P]
                            last = j == L.per - 1 and i == tiles - 1
                            if L.kind == "tokens":
                                for t in range(TT):
                                    ins = pe.matmul(b[:, t * P:(t + 1) * P], H[:, kc, t * P:(t + 1) * P], w,
                                                    start=(kc == 0 and t == 0), stop=last, skip_group_check=True)
                            else:
                                ins = pe.matmul(b[:, 0:L.n], w, rhs(kc, at), start=first, stop=last)
                            first = False
                            kc += 1
                        ins.then_inc(slab_done, 1)

                turns(pe, L, group)

            def stat(src, chunks, width, ready, b):
                for c in range(chunks):
                    n[ready] += 1
                    pe.wait_ge(ready, n[ready])
                    ins = pe.matmul(bank[b][:, 0:width], ONES, src(c), start=(c == 0), stop=(c == chunks - 1))
                ins.then_inc(stat_done, 1)

            def rope(chunk, count):
                for j in range(count):
                    n["rope"] += 1
                    if n["rope"] > 2:
                        pe.wait_ge(rope_done, n["rope"] - 2)
                    pe.matmul(bank[2 + n["rope"] % 2][:, 0:S], ROT, chunk(j), start=True, stop=True).then_inc(rope_mm, 1)

            def attend(units):
                spu = len(units[0]["subs"])
                j0, u0 = n["sub"], n["unit"]

                def scores(u):
                    for i, (q, k) in enumerate(units[u]["subs"]):
                        j = u * spu + i
                        if j >= 4:
                            pe.wait_ge(ex_ready, j0 + j - 3)
                        pe.matmul(SCORES[j % 4][:, 0:units[u]["T"]], q, k, start=True, stop=True).then_inc(sc_done, 1)

                def turn(u):
                    pe.wait_ge(pr_ready, u0 + u + 1)
                    if u >= 2:
                        pe.wait_ge(pt_ready, u0 + u - 1)
                    src = PROB[(u * spu + spu - 1) % 6]
                    for t in range(units[u]["T"] // P):
                        ins = pe.transpose(bank[5 + u % 2][:, t * P:(t + 1) * P], src[:, t * P:(t + 1) * P], IDENT)
                    ins.then_inc(tr_done, 1)

                def values(u):
                    pe.wait_ge(pt_ready, u0 + u + 1)
                    if u0 + u >= 2:
                        pe.wait_ge(o_ready, u0 + u - 1)
                    unit = units[u]
                    for t, v in enumerate(unit["v"]):
                        ins = pe.matmul(OUTB[u % 2][unit["rows"], 0:P], v,
                                        PROBT[u % 2][:, t * P:(t + 1) * P], start=(t == 0), stop=(t == len(unit["v"]) - 1))
                    ins.then_inc(pv_done, 1)

                for u in range(AHEAD):
                    scores(u)
                for u in range(len(units)):
                    if u + AHEAD < len(units):
                        scores(u + AHEAD)
                    turn(u)
                    if u:
                        values(u - 1)
                values(len(units) - 1)
                n["sub"] += len(units) * spu
                n["unit"] += len(units)

            def mod_rhs(b):
                return lambda kc, at: cvec[:, b * 16 + 2 * kc:b * 16 + 2 * kc + 2]

            def chunk_ready(count=KC):
                n["h"] += count
                return [(h_ready, n["h"])]

            pe.wait_ge(silu_c, 1)
            pe.wait_ge(const_in, 16)
            for l in range(2):
                w = TOK if l == 0 else S
                linear(f"mod1_{l}", mod_rhs(0))
                if l == 0:
                    linear("ev_qk", lambda kc, at: H[:, kc, :], chunk_ready())
                    linear("ev_v", None)
                    for j in range(5):
                        pe.wait_ge(hsq_ready, j + 1)
                        if j >= 2:
                            pe.wait_ge(hroot_ready, j - 1)
                        pe.matmul(bank[4 + j % 2][:, :], HEADS, QK[:, 8 + j, :], start=True, stop=True).then_inc(hsum_done, 1)
                    pe.wait_ge(hnorm_done, 5)
                    rope(lambda j: G[:, j, 0:S], 5)
                    pe.wait_ge(rope_done, n["rope"])
                    attend(ATT["global"])
                    pe.wait_ge(bias_ready, 1)
                    attend(ATT["near"])
                else:
                    linear("od_k", lambda kc, at: H[:, kc, :], chunk_ready())
                    linear("od_v", None)
                    linear("od_q", lambda kc, at: H[:, kc, 0:S])
                    pe.wait_ge(emptied["scalar"], LIN["od_q"].empty0["scalar"] + 8)
                    rope(lambda j: G[:, j, 0:S], 9)
                    pe.wait_ge(rope_done, n["rope"])
                    attend(ATT["window"])
                linear(f"mix1_{l}", lambda kc, at: O[:, kc, 0:w], [(o_ready, n["unit"])])
                stat(lambda c: X[:, c, 0:w], KC, w, row_ready, 2)
                stat(lambda c: H[:, c, 0:w], KC, w, sq_ready, 3)
                linear(f"up1_{l}", lambda kc, at: H[:, kc, 0:w], chunk_ready())
                n["hid"] += FC
                linear(f"down1_{l}", lambda kc, at: G[:, kc, 0:w], [(hid_ready, n["hid"])])
                stat(lambda c: X[:, c, 0:w], KC, w, row_ready, 2)
                stat(lambda c: H[:, c, 0:w], KC, w, sq_ready, 3)
            for l in range(2):
                w = TOK if l == 0 else S
                linear(f"mod2_{l}", mod_rhs(1))
                stat(lambda c: QK[:, 8 + c, :], KC, TOK, sq_ready, 3)
                linear(f"glu_{l}", lambda kc, at: H[:, kc, 0:w], chunk_ready())
                linear(f"q_{l}", lambda kc, at: H[:, kc, 0:w])
                linear(f"k_{l}", lambda kc, at: H[:, kc, :])
                stat(lambda c: CV[:, c, 0:w], 4, w, conv_ready, 2)
                linear(f"v_{l}", None)
                stat(lambda c: PM[:, c, 0:w], 4, w, sq_ready, 3)
                pe.wait_ge(root_ready, ROOTS + 13 * l + 2)
                rope(lambda j: QK[:, j, 0:S], 16)
                linear(f"p_{l}", lambda kc, at: H[:, kc, 0:w])
                linear(f"gate_{l}", lambda kc, at: H[:, kc, 0:w])
                n["pool"] += 4
                linear(f"group_{l}", lambda kc, at: PM[:, at.g, 0:w], [(pool_ready, n["pool"])])
                pe.wait_ge(rope_done, n["rope"])
                g4 = LIN[f"group_{l}"]
                pe.wait_ge(emptied["scalar"], g4.empty0["scalar"] + 4)
                attend(ATT[f"diff_{l}"])
                for h in range(8):
                    n["sub_sq"] += 1
                    pe.wait_ge(sub_sq, n["sub_sq"])
                    if h >= 2:
                        pe.wait_ge(root_ready, ROOTS + 13 * l + 2 + h - 1)
                    pe.matmul(bank[2 + h % 2][:, 0:w], ONES, QK[:, h, 0:w], start=True, stop=True).then_inc(stat_done, 1)
                g4 = LIN[f"group_{l}"]

                def branch(kc, at):
                    return (CV, PM, O)[at.u % 3][:, kc, 0:w]

                linear(f"merge_{l}", branch, [(norm_ready, NORMS + 12 * (l + 1)),
                                              (silu_c, 1 + 4 * (l + 1)),
                                              (emptied["scalar"], g4.empty0["scalar"] + 4)])
                n["merge"] += 16
                linear(f"out_{l}", lambda kc, at: H[:, kc, 0:w], [(merge_step, n["merge"])])
                L = LIN[f"out_{l}"]
                post_stat(pe, L, w)
                stat(lambda c: QK[:, 8 + c, 0:w], KC, w, sq_ready, 3)
                linear(f"up2_{l}", lambda kc, at: H[:, kc, 0:w], chunk_ready())
                linear(f"down2_{l}", lambda kc, at: G[:, kc, 0:w],
                       [(emptied["vector"], LIN[f"up2_{l}"].empty0["vector"] + FC)])
                post_stat(pe, LIN[f"down2_{l}"], w)

        @block.scalar
        def _(act):
            n = Tally()
            own = Own(act, act_own)

            def copies(name, dst):
                L = LIN[name]

                def one(at):
                    act.wait_ge(slab_done, at.full())
                    src = bank[at.u % 2][:, 0:L.n]
                    if L.kind == "tokens":
                        src = src.rearrange("p (t d) -> p t d", t=TT)
                    if name.startswith("p_"):
                        src = streams(src, L.n // S)
                    nc.scalar.copy(dst(at), src).then_inc(emptied["scalar"], 1)

                turns(act, L, one)

            def gated(name, gate, ns):
                L = LIN[name]

                def one(at):
                    act.wait_ge(slab_done, at.full())
                    if not (isinstance(at.g, int) and at.g < 2):
                        act.wait_ge(row_ready, at.g + (n["row"] - 1))
                    for s in range(ns):
                        cols = slice(s * S, s * S + S)
                        ins = nc.scalar.activation(TMP[:, at.u % 2, cols], bank[at.u % 2][:, cols], ACT.Copy,
                                                   scale=MOD[:, bass.ds(at.g + gate, 1), s])
                    ins.then_inc(emptied["scalar"], 1)

                turns(act, L, one)
                n["row"] += KC

            def squares(src, dst, count, ready, done=sq_ready):
                for c in range(count):
                    n[ready] += 1
                    act.wait_ge(ready, n[ready])
                    nc.scalar.activation(dst(c), src(c), ACT.Square).then_inc(done, 1)

            def root(b, w, scale, eps, slot=0):
                n["stat"] += 1
                act.wait_ge(stat_done, n["stat"])
                n["root"] += 1
                nc.scalar.activation(RS[:, slot, 0:w], bank[b][:, 0:w], ACT.Sqrt, scale=scale,
                                     bias=small[:, eps:eps + 1]).then_inc(root_ready, 1)

            def affine(ln, vl, w):
                for c in range(KC):
                    n["norm"] += 1
                    act.wait_ge(norm_ready, n["norm"])
                    nc.scalar.activation(X[:, c, 0:w], X[:, c, 0:w], ACT.Identity,
                                         scale=vcol(vl, V1["ln_g"] + 8 * ln + c),
                                         bias=vcol(vl, V1["ln_b"] + 8 * ln + c)).then_inc(x_ready, 1)

            def layer_norm(ln, vl, w):
                n["stat"] += 1
                squares(lambda c: X[:, c, 0:w], lambda c: H[:, c, 0:w], KC, cent_ready)
                root(3, w, 1.0 / D, 0)
                affine(ln, vl, w)

            def attend(units, vl):
                spu = len(units[0]["subs"])
                j0, u0 = n["sub"], n["unit"]

                def exps(u):
                    unit = units[u]
                    for i in range(spu):
                        j = u * spu + i
                        act.wait_ge(nm_ready, j0 + j + 1)
                        if j >= 6:
                            act.wait_ge(tr_done, u0 + (j - 6) // spu + 1)
                        m = smax[:, j % 64:j % 64 + 1]
                        if unit["sink"] is not None:
                            nc.scalar.activation(ssink[:, j % 64:j % 64 + 1], vcol(vl, V1["sink"] + unit["sink"]),
                                                 ACT.Exp, bias=m)
                        nc.scalar.activation(PROB[j % 6][:, 0:unit["T"]], SCORES[j % 4][:, 0:unit["T"]], ACT.Exp,
                                             bias=m, scale=SCALE,
                                             accum_out=ssum[:, j % 64:j % 64 + 1]).then_inc(ex_ready, 1)

                def copy(u):
                    act.wait_ge(tr_done, u0 + u + 1)
                    if u0 + u >= 2:
                        act.wait_ge(pv_done, u0 + u - 1)
                    w = units[u]["T"]
                    nc.scalar.copy(PROBT[u % 2][:, 0:w], bank[5 + u % 2][:, 0:w]).then_inc(pt_ready, 1)

                for u in range(AHEAD):
                    exps(u)
                for u in range(len(units)):
                    if u + AHEAD < len(units):
                        exps(u + AHEAD)
                    copy(u)
                n["sub"] += len(units) * spu
                n["unit"] += len(units)

            act.wait_ge(cvec_in, 16)
            act.wait_ge(vec_in, 32)
            nc.scalar.activation(cvec[:, :], cvec[:, :], ACT.Silu).then_inc(silu_c, 1)
            act.wait_ge(small_ready, 3)
            for l in range(2):
                w, ns = (TOK, 2) if l == 0 else (S, 1)
                if l == 0:
                    copies("ev_qk", lambda at: G[:, at.g, :])
                    copies("ev_v", lambda at: VT[:, :, at.g * P:(at.g + 1) * P])
                    for j in range(5):
                        if j == 0:
                            act.wait_ge(emptied["scalar"], LIN["ev_qk"].empty0["scalar"] + 13)
                        nc.scalar.activation(QK[:, 8 + j, :], G[:, j, :], ACT.Square).then_inc(hsq_ready, 1)
                    for j in range(5):
                        act.wait_ge(hsum_done, j + 1)
                        if j >= 2:
                            act.wait_ge(hnorm_done, j - 1)
                        nc.scalar.activation(RS[:, j % 2, :], bank[4 + j % 2][:, :], ACT.Sqrt, scale=1.0 / HD,
                                             bias=small[:, 1:2]).then_inc(hroot_ready, 1)
                    attend(ATT["global"], l)
                    attend(ATT["near"], l)
                else:
                    copies("od_k", lambda at: G[:, at.g, :])
                    copies("od_v", lambda at: VT[:, :, at.g * P:(at.g + 1) * P])
                    copies("od_q", lambda at: G[:, at.g + 1, 0:S])
                    attend(ATT["window"], l)
                gated(f"mix1_{l}", 16, ns)
                layer_norm(0, l, w)

                L = LIN[f"up1_{l}"]

                def conv3(at):
                    act.wait_ge(slab_done, at.full())
                    if not (isinstance(at.g, int) and at.g < 6):
                        act.wait_ge(hid_ready, at.over(2) + (n["hid"] - 2))
                    nc.scalar.activation(QK[:, at.u, 0:w], bank[at.u % 2][:, 0:w], ACT.Identity,
                                         scale=vcol(l, at.g + (V1["conv_w"] + 2 * FC)),
                                         bias=vcol(l, at.g + V1["conv_b"])).then_inc(tap_ready, 1)
                    if at.u % 2:
                        act.wait_ge(*at.emptied())
                        nc.scalar.activation(QK[:, 6 + at.u // 2, 0:w], QK[:, at.u, 0:w],
                                             ACT.Silu).then_inc(sig_ready, 1)

                turns(act, L, conv3)
                n["hid"] += FC
                gated(f"down1_{l}", 40, ns)
                layer_norm(1, l, w)
            for l in range(2):
                w, ns = (TOK, 2) if l == 0 else (S, 1)
                if l == 0:
                    act.wait_ge(ctx_in, 16)
                act.wait_ge(lam_ready, l + 1)
                nc.scalar.activation(small[:, 6:8], small[:, 4:6], ACT.Exp).then_inc(lam_exp, 1)
                act.wait_ge(x_ready, X_READS + 16 * l)
                for c in range(KC):
                    nc.scalar.activation(QK[:, 8 + c, :], X[:, c, :], ACT.Square).then_inc(sq_ready, 1)
                root(3, TOK, 1.0 / D, 1)

                def gate_half(at):
                    if at.u % 2 == 0:
                        act.wait_ge(slab_done, at.full())
                        if at.g >= 4:
                            act.wait_ge(*At(at.L, at.g - 3, at.u + 1, None).emptied())
                        nc.scalar.activation(TMP[:, at.g // 2 % 2, 0:w], bank[0][:, 0:w],
                                             ACT.Sigmoid).then_inc(emptied["scalar"], 1)

                for g in range(8):
                    gate_half(At(LIN[f"glu_{l}"], g, g % 6, None))
                copies(f"q_{l}", lambda at: QK[:, at.g, 0:w])
                copies(f"k_{l}", lambda at: QK[:, at.g + 8, :])
                n["stat"] += 1
                squares(lambda c: CV[:, c, 0:w], lambda c: PM[:, c, 0:w], 4, cent_ready)
                copies(f"v_{l}", lambda at: VT[:, :, at.g * P:(at.g + 1) * P])
                root(3, w, 1.0 / 512, 1)
                for c in range(4):
                    n["norm"] += 1
                    act.wait_ge(norm_ready, n["norm"])
                    nc.scalar.activation(CV[:, c, 0:w], CV[:, c, 0:w], ACT.Silu, scale=vcol(l, V2["conv_ln_g"] + c),
                                         bias=vcol(l, V2["conv_ln_b"] + c)).then_inc(silu_c, 1)
                act.wait_ge(pad_ready, l + 1)
                copies(f"p_{l}", lambda at: PP[:, at.g, 0:ns, POOL_PAD:POOL_PAD + S])

                def gate(at):
                    act.wait_ge(slab_done, at.full())
                    nc.scalar.activation(G[:, at.g, 0:w], bank[at.u % 2][:, 0:w], ACT.Sigmoid,
                                         bias=vcol(l, at.g + V2["b_gate"])).then_inc(emptied["scalar"], 1)

                turns(act, LIN[f"gate_{l}"], gate)

                def scaled(at):
                    act.wait_ge(slab_done, at.full())
                    nc.scalar.activation(PM[:, at.g, 0:w], bank[at.u % 2][:, 0:w], ACT.Copy,
                                         scale=vcol(l, at.g + V2["pool_scale"])).then_inc(emptied["scalar"], 1)

                turns(act, LIN[f"group_{l}"], scaled)
                attend(ATT[f"diff_{l}"], l)
                act.wait_ge(o_ready, n["unit"])
                for h in range(8):
                    nc.scalar.activation(QK[:, h, 0:w], O[:, h, 0:w], ACT.Square).then_inc(sub_sq, 1)
                for h in range(8):
                    if h >= 2:
                        act.wait_ge(norm_ready, n["norm"] + h - 1)
                    root(2 + h % 2, w, 1.0 / P, 1, h % 2)
                n["norm"] += 8

                def plain(name):
                    def one(at):
                        act.wait_ge(slab_done, at.full())
                        src = bank[at.u % 2][:, 0:w]
                        nc.scalar.copy(QK[:, at.g, 0:w], src)
                        nc.scalar.activation(QK[:, at.g + 8, 0:w], src, ACT.Square).then_inc(emptied["scalar"], 1)

                    turns(act, LIN[name], one)
                    root(3, w, 1.0 / D, 1)

                plain(f"out_{l}")
                for c in range(KC):
                    act.wait_ge(x_ready, X_READS + 16 * l + c + 1)
                    nc.scalar.activation(QK[:, 8 + c, 0:w], X[:, c, 0:w], ACT.Square).then_inc(sq_ready, 1)
                root(3, w, 1.0 / D, 1)

                def silu_half(at):
                    if at.u % 2 == 0:
                        act.wait_ge(slab_done, at.full())
                        if not (isinstance(at.g, int) and at.g < 6):
                            act.wait_ge(emptied["vector"], at.over(2) + (at.L.empty0["vector"] - 2))
                        nc.scalar.activation(QK[:, at.u, 0:w], bank[0][:, 0:w],
                                             ACT.Silu).then_inc(emptied["scalar"], 1)

                turns(act, LIN[f"up2_{l}"], silu_half)
                plain(f"down2_{l}")

        @block.vector
        def _(dve):
            v = nc.vector
            n = Tally()
            own = Own(dve, dve_own)

            def modulation(name, vl):
                L = LIN[name]

                def one(at):
                    dve.wait_ge(slab_done, at.full())
                    v.tensor_scalar(mod[:, bass.ds(at.g * 2, 2)], bank[at.u % 2][:, 0:2], vcol(vl, at.g), None,
                                    ALU.add).then_inc(emptied["vector"], 1)

                turns(dve, L, one)
                dve.wait_ge(emptied["vector"], L.empty0["vector"] + 48)

            def modulate(k, shift, ns, src=None):
                for c in range(KC):
                    for s in range(ns):
                        cols = slice(s * S, s * S + S)
                        ins = v.tensor_scalar(H[:, c, cols], (X if src is None else src)[:, c, cols], MD[:, k, c, s:s + 1],
                                              MOD[:, shift + c, s:s + 1], ALU.mult, ALU.add)
                    ins.then_inc(h_ready, 1)

            def residual(name, w):
                L = LIN[name]

                def one(at):
                    dve.wait_ge(*at.emptied())
                    xs = X[:, at.g, 0:w]
                    v.scalar_tensor_tensor(xs, xs, ALPHA, TMP[:, at.u % 2, 0:w], ALU.mult, ALU.add).then_inc(row_ready, 1)

                turns(dve, L, one)
                n["row"] += KC
                dve.wait_ge(row_ready, n["row"])

            def centre(buf, chunks, w, scale):
                n["stat"] += 1
                dve.wait_ge(stat_done, n["stat"])
                for c in range(chunks):
                    v.scalar_tensor_tensor(buf[:, c, 0:w], bank[2][:, 0:w], -scale, buf[:, c, 0:w], ALU.mult,
                                           ALU.add).then_inc(cent_ready, 1)
                n["cent"] += chunks
                dve.wait_ge(cent_ready, n["cent"])

            def inverse(w, slot=0):
                n["root"] += 1
                n["stat"] += 1
                dve.wait_ge(root_ready, n["root"])
                own.link(v.reciprocal(RS[:, slot, 0:w], RS[:, slot, 0:w]))

            def normed(buf, chunks, w):
                for c in range(chunks):
                    v.tensor_tensor(buf[:, c, 0:w], buf[:, c, 0:w], RS[:, 0, 0:w], ALU.mult).then_inc(norm_ready, 1)
                n["norm"] += chunks

            def layer_norm(w):
                centre(X, KC, w, 1.0 / D)
                inverse(w)
                normed(X, KC, w)
                n["x"] += KC
                dve.wait_ge(x_ready, n["x"])

            def rope(chunk, count):
                for j in range(count):
                    n["rope"] += 1
                    dve.wait_ge(rope_mm, n["rope"])
                    t = TMP[:, n["rope"] % 2, 0:S]
                    own.inc(v.tensor_tensor(t, bank[2 + n["rope"] % 2][:, 0:S], SIN, ALU.mult))
                    own.link(v.tensor_tensor(chunk(j), chunk(j), COS, ALU.mult))
                    v.tensor_tensor(chunk(j), chunk(j), t, ALU.add).then_inc(rope_done, 1)

            def attend(units, lam=None):
                spu = len(units[0]["subs"])
                j0, u0 = n["sub"], n["unit"]

                def maxima(u):
                    unit = units[u]
                    w = unit["T"]
                    for i in range(spu):
                        j = u * spu + i
                        dve.wait_ge(sc_done, j0 + j + 1)
                        sc = SCORES[j % 4]
                        if unit["mask"] is not None:
                            own.link(v.tensor_tensor(sc[:, 0:S], sc[:, 0:S], unit["mask"], ALU.add))
                        m = smax[:, j % 64:j % 64 + 1]
                        own.link(v.reduce_max(m, sc[:, 0:w], AX_X))
                        if unit["sink"] is not None:
                            k = unit["sink"]
                            ins = v.tensor_scalar(m, m, -SCALE, nsink[:, k:k + 1], ALU.mult, ALU.min)
                        else:
                            ins = v.tensor_scalar(m, m, -SCALE, None, ALU.mult)
                        ins.then_inc(nm_ready, 1)

                def norm(u):
                    unit = units[u]
                    w = unit["T"]
                    j = u * spu
                    dve.wait_ge(ex_ready, j0 + j + spu)
                    cols = slice(j % 64, j % 64 + spu)
                    if unit["sink"] is not None:
                        own.link(v.tensor_tensor(ssum[:, cols], ssum[:, cols], ssink[:, cols], ALU.add))
                    own.link(v.reciprocal(srec[:, cols], ssum[:, cols]))
                    p0, r0 = PROB[j % 6][:, 0:w], srec[:, j % 64:j % 64 + 1]
                    if not unit["diff"]:
                        v.tensor_scalar(p0, p0, r0, None, ALU.mult).then_inc(pr_ready, 1)
                        return
                    p1, r1 = PROB[(j + 1) % 6][:, 0:w], srec[:, j % 64 + 1:j % 64 + 2]
                    own.inc(v.tensor_tensor(r1, r1, lam, ALU.mult))
                    own.link(v.tensor_scalar(p0, p0, r0, None, ALU.mult))
                    v.scalar_tensor_tensor(p1, p1, r1, p0, ALU.mult, ALU.add).then_inc(pr_ready, 1)

                def store(u):
                    dve.wait_ge(pv_done, u0 + u + 1)
                    v.tensor_copy(units[u]["out"], OUTB[u % 2][units[u]["rows"], 0:P]).then_inc(o_ready, 1)

                for u in range(AHEAD):
                    maxima(u)
                norm(0)
                for u in range(len(units)):
                    if u + AHEAD < len(units):
                        maxima(u + AHEAD)
                    if u + 1 < len(units):
                        norm(u + 1)
                    if u:
                        store(u - 1)
                store(len(units) - 1)
                n["sub"] += len(units) * spu
                n["unit"] += len(units)

            v.memset(small[:, 0:1], LN_EPS).then_inc(small_ready, 1)
            v.memset(small[:, 1:2], RMS_EPS).then_inc(small_ready, 1)
            dve.wait_ge(const_in, 16)
            dve.wait_ge(vec_in, 32)
            v.tensor_scalar(nsink[:, :], vcol(1, V1["sink"], 16), -1.0, None, ALU.mult).then_inc(small_ready, 1)
            dve.wait_ge(small_ready, 3)
            for l in range(2):
                w, ns = (TOK, 2) if l == 0 else (S, 1)
                modulation(f"mod1_{l}", l)
                own.inc(v.tensor_scalar(MD[:, 0, :, :], MOD[:, 8:16, :], 1.0, None, ALU.add))
                own.link(v.tensor_scalar(MD[:, 1, :, :], MOD[:, 32:40, :], 1.0, None, ALU.add))
                if l == 0:
                    dve.wait_ge(x_in, 16)
                modulate(0, 0, 2)
                if l == 0:
                    dve.wait_ge(bias_in, 16 * (8 * 4))
                    dve.wait_ge(mask_in, 32)
                    for h in range(8):
                        ins = v.scalar_tensor_tensor(BIAS[:, h, :, :], BIAS[:, h, :, :], 1.0 / SCALE, MASKB, ALU.mult, ALU.add)
                    ins.then_inc(bias_ready, 1)
                    dve.wait_ge(bias_ready, 1)
                    for j in range(5):
                        gain = vcol(0, V1["q_gain"] if j < 4 else V1["k_gain"])
                        dve.wait_ge(hroot_ready, j + 1)
                        own.link(v.reciprocal(RS[:, j % 2, :], RS[:, j % 2, :]))
                        v.scalar_tensor_tensor(G[:, j, :], G[:, j, :], gain, RS[:, j % 2, :], ALU.mult,
                                               ALU.mult).then_inc(hnorm_done, 1)
                    dve.wait_ge(hnorm_done, 5)
                    rope(lambda j: G[:, j, 0:S], 5)
                    attend(ATT["global"])
                    attend(ATT["near"])
                else:
                    dve.wait_ge(mask_in, 32)
                    rope(lambda j: G[:, j, 0:S], 9)
                    attend(ATT["window"])
                residual(f"mix1_{l}", w)
                layer_norm(w)
                modulate(1, 24, ns)

                def conv3(at):
                    dve.wait_ge(tap_ready, at.g + (n["tap"] + 1))
                    y, u = streams(QK[:, at.u, 0:w], ns), streams(bank[at.u % 2][:, 0:w], ns)
                    v.scalar_tensor_tensor(y[:, :, 1:S], u[:, :, 0:S - 1], vcol(l, at.g + V1["conv_w"]),
                                           y[:, :, 1:S], ALU.mult, ALU.add).then_inc(tap_left, 1)
                    dve.wait_ge(tap_left, at.g + (n["tap"] + 1))
                    v.scalar_tensor_tensor(y[:, :, 0:S - 1], u[:, :, 1:S], vcol(l, at.g + (V1["conv_w"] + 4 * FC)),
                                           y[:, :, 0:S - 1], ALU.mult, ALU.add).then_inc(emptied["vector"], 1)
                    if at.u % 2:
                        dve.wait_ge(*at.emptied())
                        dve.wait_ge(sig_ready, at.over(2) + (n["sig"] + 1))
                        v.tensor_tensor(G[:, at.over(2), 0:w], QK[:, at.u - 1, 0:w], QK[:, 6 + at.u // 2, 0:w],
                                        ALU.mult).then_inc(hid_ready, 1)

                turns(dve, LIN[f"up1_{l}"], conv3)
                n["tap"] += 2 * FC
                n["sig"] += FC
                residual(f"down1_{l}", w)
                layer_norm(w)
            for l in range(2):
                w, ns = (TOK, 2) if l == 0 else (S, 1)
                if l == 0:
                    dve.wait_ge(lam_in, 16)
                own.link(v.tensor_tensor(LAM[:, l, 0:2, :], LAM[:, l, 0:2, :], LAM[:, l, 2:4, :], ALU.mult))
                v.tensor_reduce(small[:, 4:6], LAM[:, l, 0:2, :], AX_X, ALU.add).then_inc(lam_ready, 1)
                dve.wait_ge(lam_exp, l + 1)
                own.link(v.tensor_tensor(small[:, 8:9], small[:, 7:8], small[:, 6:7], ALU.subtract))
                own.link(v.tensor_scalar(small[:, 9:10], small[:, 8:9], -LAM_INIT[l], None, ALU.add))
                minus_lam = small[:, 9:10]
                dve.wait_ge(vec_in, 16 * (l + 3))
                modulation(f"mod2_{l}", l)
                for s in range(2):
                    for k, j, gain in ((0, 8, "g_pre_mix"), (1, 32, "g_pre_ffn")):
                        own.inc(v.scalar_tensor_tensor(MD[:, k, :, s], MOD[:, j:j + 8, s], 1.0, vcol(l, V2[gain], 8),
                                                       ALU.add, ALU.mult))
                    for k, j, gain in ((2, 16, "g_post_mix"), (3, 40, "g_post_ffn")):
                        own.inc(v.tensor_tensor(MD[:, k, :, s], MOD[:, j:j + 8, s], vcol(l, V2[gain], 8), ALU.mult))
                own.link(v.tensor_scalar(small[:, 10:11], vcol(l, V2["subln_g"]), 1.0 - LAM_INIT[l], None, ALU.mult))

                def pre_norm(k, shift, w, ns):
                    inverse(w)
                    for c in range(KC):
                        own.inc(v.tensor_tensor(H[:, c, 0:w], X[:, c, 0:w], RS[:, 0, 0:w], ALU.mult))
                    own.wait(own.n)
                    modulate(k, shift, ns, H)

                if l == 0:
                    dve.wait_ge(ctx_in, 16)
                pre_norm(0, 0, TOK, 2)
                own.link(v.memset(BIG[:, 0:8 * UW], 0.0))
                for i in range(4):
                    g = 2 * i + 1
                    at = At(LIN[f"glu_{l}"], g, g % 6, None)
                    dve.wait_ge(slab_done, at.full())
                    dve.wait_ge(*At(at.L, g - 1, (g - 1) % 6, None).emptied())
                    v.tensor_tensor(U[:, i, 0:ns, CONV_PAD:CONV_PAD + S], streams(bank[1][:, 0:w], ns),
                                    streams(TMP[:, i % 2, 0:w], ns), ALU.mult).then_inc(emptied["vector"], 1)
                dve.wait_ge(emptied["vector"], LIN[f"glu_{l}"].empty0["vector"] + 4)

                def cvs(c):
                    return streams(CV[:, c, 0:w], ns)

                for c in range(4):
                    own.inc(v.tensor_scalar(cvs(c), U[:, c, 0:ns, 0:S], vcol(l, V2["conv_w"] + c * CONV_TAPS),
                                            vcol(l, V2["conv_b"] + c), ALU.mult, ALU.add))
                base = own.n
                with dve.Fori(1, CONV_TAPS - 1) as k:
                    for c in range(4):
                        dve.wait_ge(dve_own, k * 4 + (base - 8 + c + 1))
                        v.scalar_tensor_tensor(cvs(c), U[:, c, 0:ns, bass.ds(k, S)],
                                               vcol(l, k + (V2["conv_w"] + c * CONV_TAPS)), cvs(c),
                                               ALU.mult, ALU.add).then_inc(dve_own, 1)
                own.n += 4 * (CONV_TAPS - 2)
                k = CONV_TAPS - 1
                for c in range(4):
                    own.wait(own.n - 3 + c)
                    v.scalar_tensor_tensor(cvs(c), U[:, c, 0:ns, k:k + S], vcol(l, k + V2["conv_w"] + c * CONV_TAPS),
                                           cvs(c), ALU.mult, ALU.add).then_inc(conv_ready, 1)
                n["conv"] += 4
                dve.wait_ge(conv_ready, n["conv"])
                centre(CV, 4, w, 1.0 / 512)
                inverse(w)
                normed(CV, 4, w)
                dve.wait_ge(emptied["scalar"], LIN[f"k_{l}"].empty0["scalar"] + 8)
                rope(lambda j: QK[:, j, 0:S], 16)
                dve.wait_ge(rope_done, n["rope"])
                attend(ATT[f"diff_{l}"], minus_lam)
                for h in range(8):
                    inverse(w, h % 2)
                    v.scalar_tensor_tensor(O[:, h, 0:w], O[:, h, 0:w], small[:, 10:11], RS[:, h % 2, 0:w],
                                           ALU.mult, ALU.mult).then_inc(norm_ready, 1)
                n["norm"] += 8

                def merge(at):
                    c = at.over(3)
                    dve.wait_ge(slab_done, at.full())
                    b, m = bank[at.u % 2][:, 0:w], H[:, c, 0:w]
                    part = at.u % 3
                    if part == 0:
                        v.tensor_tensor(m, b, G[:, c, 0:w], ALU.mult).then_inc(emptied["vector"], 1)
                        return
                    t = TMP[:, part - 1, 0:w]
                    v.tensor_tensor(t, b, G[:, c + (16, 8)[part - 1], 0:w], ALU.mult).then_inc(emptied["vector"], 1)
                    dve.wait_ge(*at.emptied())
                    if part == 2:
                        dve.wait_ge(merge_step, c * 2 + (n["merge"] + 1))
                    v.tensor_tensor(m, m, t, ALU.add).then_inc(merge_step, 1)

                turns(dve, LIN[f"merge_{l}"], merge)
                n["merge"] += 16

                def post_norm(k):
                    inverse(w)
                    for c in range(KC):
                        own.inc(v.tensor_tensor(QK[:, c, 0:w], QK[:, c, 0:w], RS[:, 0, 0:w], ALU.mult))
                    for c in range(KC):
                        own.wait(own.n - KC + 1 + c)
                        for s in range(ns):
                            cols = slice(s * S, s * S + S)
                            ins = v.scalar_tensor_tensor(X[:, c, cols], QK[:, c, cols], MD[:, k, c, s:s + 1], X[:, c, cols],
                                                         ALU.mult, ALU.add)
                        ins.then_inc(x_ready, 1)
                    n["x"] += KC
                    dve.wait_ge(x_ready, n["x"])

                post_norm(2)
                pre_norm(1, 24, w, ns)

                def hidden(at):
                    if at.u % 2:
                        dve.wait_ge(slab_done, at.full())
                        who = emptied["scalar"]
                        dve.wait_ge(who, at.over(2) + (at.L.empty0["scalar"] + 1))
                        v.tensor_tensor(G[:, at.over(2), 0:w], bank[1][:, 0:w], QK[:, at.u - 1, 0:w],
                                        ALU.mult).then_inc(emptied["vector"], 1)

                turns(dve, LIN[f"up2_{l}"], hidden)
                post_norm(3)

        @block.gpsimd
        def _(pool):
            g = nc.gpsimd
            own = Own(pool, pool_step)
            pool.dma_start(con[:, :], T["consts"]).then_inc(const_in, 16)
            pool.dma_start(vec[:, 0:NV1], T["vecs1"][0]).then_inc(vec_in, 16)
            pool.dma_start(vec[:, NV:NV + NV1], T["vecs1"][1]).then_inc(vec_in, 16)
            pool.dma_start(X[:, :, :], T["x"]).then_inc(x_in, 16)
            pool.dma_start(MASKB, T["masks"][0]).then_inc(mask_in, 16)
            pool.dma_start(MASKC, T["masks"][1]).then_inc(mask_in, 16)
            rpb = T["rpb"]
            wide = rpb.shape[2] // GRID_W
            for h in range(8):
                for qt in range(2):
                    for r in range(2):
                        row = 2 * qt + r
                        src = bass.AP(rpb.tensor, (h * 15 + 7 - row) * GRID_W * wide + wide // 2,
                                      [[wide - 1, GRID_W], [GRID_W * wide, 4], [1, GRID_W]])
                        dst = BIAS[GRID_W * r:GRID_W * r + GRID_W, h, qt, :].rearrange("p (k c) -> p k c", k=4)
                        pool.dma_start(dst, src).then_inc(bias_in, 16)
            pool.dma_start(lamv[:, :], T["lam"]).then_inc(lam_in, 16)
            for l in range(2):
                pool.wait_ge(x_ready, 16 * (l + 1))
                pool.dma_start(vec[:, l * NV:l * NV + NV2], T["vecs2"][l]).then_inc(vec_in, 16)
                if l == 1:
                    pool.dma_start(X[:, :, S:TOK], T["ctx2"]).then_inc(ctx_in, 16)
            for l in range(2):
                ns = 2 - l
                pool.wait_ge(h_ready, 4 * KC + KC + 2 * KC * l)
                g.memset(O_[:, 0:12 * PW], 0.0).then_inc(pad_ready, 1)
                L = LIN[f"p_{l}"]
                for i in range(4):
                    pool.wait_ge(emptied["scalar"], L.empty0["scalar"] + i + 1)
                    src, width, last = PP[:, i, 0:ns, :], PW, 1
                    for d in range(i + 1):
                        dst = (PT0, PT1)[d % 2][:, 0:ns, :]
                        width -= last
                        own.link(g.tensor_tensor(dst[:, :, 0:width], src[:, :, 0:width], src[:, :, last:last + width], ALU.add))
                        src, last = dst, 2 * last
                    half = POOL_WINDOWS[i] // 2
                    win = src[:, :, POOL_PAD - half:POOL_PAD - half + S]
                    out = streams(PM[:, i, 0:ns * S], ns)
                    own.link(g.tensor_scalar(out, win, 1.0 / POOL_WINDOWS[i], None, ALU.mult))
                    for e in range(2):
                        cols = slice(0, POOL_PAD) if e == 0 else slice(S - POOL_PAD, S)
                        at = C_EDGE + (2 * i + e) * POOL_PAD
                        for s in range(ns):
                            own.inc(g.tensor_tensor(out[:, s, cols], out[:, s, cols], con[:, at:at + POOL_PAD], ALU.mult))
                    own.wait(own.n)
                    g.tensor_tensor(out, out, PP[:, i, 0:ns, POOL_PAD:POOL_PAD + S], ALU.subtract).then_inc(pool_ready, 1)


def kernel(**inputs):
    import concourse.bacc as bacc
    from concourse.bass_utils import run_bass_kernel_spmd

    a = {k: np.asarray(v) for k, v in inputs.items()}

    def by_feature(x):
        return x.T.reshape(-1, P, x.shape[0]).transpose(1, 0, 2)

    def cols(x):
        return x.reshape(-1, P).T

    def pack(w, order=None):
        k, m = w.shape
        t = w.reshape(k // P, P, m // P, P).transpose(2, 1, 0, 3)
        if order is not None:
            t = t[order]
        return t.reshape(t.shape[0], P, k)

    def zip_groups(n):
        return [i + n * j for i in range(n) for j in range(2)]

    def paired(w, heads, axis):
        shape = w.shape
        t = w.reshape(shape[:axis] + (heads, HD) + shape[axis + 1:])
        order = [i + heads // 2 * j for i in range(heads // 2) for j in range(2)]
        return np.take(t, order, axis).reshape(shape)

    arrays = {}
    x = np.concatenate([by_feature(a["x"][0]), by_feature(a["ctx"][0])], 2)
    arrays["x"] = x
    arrays["ctx2"] = by_feature(a["ctx_2"][0])
    arrays["cvecs"] = np.concatenate([np.stack([cols(a["c" + s][0]), cols(a["c_ctx" + s])], 2).reshape(P, 16)
                                      for s in ("", "_2")], 1)
    ew, eo = a["ev_w_in"][0], a["ev_w_out"][0]
    ev = np.concatenate([paired(ew[:, 0:512], 8, 1), ew[:, 512:]], 1)
    arrays["w_ev_qk"] = pack(ev, [0, 1, 2, 3, 4, 6, 7, 8, 9, 10, 11, 12, 13])
    arrays["w_ev_v"] = pack(ev, [5, 14, 15, 16, 17])
    arrays["w_mix1_0"] = pack(np.concatenate([paired(eo[0:512], 8, 0), eo[512:]], 0))
    ow = a["od_w_in"][0]
    arrays["w_od_q"] = pack(paired(ow[:, 0:D], 16, 1))
    arrays["w_od_k"] = pack(ow[:, D:D + P])
    arrays["w_od_v"] = pack(ow[:, D + P:])
    arrays["w_mix1_1"] = pack(paired(a["od_w_out"][0], 16, 0))
    vecs1, vecs2 = [], []
    two = zip_groups(FC)
    for l in range(2):
        arrays[f"w_mod1_{l}"] = pack(a["ada_w"][l])
        arrays[f"w_up1_{l}"] = pack(a["ffn_w_up"][l], two)
        arrays[f"w_down1_{l}"] = pack(a["ffn_w_down"][l])
        wide = lambda v: np.broadcast_to(v, (P, v.shape[-1]))
        vecs1.append(np.concatenate(
            [cols(a["ada_b"][l]), cols(a["ln_g"][l]), cols(a["ln_b"][l])]
            + [cols(a["ffn_conv_w"][l, j])[:, two] for j in range(3)]
            + [cols(a["ffn_conv_b"][l])[:, two]]
            + [np.concatenate([a[k][0], a[k][0]])[:, None] for k in ("ev_q_gain", "ev_k_gain")]
            + [wide(a["od_sink"][0])], 1))
        w = a["w_in_2"][l]
        arrays[f"w_mod2_{l}"] = pack(a["w_mod_2"][l])
        arrays[f"w_glu_{l}"] = pack(w[:, 0:1024], [i + 4 * j for i in range(4) for j in (1, 0)])
        for k, (lo, hi) in dict(q=(1024, 2048), k=(2048, 3072), v=(3072, 4096), p=(4096, 4608), gate=(4608, 7680)).items():
            arrays[f"w_{k}_{l}"] = pack(w[:, lo:hi])
        arrays[f"w_group_{l}"] = a["w_pool_group_2"][l]
        conv, att, pool = (pack(a[k][l]) for k in ("w_conv_out_2", "w_attn_out_2", "w_pool_out_2"))
        short = lambda t: np.concatenate([t, t], 2)
        arrays[f"w_merge_{l}"] = np.stack([short(conv), short(pool), att], 1).reshape(24, P, D)
        arrays[f"w_out_{l}"] = pack(a["w_out_2"][l])
        arrays[f"w_up2_{l}"] = pack(a["w_ffn_in_2"][l], two)
        arrays[f"w_down2_{l}"] = pack(a["w_ffn_out_2"][l])
        vecs2.append(np.concatenate(
            [cols(a["b_mod_2"][l])] + [cols(a[k + "_2"][l]) for k in ("g_pre_mix", "g_post_mix", "g_pre_ffn", "g_post_ffn")]
            + [cols(a["b_gate_2"][l]), a["conv_w_2"][l].T.reshape(4, P, CONV_TAPS).transpose(1, 0, 2).reshape(P, -1)]
            + [cols(a[k + "_2"][l]) for k in ("conv_b", "conv_ln_g", "conv_ln_b", "subln_g", "pool_scale")], 1))
    arrays["vecs1"], arrays["vecs2"] = np.stack(vecs1), np.stack(vecs2)
    arrays["lam"] = np.broadcast_to(
        np.concatenate([a[k + "_2"][l] for l in range(2) for k in ("lam_q1", "lam_q2", "lam_k1", "lam_k2")]), (P, 8 * HD))
    pad = GRID_W - 16
    arrays["rpb"] = np.tile(np.pad(a["ev_rpb"][0], ((0, 0), (0, 0), (pad, pad))), (1, 1, GRID_W))

    t = np.arange(S)
    half = HD // 2
    freq = (10000.0 ** (-np.arange(0, half, 2, dtype=np.float32) / np.float32(half))).astype(np.float32)
    by_row = (t // GRID_W).astype(np.float32)[:, None] * freq
    by_col = (t % GRID_W).astype(np.float32)[:, None] * freq
    ang = np.concatenate([by_row, by_row, by_col, by_col], 1).T
    rot = np.zeros((P, P), np.float32)
    for i in range(P):
        low = i % half < half // 2
        rot[i + half // 2 if low else i - half // 2, i] = -1.0 if low else 1.0
    head = np.kron(np.eye(2), np.ones((HD, HD)))
    edge = []
    for w in POOL_WINDOWS:
        count = np.clip(t + w // 2, 0, S) - np.clip(t - w // 2, 0, S)
        edge += [w / count[:POOL_PAD], w / count[-POOL_PAD:]]
    arrays["consts"] = np.concatenate(
        [np.tile(np.cos(ang), (2, 1)), np.tile(np.sin(ang), (2, 1)), np.ones((P, P)), np.eye(P), rot, head,
         np.broadcast_to(np.concatenate(edge), (P, 8 * POOL_PAD))], 1).astype(np.float32)
    col = t % GRID_W
    first = np.clip(col - 8, 0, GRID_W - 16)
    near = (col[None, :] >= first[:, None]) & (col[None, :] < first[:, None] + 16)
    window = np.abs(t[None, :] - t[:, None]) <= 128
    arrays["masks"] = np.stack([np.where(m, 0.0, NEG).astype(np.float32).reshape(2, P, S).transpose(1, 0, 2)
                                for m in (near, window)])

    nc = bacc.Bacc("TRN2", target_bir_lowering=False, num_devices=1)
    tensors, fed = {}, {}
    for k, v in arrays.items():
        v = np.ascontiguousarray(v)
        fed["in_" + k] = v
        tensors[k] = nc.dram_tensor("in_" + k, v.shape, F32, kind="ExternalInput").ap()
    tensors["out"] = nc.dram_tensor("out", (P, KC, S), F32, kind="ExternalOutput").ap()
    build(nc, tensors)
    r = run_bass_kernel_spmd(nc, [fed], core_ids=[0])
    y = r.results[0]["out"]
    return np.ascontiguousarray(y.transpose(2, 1, 0).reshape(1, S, D))
```

```python
from contextlib import ExitStack
import math

import numpy as np

import concourse.bass as bass
from concourse import mybir

F32 = mybir.dt.float32
F32R = mybir.dt.float32r
ALU = mybir.AluOpType
ACT = mybir.ActivationFunctionType
AX_X = mybir.AxisListType.X

P = 128
D = 1024
KC = D // P
S = 256
TOK = 2 * S
TT = TOK // P
HD = 64
FF = 2816
FC = FF // P
GRID_W = 64
ALPHA = 4.0 ** 0.25
LN_EPS = 1e-5
RMS_EPS = 1e-6
SCALE = HD ** -0.5
NEG = -1e30
CONV_TAPS = 31
CONV_PAD = CONV_TAPS // 2
POOL_PAD = 8
POOL_WINDOWS = (2, 4, 8, 16)
LAM_INIT = [0.8 - 0.6 * math.exp(-0.3 * l) for l in range(2)]

RING = 4
AHEAD_SLABS = 2
SLAB = 8
DOWN = [6, 5, 6, 5]

def columns(spec):
    at, out = 0, {}
    for name, n in spec:
        out[name] = at
        at += n
    return out, at


V1, NV1 = columns([("mod_b", 48), ("ln_g", 16), ("ln_b", 16), ("conv_w", 3 * 2 * FC), ("conv_b", 2 * FC),
                   ("q_gain", 1), ("k_gain", 1), ("sink", 16)])
V2, NV2 = columns([("mod_b", 48), ("g_pre_mix", 8), ("g_post_mix", 8), ("g_pre_ffn", 8), ("g_post_ffn", 8),
                   ("b_gate", 24), ("conv_w", 4 * CONV_TAPS), ("conv_b", 4), ("conv_ln_g", 4), ("conv_ln_b", 4),
                   ("subln_g", 1), ("pool_scale", 4)])
NV = max(NV1, NV2)
C_COS, C_SIN, C_ONE, C_ID, C_ROT, C_HEAD, C_EDGE = 0, S, 2 * S, 2 * S + P, 2 * S + 2 * P, 2 * S + 3 * P, 2 * S + 4 * P
NCONST = C_EDGE + 4 * 2 * POOL_PAD


ROOTS, NORMS, X_READS = 4, 4 * KC, 4 * KC


class Linear:

    def __init__(self, name, groups, tiles, n, emptied, kind="features", halved=True):
        self.name, self.groups, self.tiles, self.n, self.kind, self.halved = name, groups, tiles, n, kind, halved
        self.emptied = emptied if isinstance(emptied, tuple) else (emptied, emptied)
        self.per = len(tiles)
        self.step = 12 if name.startswith("merge") else RING if self.per == 1 else 2

    def tiles_of(self, g, j):
        return self.tiles[j] if not self.name.startswith("merge") else (4, 4, 8)[g % 3]

    def halved_at(self, g):
        return self.halved and not (self.name.startswith("merge") and g % 3 < 2)


def plan_linears():
    plan = []

    def modulation(b, l, *parts):
        plan.extend(Linear(f"mod{b}_{l}_{i}", 4, [8] * 4, 2, "vector", "rows", False) for i in parts)

    modulation(1, 0, 0)
    for l in range(2):
        n = TOK if l == 0 else S
        if l == 0:
            plan += [Linear("ev_qk", 13, [8], TOK, "scalar"), Linear("ev_v", 5, [8], TOK, "scalar", "tokens")]
            modulation(1, 0, 1, 2)
        else:
            plan += [Linear("od_k", 1, [8], TOK, "scalar"), Linear("od_v", 1, [8], TOK, "scalar", "tokens"),
                     Linear("od_q", 8, [8], S, "scalar")]
            modulation(1, 1, 2)
        plan.append(Linear(f"mix1_{l}", 8, [8], n, "scalar"))
        modulation(*((1, 1, 0) if l == 0 else (2, 0, 0)))
        plan += [Linear(f"up1_{l}", 2 * FC, [8], n, "vector"), Linear(f"down1_{l}", 8, DOWN, n, "scalar")]
        modulation(*((1, 1, 1) if l == 0 else (2, 0, 1)))
    for l in range(2):
        n = TOK if l == 0 else S
        plan += [Linear(f"glu_{l}", 8, [8], n, ("scalar", "vector")), Linear(f"p_{l}", 4, [8], n, "scalar"),
                 Linear(f"q_{l}", 8, [8], n, "scalar"), Linear(f"k_{l}", 8, [8], TOK, "scalar"),
                 Linear(f"v_{l}", 8, [8], TOK, "scalar", "tokens"),
                 Linear(f"gate_{l}_0", 12, [8], n, "scalar"), Linear(f"gate_{l}_1", 12, [8], n, "scalar"),
                 Linear(f"group_{l}", 4, [1], n, "scalar", halved=False)]
        modulation(2, l, 2)
        plan += [Linear(f"merge_{l}", 24, [8], n, "vector"), Linear(f"out_{l}", 8, [8], n, "scalar")]
        if l == 0:
            modulation(2, 1, 0)
        plan += [Linear(f"up2_{l}", 2 * FC, [8], n, ("scalar", "vector")),
                 Linear(f"down2_{l}", 8, DOWN, n, "scalar")]
        if l == 0:
            modulation(2, 1, 1)
    slab, emptied, last, half = 0, {"scalar": 0, "vector": 0}, {0: None, 1: None}, 0
    for i, L in enumerate(plan):
        L.next = plan[i + 1] if i + 1 < len(plan) else None
        L.slab0, L.half0 = slab, half
        L.empty0 = dict(emptied)
        L.before = dict(last)
        slab += L.groups * L.per
        half += sum(L.halved_at(g) for g in range(L.groups)) * L.per
        if L.kind == "rows":
            continue
        for g in range(L.groups):
            emptied[L.emptied[g % 2]] += 1
            last[g % 2] = (L.emptied[g % 2], emptied[L.emptied[g % 2]])
    return {L.name: L for L in plan}, plan


def build(nc, T):
    LIN, ORDER = plan_linears()
    ctx = ExitStack()
    with ctx:
        def sem(name):
            return ctx.enter_context(nc.semaphore(name))

        bank = [ctx.enter_context(nc.psum_tensor(f"bank{i}", [P, 512], F32)) for i in range(8)]
        where = [-(-nc.sbuf_base // 32) * 32]

        def region(words):
            at = where[0]
            where[0] += -(-4 * words // 32) * 32
            return at

        def view(name, at, words, dt=F32):
            return nc.alloc_sbuf_tensor_at(name, [P, words], dt, offset=at)

        def sb(name, words):
            return view(name, region(words), words)

        R_H, R_L = region(KC * TOK), region(KC * TOK)
        R_1, R_2, R_C = region(24 * TOK), region(24 * TOK), region(8 * TOK)
        R_W, R_WH = region(RING * SLAB * P), region(RING * SLAB * P)
        X_ = sb("x", KC * TOK)
        BIG = view("big", R_1, 24 * TOK)
        QK_ = view("qk", R_2, 16 * TOK)
        VT_ = view("v_tokens", R_2 + 4 * 16 * TOK, TT * D)
        HF = view("h_space", R_H, KC * TOK)
        LF = view("l_space", R_L, KC * TOK)
        SC_ = view("conv_space", R_C, 8 * TOK)
        TMP_ = sb("tmp", 2 * TOK)
        RS_ = sb("rstd", TOK)
        raw = view("ring", R_W, RING * SLAB * P)
        vec = sb("vec", 2 * NV)
        con = sb("con", NCONST)
        mod = sb("mod", 4 * 96)
        mods = sb("mod_derived", 2 * 4 * 16)
        cvec = sb("cvec", 32)
        small = sb("small", 16)
        nsink = sb("minus_sink", 16)
        NS = 32
        smax = sb("smax", NS)
        ssum = sb("ssum", NS)
        srec = sb("srec", NS)
        ssink = sb("ssink", NS)
        assert where[0] <= nc.sbuf_usable_end
        HH_, HL_ = view("h_high", R_H, KC * TOK, F32R), view("h_low", R_L, KC * TOK, F32R)
        FH_, FL_ = view("f_high", R_1, FC * TOK, F32R), view("f_low", R_2, FC * TOK, F32R)
        OHL = view("o_halves", R_2, 16 * TOK, F32R)
        wh, wl = view("w_high", R_WH, RING * SLAB * P, F32R), view("w_low", R_W, RING * SLAB * P, F32R)

        def chunks(t, c):
            return t[:, :].rearrange("p (c n) -> p c n", c=c)

        X, QK, G, SC = chunks(X_, KC), chunks(QK_, 16), chunks(BIG, 24), chunks(SC_, 8)
        HH, HL, FH, FL, OH = chunks(HH_, KC), chunks(HL_, KC), chunks(FH_, FC), chunks(FL_, FC), chunks(OHL, 16)
        HS, O = chunks(HF, KC), chunks(LF, KC)
        CV, PM = SC[:, 0:4, :], SC[:, 4:8, :]
        TMP = chunks(TMP_, 2)
        ROOT = [RS_[:, :], TMP_[:, 0:TOK]]
        VT = VT_[:, :].rearrange("p (t d) -> p t d", t=TT)
        MOD = mod[:, :].rearrange("p (k j s) -> p k j s", k=4, s=2)
        MDS = mods[:, :].rearrange("p (l k c s) -> p l k c s", l=2, k=4, s=2)
        UW = S + 2 * CONV_PAD
        U = BIG[:, 0:4 * 2 * UW].rearrange("p (c s n) -> p c s n", c=4, s=2)
        PW = S + 2 * POOL_PAD
        PADS = BIG[:, 8 * UW:8 * UW + 12 * PW]
        PP = PADS[:, 0:8 * PW].rearrange("p (c s n) -> p c s n", c=4, s=2)
        PT0 = PADS[:, 8 * PW:10 * PW].rearrange("p (s n) -> p s n", s=2)
        PT1 = PADS[:, 10 * PW:12 * PW].rearrange("p (s n) -> p s n", s=2)
        LAM = TMP_[:, 0:8 * HD].rearrange("p (l j d) -> p l j d", l=2, j=4)
        BIAS = BIG[:, 13 * TOK:13 * TOK + 8 * 2 * S].rearrange("p (h q t) -> p h q t", h=8, q=2)
        MASKB = BIG[:, 22 * TOK:22 * TOK + 2 * S].rearrange("p (q t) -> p q t", q=2)
        MASKC = BIG[:, 23 * TOK:23 * TOK + 2 * S].rearrange("p (q t) -> p q t", q=2)
        COS, SIN = con[:, C_COS:C_COS + S], con[:, C_SIN:C_SIN + S]
        ONES, IDENT = con[:, C_ONE:C_ONE + P], con[:, C_ID:C_ID + P]
        ROT, HEADS = con[:, C_ROT:C_ROT + P], con[:, C_HEAD:C_HEAD + P]
        PROB = [HS[:, i, :] for i in range(6)]
        PROBT = [HS[:, 6 + i, :] for i in range(2)]
        SCORES = [bank[i] for i in (2, 3, 4, 0)]
        OUTB = [bank[7], bank[1]]

        def vcol(layer, at, n=1):
            return vec[:, bass.ds(at + NV * (layer % 2), n)]

        landed = [sem(f"slab_landed{i}") for i in range(RING)]
        slab_done = sem("slab_done")
        emptied = {"scalar": sem("banks_emptied_by_scalar"), "vector": sem("banks_emptied_by_vector")}
        act_step, dve_step, pool_step = sem("act_step"), sem("dve_step"), sem("pool_step")
        const_in, cvec_in, vec_in, mask_in, x_in, ctx_in = sem("const_in"), sem("cvec_in"), sem("vec_in"), sem("mask_in"), sem("x_in"), sem("ctx_in")
        bias_in, lam_in = sem("bias_in"), sem("lam_in")
        silu_c = sem("silu_c_ready")
        high_ready, low_ready = sem("weights_high_ready"), sem("weights_low_ready")
        t_ready, hh_ready = sem("values_to_halve"), sem("high_half_ready")
        h_ready = sem("both_halves_ready")
        rows_copied, mod_turned, mod_stored = sem("mod_rows_copied"), sem("mod_turned"), sem("mod_stored")
        row_ready = sem("residual_chunk_ready")
        cent_ready = sem("centred_chunk_ready")
        sq_ready = sem("square_chunk_ready")
        presum = sem("presum_ready")
        stat_done = sem("stat_done")
        root_ready = sem("root_ready")
        norm_ready = sem("normed_chunk_ready")
        x_ready = sem("x_chunk_ready")
        prod_ready, fh_ready = sem("hidden_product"), sem("hidden_high")
        rope_mm = sem("rope_product_done")
        rope_done = sem("rope_chunk_done")
        hsq_ready, hsum_done, hroot_ready, hnorm_done = sem("head_square"), sem("head_sum"), sem("head_root"), sem("head_norm")
        sc_done, nm_ready, ex_ready, pr_ready = sem("scores_done"), sem("max_ready"), sem("exp_ready"), sem("probs_ready")
        tr_done, pt_ready, pv_done, o_ready = sem("probs_turned"), sem("turned_copied"), sem("pv_done"), sem("o_ready")
        sig_ready, tap_ready = sem("sigmoid_ready"), sem("conv_centre_ready")
        hid_ready = sem("hidden_ready")
        conv_ready = sem("conv_ready")
        pad_ready, pool_ready = sem("pads_ready"), sem("pooled_ready")
        bias_ready = sem("bias_ready")
        lam_ready, lam_exp = sem("lam_ready"), sem("lam_exp")
        sub_sq = sem("subln_square")
        out_sem = sem("out_stored")

        act_own, dve_own = sem("act_own"), sem("dve_own")
        tap_left = sem("conv_left_tap_done")
        tap_done = sem("filter_tap_done")
        merge_step = sem("merge_sum_done")
        small_ready = sem("small_ready")

        class Own:

            def __init__(self, eng, s):
                self.eng, self.s, self.n = eng, s, 0

            def inc(self, ins):
                ins.then_inc(self.s, 1)
                self.n += 1
                return self.n

            def wait(self, n):
                self.eng.wait_ge(self.s, n)

            def link(self, ins):
                self.wait(self.inc(ins))

        class Tally(dict):

            def __missing__(self, k):
                return 0

        class At:

            def __init__(self, L, g, u, turn):
                self.L, self.g, self.u, self.turn = L, g, u, turn

            def over(self, k):
                return self.g // k if self.turn is None else self.turn * (self.L.step // k) + self.u // k

            def full(self):
                return self.g * self.L.per + (self.L.per + self.L.slab0)

            def emptied(self, back=0):
                L, who = self.L, self.L.emptied[self.u % 2]
                if L.emptied[0] == L.emptied[1]:
                    return emptied[who], self.g + (L.empty0[who] + 1 - back)
                return emptied[who], self.over(2) + (L.empty0[who] + 1 - back // 2)

            def slot(self, j):
                return (self.L.slab0 + self.u * self.L.per + j) % RING * SLAB * P

            def landed(self, j):
                L = self.L
                n = L.slab0 + (self.g if self.turn is None else self.u) * L.per + j
                use = n // RING + 1
                if self.turn is not None:
                    use = self.turn * (L.step * L.per // RING) + use
                s = landed[(L.slab0 + self.u * L.per + j) % RING]
                return s, use * 16

            def halved(self, j):
                L = self.L
                if L.name.startswith("merge"):
                    return L.half0 + self.g // 3 + 1
                return self.g * L.per + (L.half0 + j + 1)

            def later(self, k):
                L = self.L
                j = k % L.per
                if self.turn is not None:
                    u = self.u + k // L.per
                    return At(L, self.turn * L.step + u, u, self.turn), j
                g = self.g + k // L.per
                if g < L.groups:
                    return At(L, g, g % L.step, None), j
                if L.next is None or L.next.kind == "rows":
                    return None
                k -= (L.groups - self.g) * L.per
                N = L.next
                return At(N, k // N.per, k // N.per, None), k % N.per

        def turns(eng, L, body, ahead=None):
            def group(at):
                if ahead is not None:
                    for j in range(L.per):
                        ahead(at.later(j + AHEAD_SLABS))
                if body is not None:
                    body(at)

            whole = L.groups // L.step
            whole = whole if whole > 3 else 0
            for g in range(L.step if whole else L.groups):
                group(At(L, g, g % L.step, None))
            if whole:
                with eng.Fori(1, whole - 1) as turn:
                    for u in range(L.step):
                        group(At(L, turn * L.step + u, u, turn))
                for g in range((whole - 1) * L.step, L.groups):
                    group(At(L, g, g % L.step, None))

        def begin(L, ahead):
            for k in range(AHEAD_SLABS):
                ahead((At(L, k // L.per, k // L.per, None), k % L.per))

        def streams(ap, ns):
            return ap.rearrange("p (s n) -> p s n", s=ns)

        def units_pair(qchunk, kchunk, chunk0, vcols, tiles, mask, sink, shared):
            out = []
            for c in range(8 if sink else 4):
                for half in range(2):
                    rows = slice(HD * half, HD * half + HD)
                    for qt in tiles:
                        keys = slice(0, TOK) if qt < 2 else slice(S, TOK)
                        k0 = keys.start // P
                        m = None if qt >= 2 or mask is None else mask(2 * c + half, qt)
                        q = G[rows, qchunk + c, qt * P:(qt + 1) * P]
                        k = G[rows, kchunk + (0 if shared else c), keys]
                        v0 = vcols + (0 if shared else c * P) + HD * half
                        out.append(dict(
                            subs=[(q, k)], T=keys.stop - keys.start, mask=m, diff=False,
                            sink=(c + 8 * half) if sink else None,
                            v=[VT[:, k0 + t, v0:v0 + HD] for t in range((keys.stop - keys.start) // P)],
                            rows=rows, out=O[rows, chunk0 + c, qt * P:(qt + 1) * P]))
            return out

        def units_diff(tiles):
            out = []
            for h in range(8):
                for qt in tiles:
                    keys = slice(0, TOK) if qt < 2 else slice(S, TOK)
                    k0 = keys.start // P
                    subs = [(QK[HD * i:HD * i + HD, h, qt * P:(qt + 1) * P], QK[HD * i:HD * i + HD, 8 + h, keys])
                            for i in range(2)]
                    out.append(dict(subs=subs, T=keys.stop - keys.start, mask=None, diff=True, sink=None,
                                    v=[VT[:, k0 + t, h * P:(h + 1) * P] for t in range((keys.stop - keys.start) // P)],
                                    rows=slice(0, P), out=O[:, h, qt * P:(qt + 1) * P]))
            return out

        ATT = {
            "global": units_pair(0, 4, 0, 0, range(4), None, False, True),
            "near": units_pair(5, 9, 4, P, range(4), lambda h, qt: BIAS[:, h, qt, :], False, False),
            "window": units_pair(1, 0, 0, 0, range(2), lambda h, qt: MASKC[:, qt, :], True, True),
            "diff_0": units_diff(range(4)),
            "diff_1": units_diff(range(2)),
        }
        AHEAD = 2


        MODS = {"1_0_0": (6, SC[:, 7, :]), "1_0_1": (6, SC[:, 7, :]), "1_0_2": (7, SC[:, 6, :]), "1_1_2": (6, SC[:, 7, :]),
                "2_0_2": (6, HS[:, 7, :]), "2_1_2": (6, HS[:, 7, :])}
        for name in ("1_1_0", "1_1_1", "2_0_0", "2_0_1", "2_1_0", "2_1_1"):
            MODS[name] = (6, SC[:, 7, :])
        TAPS = [(k, c) for k in range(1, CONV_TAPS) for c in range(4)]
        TAP_SHARE = [{"q": 7, "k": 4, "v": 5}, {"q": 4, "k": 6, "v": 6}]
        for l in range(2):
            assert 8 * sum(TAP_SHARE[l].values()) >= len(TAPS)

        block = ctx.enter_context(nc.Block())

        @block.sync
        def _(sp):
            sp.dma_start(cvec[:, :], T["cvecs"]).then_inc(cvec_in, 16)
            for L in ORDER:
                w = T["w_" + L.name]

                def load(at):
                    for j in range(L.per):
                        n = at.g * L.per + (L.slab0 + j)
                        if not (isinstance(n, int) and n < RING):
                            sp.wait_ge(slab_done, n - (RING - 1))
                        words = L.tiles_of(at.u, j) * P
                        if L.kind == "rows":
                            src = w[at.g, j]
                        elif L.per == 1:
                            src = w[at.g]
                        else:
                            first = sum(L.tiles[:j]) * P
                            src = w[at.g, :, first:first + words]
                        sp.dma_start(raw[:, at.slot(j):at.slot(j) + words], src[:, 0:words]).then_inc(at.landed(j)[0], 16)

                turns(sp, L, load)
            sp.wait_ge(x_ready, X_READS + 32)
            sp.dma_start(T["out"], X[:, :, 0:S]).then_inc(out_sem, 16)
            sp.wait_ge(out_sem, 16)

        @block.tensor
        def _(pe):
            n = Tally()

            def linear(name, rhs, waits=(), extra=None):
                L = LIN[name]
                for s, v in waits:
                    pe.wait_ge(s, v)

                def group(at):
                    b = bank[at.u % 2]
                    if isinstance(at.g, int) and at.g < 2:
                        if L.before[at.u % 2] is not None:
                            who, count = L.before[at.u % 2]
                            pe.wait_ge(emptied[who], count)
                    else:
                        pe.wait_ge(*at.emptied(back=2))
                    kc = 0
                    for j in range(L.per):
                        if L.halved_at(at.u):
                            pe.wait_ge(low_ready, at.halved(j))
                        else:
                            pe.wait_ge(*at.landed(j))
                        tiles = L.tiles_of(at.u, j)
                        for i in range(tiles):
                            cols = slice(at.slot(j) + i * P, at.slot(j) + (i + 1) * P)
                            first = kc == 0
                            last = j == L.per - 1 and i == tiles - 1
                            if L.kind == "tokens":
                                for t in range(TT):
                                    out, tok = b[:, t * P:(t + 1) * P], slice(t * P, (t + 1) * P)
                                    pe.matmul(out, HH[:, kc, tok], wh[:, cols], start=(first and t == 0), stop=False,
                                              skip_group_check=True)
                                    pe.matmul(out, HL[:, kc, tok], wh[:, cols], start=False, stop=False, skip_group_check=True)
                                    ins = pe.matmul(out, HH[:, kc, tok], wl[:, cols], start=False, stop=last,
                                                    skip_group_check=True)
                            elif L.halved_at(at.u):
                                high, low = rhs(kc, at)
                                pe.matmul(b[:, 0:L.n], wh[:, cols], high, start=first, stop=False)
                                pe.matmul(b[:, 0:L.n], wh[:, cols], low, start=False, stop=False)
                                ins = pe.matmul(b[:, 0:L.n], wl[:, cols], high, start=False, stop=last)
                            else:
                                ins = pe.matmul(b[:, 0:L.n], raw[:, cols], rhs(kc, at), start=first, stop=last)
                            kc += 1
                        ins.then_inc(slab_done, 1)
                    if extra is not None:
                        extra(at.g)

                turns(pe, L, group)

            def mod_rows(name, groups=range(4)):
                L, (b, _) = LIN["mod" + name], MODS[name]
                for g in groups:
                    at = At(L, g, g % L.step, None)
                    for j in range(L.per):
                        pe.wait_ge(*at.landed(j))
                        for i in range(2):
                            kc = 2 * j + i
                            vec0 = 16 * (int(name[0]) - 1) + 2 * kc
                            ins = pe.matmul(bank[b][32 * g:32 * g + 2, :], cvec[:, vec0:vec0 + 2],
                                            raw[:, at.slot(j) + 512 * i:at.slot(j) + 512 * (i + 1)],
                                            start=(kc == 0), stop=(kc == KC - 1))
                        ins.then_inc(slab_done, 1)

            def mod_turn(name):
                b, space = MODS[name]
                n["rows"] += 4
                pe.wait_ge(rows_copied, n["rows"])
                for g in range(4):
                    q = slice(32 * g, 32 * g + 2)
                    if g:
                        pe.wait_ge(mod_turned, n["rows"] - 4 + g)
                    for i in range(4):
                        col = (4 * g + i) * 2
                        ins = pe.transpose(bank[b][:, col:col + 2], space[q, i * P:(i + 1) * P], IDENT[q, q])
                    ins.then_inc(mod_turned, 1)

            def stat(src, chunks, width, ready, b):
                for c in range(chunks):
                    n[ready] += 1
                    pe.wait_ge(ready, n[ready])
                    ins = pe.matmul(bank[b][:, 0:width], ONES, src(c), start=(c == 0), stop=(c == chunks - 1))
                ins.then_inc(stat_done, 1)

            def rope(chunk, after):
                n["rope"] += 1
                pe.wait_ge(*after)
                if n["rope"] > 2:
                    pe.wait_ge(rope_done, n["rope"] - 2)
                pe.matmul(bank[2 + n["rope"] % 2][:, 0:S], ROT, chunk, start=True, stop=True).then_inc(rope_mm, 1)

            def attend(units):
                spu = len(units[0]["subs"])
                j0, u0 = n["sub"], n["unit"]

                def scores(u):
                    for i, (q, k) in enumerate(units[u]["subs"]):
                        j = u * spu + i
                        if j >= 4:
                            pe.wait_ge(ex_ready, j0 + j - 3)
                        pe.matmul(SCORES[j % 4][:, 0:units[u]["T"]], q, k, start=True, stop=True).then_inc(sc_done, 1)

                def turn(u):
                    pe.wait_ge(pr_ready, u0 + u + 1)
                    if u >= 2:
                        pe.wait_ge(pt_ready, u0 + u - 1)
                    src = PROB[(u * spu + spu - 1) % 6]
                    for t in range(units[u]["T"] // P):
                        ins = pe.transpose(bank[5 + u % 2][:, t * P:(t + 1) * P], src[:, t * P:(t + 1) * P], IDENT)
                    ins.then_inc(tr_done, 1)

                def values(u):
                    pe.wait_ge(pt_ready, u0 + u + 1)
                    if u0 + u >= 2:
                        pe.wait_ge(o_ready, u0 + u - 1)
                    unit = units[u]
                    for t, v in enumerate(unit["v"]):
                        ins = pe.matmul(OUTB[u % 2][unit["rows"], 0:P], v,
                                        PROBT[u % 2][:, t * P:(t + 1) * P], start=(t == 0), stop=(t == len(unit["v"]) - 1))
                    ins.then_inc(pv_done, 1)

                for u in range(AHEAD):
                    scores(u)
                for u in range(len(units)):
                    if u + AHEAD < len(units):
                        scores(u + AHEAD)
                    turn(u)
                    if u:
                        values(u - 1)
                values(len(units) - 1)
                n["sub"] += len(units) * spu
                n["unit"] += len(units)

            def chunk_ready(count=KC):
                n["h"] += count
                return [(h_ready, n["h"])]

            def of_h(w):
                return lambda kc, at: (HH[:, kc, 0:w], HL[:, kc, 0:w])

            def of_f(w):
                return lambda kc, at: (FH[:, kc, 0:w], FL[:, kc, 0:w])

            def stored():
                n["mod"] += 1
                pe.wait_ge(mod_stored, n["mod"])

            def layer_norm(w, name, rest):
                stat(lambda c: HS[:, 0, 0:w], 1, w, presum, 2)
                mod_rows(name, range(1))
                stat(lambda c: O[:, c, 0:w], KC, w, sq_ready, 3)
                mod_rows(name, rest)

            pe.wait_ge(silu_c, 1)
            pe.wait_ge(const_in, 16)
            mod_rows("1_0_0")
            mod_turn("1_0_0")
            for l in range(2):
                w = TOK if l == 0 else S
                if l == 0:
                    linear("ev_qk", of_h(TOK), chunk_ready())
                    linear("ev_v", None)
                    for j in range(5):
                        pe.wait_ge(hsq_ready, j + 1)
                        if j >= 2:
                            pe.wait_ge(hroot_ready, j - 1)
                        pe.matmul(bank[4 + j % 2][:, :], HEADS, QK[:, 8 + j, :], start=True, stop=True).then_inc(hsum_done, 1)
                        if j == 1:
                            stored()
                            mod_rows("1_0_1")
                    mod_rows("1_0_2")
                    for j in range(5):
                        rope(G[:, j, 0:S], (hnorm_done, j + 1))
                    mod_turn("1_0_1")
                    mod_turn("1_0_2")
                    stored()
                    stored()
                    pe.wait_ge(rope_done, n["rope"])
                    attend(ATT["global"])
                    pe.wait_ge(bias_ready, 1)
                    attend(ATT["near"])
                else:
                    linear("od_k", of_h(TOK), chunk_ready())
                    linear("od_v", None)
                    linear("od_q", of_h(S))
                    mod_turn("1_1_1")
                    stored()
                    mod_rows("1_1_2")
                    for j in range(9):
                        at = LIN["od_q"].empty0["scalar"]
                        rope(G[:, j, 0:S], (emptied["scalar"], at + max(j, 1)))
                    mod_turn("1_1_2")
                    stored()
                    pe.wait_ge(rope_done, n["rope"])
                    pe.wait_ge(emptied["scalar"], LIN["od_q"].empty0["scalar"] + 8)
                    attend(ATT["window"])
                linear(f"mix1_{l}", lambda kc, at: (OH[:, kc, 0:w], OH[:, 8 + kc, 0:w]), chunk_ready())
                name = ("1_1_0", "2_0_0")[l]
                layer_norm(w, name, range(1, 4))
                linear(f"up1_{l}", of_h(w), chunk_ready())
                mod_turn(name)
                n["hid"] += FC
                linear(f"down1_{l}", of_f(w), [(hid_ready, n["hid"])])
                stored()
                name = ("1_1_1", "2_0_1")[l]
                layer_norm(w, name, range(1, 4) if l == 0 else range(1, 3))
            for l in range(2):
                w = TOK if l == 0 else S
                name = ("2_0_1", "2_1_1")[l]
                stat(lambda c: QK[:, 8 + c, :], KC, TOK, sq_ready, 3)
                mod_rows(name, range(3, 4) if l == 0 else range(1, 4))
                linear(f"glu_{l}", of_h(w), chunk_ready())
                mod_turn(name)
                linear(f"p_{l}", of_h(w))
                linear(f"q_{l}", of_h(w))
                eq, ek = (LIN[f"{k}_{l}"].empty0["scalar"] for k in ("q", "k"))
                linear(f"k_{l}", of_h(TOK), extra=lambda g: rope(QK[:, g, 0:S], (emptied["scalar"], eq + g + 1)))
                linear(f"v_{l}", None, extra=lambda g: rope(QK[:, 8 + g, 0:S], (emptied["scalar"], ek + g + 1)))
                pe.wait_ge(rope_done, n["rope"])
                stat(lambda c: CV[:, c, 0:w], 4, w, conv_ready, 2)
                linear(f"gate_{l}_0", of_h(w))
                stat(lambda c: G[:, 12 + c, 0:w], 4, w, sq_ready, 3)
                linear(f"gate_{l}_1", of_h(w))
                n["pool"] += 4
                linear(f"group_{l}", lambda kc, at: PM[:, at.g, 0:w], [(pool_ready, n["pool"])])
                g4 = LIN[f"group_{l}"]
                stored()
                pe.wait_ge(root_ready, ROOTS + 13 * l + 2)
                pe.wait_ge(emptied["scalar"], g4.empty0["scalar"] + 4)
                attend(ATT[f"diff_{l}"])
                for h in range(8):
                    n["sub_sq"] += 1
                    pe.wait_ge(sub_sq, n["sub_sq"])
                    if h >= 2:
                        pe.wait_ge(root_ready, ROOTS + 13 * l + 2 + h - 1)
                    pe.matmul(bank[2 + h % 2][:, 0:w], ONES, QK[:, h, 0:w], start=True, stop=True).then_inc(stat_done, 1)
                    if h % 2:
                        mod_rows(f"2_{l}_2", range(h // 2, h // 2 + 1))
                mod_turn(f"2_{l}_2")

                def branch(kc, at):
                    if at.u % 3 == 2:
                        return OH[:, kc, 0:w], OH[:, 8 + kc, 0:w]
                    return (CV, PM)[at.u % 3][:, kc, 0:w]

                linear(f"merge_{l}", branch, chunk_ready() + [(silu_c, 1 + 4 * (l + 1)),
                                                              (emptied["scalar"], g4.empty0["scalar"] + 4)])
                stored()
                linear(f"out_{l}", of_h(w), chunk_ready())
                stat(lambda c: QK[:, 8, 0:w], 1, w, presum, 3)
                if l == 0:
                    mod_rows("2_1_0", range(1))
                stat(lambda c: QK[:, 8 + c, 0:w], KC, w, sq_ready, 3)
                if l == 0:
                    mod_rows("2_1_0", range(1, 4))
                linear(f"up2_{l}", of_h(w), chunk_ready())
                if l == 0:
                    mod_turn("2_1_0")
                n["hid"] += FC
                linear(f"down2_{l}", of_f(w), [(hid_ready, n["hid"])])
                stat(lambda c: O[:, 0, 0:w], 1, w, presum, 3)
                if l == 0:
                    stored()
                    mod_rows("2_1_1", range(1))

        @block.scalar
        def _(act):
            n = Tally()

            def ahead(what):
                if what is None or not what[0].L.halved_at(what[0].u):
                    return
                at, j = what
                act.wait_ge(*at.landed(j))
                cols = slice(at.slot(j), at.slot(j) + at.L.tiles_of(at.u, j) * P)
                nc.scalar.copy(wh[:, cols], raw[:, cols]).then_inc(high_ready, 1)

            def products(name, body):
                turns(act, LIN[name], body, ahead)

            def copies(name, dst):
                L = LIN[name]

                def one(at):
                    act.wait_ge(slab_done, at.full())
                    src = bank[at.u % 2][:, 0:L.n]
                    if L.kind == "tokens":
                        src = src.rearrange("p (t d) -> p t d", t=TT)
                    if name.startswith("p_"):
                        src = streams(src, L.n // S)
                    nc.scalar.copy(dst(at), src).then_inc(emptied["scalar"], 1)

                products(name, one)

            def mod_copy(name, groups=range(4)):
                L, (b, space) = LIN["mod" + name], MODS[name]
                for g in groups:
                    act.wait_ge(slab_done, At(L, g, g % L.step, None).full())
                    q = slice(32 * g, 32 * g + 2)
                    nc.scalar.copy(space[q, :], bank[b][q, :]).then_inc(rows_copied, 1)

            def gated(name, k, gate, ns):
                def one(at):
                    act.wait_ge(slab_done, at.full())
                    if not (isinstance(at.g, int) and at.g < 2):
                        act.wait_ge(row_ready, at.g + (n["row"] - 1))
                    for s in range(ns):
                        cols = slice(s * S, s * S + S)
                        ins = nc.scalar.activation(TMP[:, at.u % 2, cols], bank[at.u % 2][:, cols], ACT.Copy,
                                                   scale=MOD[:, k, bass.ds(at.g + gate, 1), s])
                    ins.then_inc(emptied["scalar"], 1)

                products(name, one)
                n["row"] += KC

            def squares(src, dst, count, ready, done=sq_ready):
                for c in range(count):
                    n[ready] += 1
                    act.wait_ge(ready, n[ready])
                    nc.scalar.activation(dst(c), src(c), ACT.Square).then_inc(done, 1)

            def root(b, w, scale, eps, slot=0):
                n["stat"] += 1
                act.wait_ge(stat_done, n["stat"])
                nc.scalar.activation(ROOT[slot][:, 0:w], bank[b][:, 0:w], ACT.Sqrt, scale=scale,
                                     bias=small[:, eps:eps + 1]).then_inc(root_ready, 1)

            def high(dst, src, count, w, ready=None):
                for c in range(count):
                    if ready is not None:
                        n[ready] += 1
                        act.wait_ge(ready, n[ready])
                    nc.scalar.copy(dst(c)[:, 0:w], src(c)[:, 0:w]).then_inc(hh_ready, 1)

            def high_shifted(k, shift, ns):
                for c in range(KC):
                    n["t"] += 1
                    act.wait_ge(t_ready, n["t"])
                    for s in range(ns):
                        cols = slice(s * S, s * S + S)
                        ins = nc.scalar.activation(HH[:, c, cols], O[:, c, cols], ACT.Identity,
                                                   bias=MOD[:, k, shift + c, s:s + 1])
                    ins.then_inc(hh_ready, 1)

            def layer_norm(ln, vl, w, name):
                n["stat"] += 1
                squares(lambda c: X[:, c, 0:w], lambda c: O[:, c, 0:w], KC, cent_ready)
                mod_copy(name, range(1))
                root(3, w, 1.0 / D, 0)
                for c in range(KC):
                    n["norm"] += 1
                    act.wait_ge(norm_ready, n["norm"])
                    nc.scalar.activation(X[:, c, 0:w], X[:, c, 0:w], ACT.Identity,
                                         scale=vcol(vl, V1["ln_g"] + 8 * ln + c),
                                         bias=vcol(vl, V1["ln_b"] + 8 * ln + c)).then_inc(x_ready, 1)

            def attend(units, vl):
                spu = len(units[0]["subs"])
                j0, u0 = n["sub"], n["unit"]

                def exps(u):
                    unit = units[u]
                    for i in range(spu):
                        j = u * spu + i
                        act.wait_ge(nm_ready, j0 + j + 1)
                        if j >= 6:
                            act.wait_ge(tr_done, u0 + (j - 6) // spu + 1)
                        m = smax[:, j % NS:j % NS + 1]
                        if unit["sink"] is not None:
                            nc.scalar.activation(ssink[:, j % NS:j % NS + 1], vcol(vl, V1["sink"] + unit["sink"]),
                                                 ACT.Exp, bias=m)
                        nc.scalar.activation(PROB[j % 6][:, 0:unit["T"]], SCORES[j % 4][:, 0:unit["T"]], ACT.Exp,
                                             bias=m, scale=SCALE,
                                             accum_out=ssum[:, j % NS:j % NS + 1]).then_inc(ex_ready, 1)

                def copy(u):
                    act.wait_ge(tr_done, u0 + u + 1)
                    if u0 + u >= 2:
                        act.wait_ge(pv_done, u0 + u - 1)
                    w = units[u]["T"]
                    nc.scalar.copy(PROBT[u % 2][:, 0:w], bank[5 + u % 2][:, 0:w]).then_inc(pt_ready, 1)

                for u in range(AHEAD):
                    exps(u)
                for u in range(len(units)):
                    if u + AHEAD < len(units):
                        exps(u + AHEAD)
                    copy(u)
                n["sub"] += len(units) * spu
                n["unit"] += len(units)

            act.wait_ge(cvec_in, 16)
            nc.scalar.activation(cvec[:, :], cvec[:, :], ACT.Silu).then_inc(silu_c, 1)
            mod_copy("1_0_0")
            act.wait_ge(vec_in, 32)
            act.wait_ge(small_ready, 3)
            for l in range(2):
                act.wait_ge(lam_ready, l + 1)
                nc.scalar.activation(small[:, 6 + 2 * l:8 + 2 * l], small[:, 2 + 2 * l:4 + 2 * l], ACT.Exp).then_inc(lam_exp, 1)
            for l in range(2):
                w, ns = (TOK, 2) if l == 0 else (S, 1)
                if l == 0:
                    high_shifted(0, 0, 2)
                    begin(LIN["ev_qk"], ahead)
                    copies("ev_qk", lambda at: G[:, at.g, :])
                    copies("ev_v", lambda at: VT[:, :, at.g * P:(at.g + 1) * P])
                    act.wait_ge(emptied["scalar"], LIN["ev_qk"].empty0["scalar"] + 13)
                    for j in range(5):
                        nc.scalar.activation(QK[:, 8 + j, :], G[:, j, :], ACT.Square).then_inc(hsq_ready, 1)
                    for j in range(5):
                        act.wait_ge(hsum_done, j + 1)
                        if j >= 2:
                            act.wait_ge(hnorm_done, j - 1)
                        nc.scalar.activation(ROOT[j % 2][:, :], bank[4 + j % 2][:, :], ACT.Sqrt, scale=1.0 / HD,
                                             bias=small[:, 1:2]).then_inc(hroot_ready, 1)
                        if j == 3:
                            mod_copy("1_0_1")
                    mod_copy("1_0_2")
                    attend(ATT["global"], l)
                    attend(ATT["near"], l)
                else:
                    begin(LIN["od_k"], ahead)
                    copies("od_k", lambda at: G[:, at.g, :])
                    copies("od_v", lambda at: VT[:, :, at.g * P:(at.g + 1) * P])
                    copies("od_q", lambda at: G[:, at.g + 1, 0:S])
                    mod_copy("1_1_2")
                    attend(ATT["window"], l)
                act.wait_ge(o_ready, n["unit"])
                high(lambda c: OH[:, c, :], lambda c: O[:, c, :], KC, w)
                begin(LIN[f"mix1_{l}"], ahead)
                gated(f"mix1_{l}", l, 16, ns)
                name = ("1_1_0", "2_0_0")[l]
                layer_norm(0, l, w, name)
                high_shifted(l, 24, ns)
                mod_copy(name, range(1, 4))
                L = LIN[f"up1_{l}"]
                begin(L, ahead)

                def silu_last(u, count):
                    act.wait_ge(emptied["vector"], count)
                    nc.scalar.activation(SC[:, u, 0:w], SC[:, u, 0:w], ACT.Silu).then_inc(sig_ready, 1)

                def high_last(f, u, count):
                    act.wait_ge(prod_ready, count)
                    nc.scalar.copy(FH[:, bass.ds(f - 1, 1), 0:w], SC[:, u:u + 1, 0:w]).then_inc(fh_ready, 1)

                def conv3(at):
                    f, first = at.over(2), isinstance(at.g, int) and at.g < 2
                    act.wait_ge(slab_done, at.full())
                    if not (isinstance(at.g, int) and at.g < 4):
                        act.wait_ge(hid_ready, f + (n["hid"] - 1))
                    nc.scalar.activation(SC[:, at.u, 0:w], bank[at.u % 2][:, 0:w], ACT.Identity,
                                         scale=vcol(l, at.g + (V1["conv_w"] + 2 * FC)),
                                         bias=vcol(l, at.g + V1["conv_b"])).then_inc(tap_ready, 1)
                    if first:
                        return
                    if at.u % 2 == 0:
                        silu_last((at.u + 3) % 4, at.g + at.L.empty0["vector"])
                    else:
                        high_last(f, (at.u + 1) % 4, f + n["hid"])

                products(f"up1_{l}", conv3)
                silu_last(3, L.empty0["vector"] + 2 * FC)
                high_last(FC, 2, n["hid"] + FC)
                n["hid"] += FC
                gated(f"down1_{l}", l, 40, ns)
                name = ("1_1_1", "2_0_1")[l]
                layer_norm(1, l, w, name)
                if l == 0:
                    high_shifted(1, 0, 2)
                    mod_copy(name, range(1, 4))
            for l in range(2):
                w, ns = (TOK, 2) if l == 0 else (S, 1)
                if l == 0:
                    act.wait_ge(ctx_in, 16)
                act.wait_ge(x_ready, X_READS + 16 * l)
                for c in range(KC):
                    nc.scalar.activation(QK[:, 8 + c, :], X[:, c, :], ACT.Square).then_inc(sq_ready, 1)
                name = ("2_0_1", "2_1_1")[l]
                mod_copy(name, range(1, 3) if l == 0 else range(1))
                root(3, TOK, 1.0 / D, 1)
                high_shifted(2 + l, 0, 2)
                mod_copy(name, range(3, 4) if l == 0 else range(1, 4))
                begin(LIN[f"glu_{l}"], ahead)

                def gate_half(at):
                    if at.u % 2 == 0:
                        act.wait_ge(slab_done, at.full())
                        if at.g >= 4:
                            act.wait_ge(*At(at.L, at.g - 3, (at.g - 3) % 4, None).emptied())
                        nc.scalar.activation(TMP[:, at.g // 2 % 2, 0:w], bank[0][:, 0:w],
                                             ACT.Sigmoid).then_inc(emptied["scalar"], 1)

                products(f"glu_{l}", gate_half)
                act.wait_ge(pad_ready, l + 1)
                copies(f"p_{l}", lambda at: PP[:, at.g, 0:ns, POOL_PAD:POOL_PAD + S])
                copies(f"q_{l}", lambda at: QK[:, at.g, 0:w])
                copies(f"k_{l}", lambda at: QK[:, at.g + 8, :])
                copies(f"v_{l}", lambda at: VT[:, :, at.g * P:(at.g + 1) * P])
                n["stat"] += 1
                squares(lambda c: CV[:, c, 0:w], lambda c: G[:, 12 + c, 0:w], 4, cent_ready)
                act.wait_ge(pool_ready, 4 * (l + 1))

                def gate(first):
                    def one(at):
                        act.wait_ge(slab_done, at.full())
                        nc.scalar.activation(G[:, at.g + first, 0:w], bank[at.u % 2][:, 0:w], ACT.Sigmoid,
                                             bias=vcol(l, at.g + (V2["b_gate"] + first))).then_inc(emptied["scalar"], 1)
                    return one

                products(f"gate_{l}_0", gate(0))
                root(3, w, 1.0 / 512, 1)
                for c in range(4):
                    n["norm"] += 1
                    act.wait_ge(norm_ready, n["norm"])
                    nc.scalar.activation(CV[:, c, 0:w], CV[:, c, 0:w], ACT.Silu, scale=vcol(l, V2["conv_ln_g"] + c),
                                         bias=vcol(l, V2["conv_ln_b"] + c)).then_inc(silu_c, 1)
                products(f"gate_{l}_1", gate(12))

                def scaled(at):
                    act.wait_ge(slab_done, at.full())
                    nc.scalar.activation(PM[:, at.g, 0:w], bank[at.u % 2][:, 0:w], ACT.Copy,
                                         scale=vcol(l, at.g + V2["pool_scale"])).then_inc(emptied["scalar"], 1)

                products(f"group_{l}", scaled)
                attend(ATT[f"diff_{l}"], l)
                act.wait_ge(o_ready, n["unit"])
                for h in range(8):
                    nc.scalar.activation(QK[:, h, 0:w], O[:, h, 0:w], ACT.Square).then_inc(sub_sq, 1)
                for h in range(8):
                    if h >= 2:
                        act.wait_ge(norm_ready, n["norm"] + h - 1)
                    root(2 + h % 2, w, 1.0 / P, 1, h % 2)
                    if h >= 2:
                        nc.scalar.copy(OH[:, h - 2, 0:w], O[:, h - 2, 0:w]).then_inc(hh_ready, 1)
                for h in range(6, 8):
                    act.wait_ge(norm_ready, n["norm"] + h + 1)
                    nc.scalar.copy(OH[:, h, 0:w], O[:, h, 0:w]).then_inc(hh_ready, 1)
                n["norm"] += 8
                mod_copy(f"2_{l}_2")
                begin(LIN[f"merge_{l}"], ahead)

                def merged(at):
                    if at.u % 3 == 2:
                        c = at.g // 3
                        act.wait_ge(merge_step, n["merge"] + 2 * c + 2)
                        nc.scalar.copy(HH[:, c, 0:w], G[:, c, 0:w]).then_inc(hh_ready, 1)

                products(f"merge_{l}", merged)
                n["merge"] += 16

                def plain(name, y, sq):
                    def one(at):
                        act.wait_ge(slab_done, at.full())
                        src = bank[at.u % 2][:, 0:w]
                        nc.scalar.copy(y[:, at.g, 0:w], src)
                        nc.scalar.activation(sq[:, at.g, 0:w], src, ACT.Square).then_inc(emptied["scalar"], 1)

                    products(name, one)
                    root(3, w, 1.0 / D, 1)

                plain(f"out_{l}", QK[:, 0:8, :], QK[:, 8:16, :])
                for c in range(KC):
                    act.wait_ge(x_ready, X_READS + 16 * l + c + 1)
                    nc.scalar.activation(QK[:, 8 + c, 0:w], X[:, c, 0:w], ACT.Square).then_inc(sq_ready, 1)
                if l == 0:
                    mod_copy("2_1_0", range(1))
                root(3, w, 1.0 / D, 1)
                high_shifted(2 + l, 24, ns)
                if l == 0:
                    mod_copy("2_1_0", range(1, 4))
                    begin(LIN[f"up2_{l}"], ahead)
                L = LIN[f"up2_{l}"]

                def high_hidden(f, u, count):
                    act.wait_ge(emptied["vector"], count)
                    nc.scalar.copy(FH[:, bass.ds(f - 1, 1), 0:w], SC[:, u:u + 1, 0:w]).then_inc(fh_ready, 1)

                def silu_half(at):
                    f = at.over(2)
                    if at.u % 2 == 0:
                        act.wait_ge(slab_done, at.full())
                        if not (isinstance(at.g, int) and at.g < 4):
                            act.wait_ge(hid_ready, f + (n["hid"] - 1))
                        nc.scalar.activation(SC[:, at.u, 0:w], bank[0][:, 0:w], ACT.Silu).then_inc(emptied["scalar"], 1)
                        if not (isinstance(at.g, int) and at.g < 2):
                            high_hidden(f, (at.u + 2) % 4, f + at.L.empty0["vector"])

                products(f"up2_{l}", silu_half)
                high_hidden(FC, 2, L.empty0["vector"] + FC)
                n["hid"] += FC
                plain(f"down2_{l}", HS, O)

        @block.vector
        def _(dve):
            v = nc.vector
            n = Tally()
            own = Own(dve, dve_own)

            def ahead(what):
                if what is None or not what[0].L.halved_at(what[0].u):
                    return
                at, j = what
                dve.wait_ge(high_ready, at.halved(j))
                cols = slice(at.slot(j), at.slot(j) + at.L.tiles_of(at.u, j) * P)
                v.tensor_tensor(wl[:, cols], raw[:, cols], wh[:, cols].bitcast(F32), ALU.subtract).then_inc(low_ready, 1)

            def products(name, body=None):
                turns(dve, LIN[name], body, ahead)

            def mod_store(name):
                b, _ = MODS[name]
                block, l, i = (int(x) for x in name.split("_"))
                k = 2 * (block - 1) + l
                V = (V1, V2)[block - 1]
                n["mod"] += 1
                dve.wait_ge(mod_turned, 4 * n["mod"])
                if block == 2 and i == 0:
                    dve.wait_ge(vec_in, 16 * (3 + l))
                rows = slice(16 * i, 16 * i + 16)
                for s in range(2):
                    src = bank[b][:, 0:32].rearrange("p (j s) -> p j s", s=2)[:, :, s]
                    ins = v.tensor_tensor(MOD[:, k, rows, s], src, vcol(l, V["mod_b"] + 16 * i, 16), ALU.add)
                ins.then_inc(mod_stored, 1)
                dve.wait_ge(mod_stored, n["mod"])
                MD = MDS[:, l]
                for kind, j, gain in ((0, 8, "g_pre_mix"), (2, 16, "g_post_mix"), (1, 32, "g_pre_ffn"), (3, 40, "g_post_ffn")):
                    if not rows.start <= j < rows.stop:
                        continue
                    for s in range(2):
                        src, dst = MOD[:, k, j:j + 8, s], MD[:, kind, :, s]
                        if block == 1:
                            if kind < 2:
                                own.inc(v.tensor_scalar(dst, src, 1.0, None, ALU.add))
                        elif kind < 2:
                            own.inc(v.scalar_tensor_tensor(dst, src, 1.0, vcol(l, V[gain], 8), ALU.add, ALU.mult))
                        else:
                            own.inc(v.tensor_tensor(dst, src, vcol(l, V[gain], 8), ALU.mult))
                own.wait(own.n)

            def low(dst, src, highs, count, w):
                for c in range(count):
                    n["hh"] += 1
                    dve.wait_ge(hh_ready, n["hh"])
                    v.tensor_tensor(dst(c)[:, 0:w], src(c)[:, 0:w], highs(c)[:, 0:w].bitcast(F32),
                                    ALU.subtract).then_inc(h_ready, 1)

            def modulate(l, k, kind, shift, ns, rooted):
                MD = MDS[:, l]

                def scaled(c):
                    for s in range(ns):
                        cols = slice(s * S, s * S + S)
                        t, x, m = O[:, c, cols], X[:, c, cols], MD[:, kind, c, s:s + 1]
                        if rooted:
                            ins = v.scalar_tensor_tensor(t, x, m, RS_[:, cols], ALU.mult, ALU.mult)
                        else:
                            ins = v.tensor_scalar(t, x, m, None, ALU.mult)
                    ins.then_inc(t_ready, 1)

                def low_half(c):
                    n["hh"] += 1
                    dve.wait_ge(hh_ready, n["hh"])
                    for s in range(ns):
                        cols = slice(s * S, s * S + S)
                        ins = v.scalar_tensor_tensor(HL[:, c, cols], O[:, c, cols], MOD[:, k, shift + c, s:s + 1],
                                                     HH[:, c, cols].bitcast(F32), ALU.add, ALU.subtract)
                    ins.then_inc(h_ready, 1)

                for c in range(KC):
                    scaled(c)
                    if c:
                        low_half(c - 1)
                low_half(KC - 1)

            def residual(name, w):
                def one(at):
                    dve.wait_ge(*at.emptied())
                    xs = X[:, at.g, 0:w]
                    v.scalar_tensor_tensor(xs, xs, ALPHA, TMP[:, at.u % 2, 0:w], ALU.mult, ALU.add).then_inc(row_ready, 1)

                products(name, one)
                n["row"] += KC
                dve.wait_ge(row_ready, n["row"])

            def centre(buf, chunks, w, scale):
                n["stat"] += 1
                dve.wait_ge(stat_done, n["stat"])
                for c in range(chunks):
                    v.scalar_tensor_tensor(buf[:, c, 0:w], bank[2][:, 0:w], -scale, buf[:, c, 0:w], ALU.mult,
                                           ALU.add).then_inc(cent_ready, 1)
                n["cent"] += chunks
                dve.wait_ge(cent_ready, n["cent"])

            def inverse(w, slot=0):
                n["root"] += 1
                n["stat"] += 1
                dve.wait_ge(root_ready, n["root"])
                own.link(v.reciprocal(ROOT[slot][:, 0:w], ROOT[slot][:, 0:w]))

            def normed(buf, chunks, w):
                for c in range(chunks):
                    v.tensor_tensor(buf[:, c, 0:w], buf[:, c, 0:w], RS_[:, 0:w], ALU.mult).then_inc(norm_ready, 1)
                n["norm"] += chunks

            def layer_norm(w):
                centre(X, KC, w, 1.0 / D)
                inverse(w)
                normed(X, KC, w)
                n["x"] += KC
                dve.wait_ge(x_ready, n["x"])

            def rope(chunk):
                n["rope"] += 1
                dve.wait_ge(rope_mm, n["rope"])
                t = TMP[:, n["rope"] % 2, 0:S]
                own.inc(v.tensor_tensor(t, bank[2 + n["rope"] % 2][:, 0:S], SIN, ALU.mult))
                own.link(v.tensor_tensor(chunk, chunk, COS, ALU.mult))
                v.tensor_tensor(chunk, chunk, t, ALU.add).then_inc(rope_done, 1)

            def attend(units, lam=None):
                spu = len(units[0]["subs"])
                j0, u0 = n["sub"], n["unit"]

                def maxima(u):
                    unit = units[u]
                    w = unit["T"]
                    for i in range(spu):
                        j = u * spu + i
                        dve.wait_ge(sc_done, j0 + j + 1)
                        sc = SCORES[j % 4]
                        if unit["mask"] is not None:
                            own.link(v.tensor_tensor(sc[:, 0:S], sc[:, 0:S], unit["mask"], ALU.add))
                        m = smax[:, j % NS:j % NS + 1]
                        own.link(v.reduce_max(m, sc[:, 0:w], AX_X))
                        if unit["sink"] is not None:
                            k = unit["sink"]
                            ins = v.tensor_scalar(m, m, -SCALE, nsink[:, k:k + 1], ALU.mult, ALU.min)
                        else:
                            ins = v.tensor_scalar(m, m, -SCALE, None, ALU.mult)
                        ins.then_inc(nm_ready, 1)

                def norm(u):
                    unit = units[u]
                    w = unit["T"]
                    j = u * spu
                    dve.wait_ge(ex_ready, j0 + j + spu)
                    cols = slice(j % NS, j % NS + spu)
                    if unit["sink"] is not None:
                        own.link(v.tensor_tensor(ssum[:, cols], ssum[:, cols], ssink[:, cols], ALU.add))
                    own.link(v.reciprocal(srec[:, cols], ssum[:, cols]))
                    p0, r0 = PROB[j % 6][:, 0:w], srec[:, j % NS:j % NS + 1]
                    if not unit["diff"]:
                        v.tensor_scalar(p0, p0, r0, None, ALU.mult).then_inc(pr_ready, 1)
                        return
                    p1, r1 = PROB[(j + 1) % 6][:, 0:w], srec[:, j % NS + 1:j % NS + 2]
                    own.inc(v.tensor_tensor(r1, r1, lam, ALU.mult))
                    own.link(v.tensor_scalar(p0, p0, r0, None, ALU.mult))
                    v.scalar_tensor_tensor(p1, p1, r1, p0, ALU.mult, ALU.add).then_inc(pr_ready, 1)

                def store(u):
                    dve.wait_ge(pv_done, u0 + u + 1)
                    v.tensor_copy(units[u]["out"], OUTB[u % 2][units[u]["rows"], 0:P]).then_inc(o_ready, 1)

                for u in range(AHEAD):
                    maxima(u)
                norm(0)
                for u in range(len(units)):
                    if u + AHEAD < len(units):
                        maxima(u + AHEAD)
                    if u + 1 < len(units):
                        norm(u + 1)
                    if u:
                        store(u - 1)
                store(len(units) - 1)
                n["sub"] += len(units) * spu
                n["unit"] += len(units)
                dve.wait_ge(o_ready, n["unit"])

            v.memset(small[:, 0:1], LN_EPS).then_inc(small_ready, 1)
            v.memset(small[:, 1:2], RMS_EPS).then_inc(small_ready, 1)
            dve.wait_ge(vec_in, 32)
            v.tensor_scalar(nsink[:, :], vcol(1, V1["sink"], 16), -1.0, None, ALU.mult).then_inc(small_ready, 1)
            dve.wait_ge(small_ready, 3)
            dve.wait_ge(lam_in, 16)
            for l in range(2):
                own.link(v.tensor_tensor(LAM[:, l, 0:2, :], LAM[:, l, 0:2, :], LAM[:, l, 2:4, :], ALU.mult))
                v.tensor_reduce(small[:, 2 + 2 * l:4 + 2 * l], LAM[:, l, 0:2, :], AX_X, ALU.add).then_inc(lam_ready, 1)
            for l in range(2):
                dve.wait_ge(lam_exp, l + 1)
                e = 6 + 2 * l
                own.link(v.tensor_tensor(small[:, 10 + l:11 + l], small[:, e + 1:e + 2], small[:, e:e + 1], ALU.subtract))
                own.link(v.tensor_scalar(small[:, 10 + l:11 + l], small[:, 10 + l:11 + l], -LAM_INIT[l], None, ALU.add))
            mod_store("1_0_0")
            for l in range(2):
                w, ns = (TOK, 2) if l == 0 else (S, 1)
                if l == 0:
                    dve.wait_ge(x_in, 16)
                    modulate(0, 0, 0, 0, 2, False)
                    begin(LIN["ev_qk"], ahead)
                    products("ev_qk")
                    products("ev_v")
                    for j in range(5):
                        gain = vcol(0, V1["q_gain"] if j < 4 else V1["k_gain"])
                        dve.wait_ge(hroot_ready, j + 1)
                        own.link(v.reciprocal(ROOT[j % 2][:, :], ROOT[j % 2][:, :]))
                        v.scalar_tensor_tensor(G[:, j, :], G[:, j, :], gain, ROOT[j % 2][:, :], ALU.mult,
                                               ALU.mult).then_inc(hnorm_done, 1)
                    dve.wait_ge(hnorm_done, 5)
                    dve.wait_ge(bias_in, 16 * (8 * 4))
                    dve.wait_ge(mask_in, 32)
                    for h in range(8):
                        ins = v.scalar_tensor_tensor(BIAS[:, h, :, :], BIAS[:, h, :, :], 1.0 / SCALE, MASKB, ALU.mult, ALU.add)
                    ins.then_inc(bias_ready, 1)
                    dve.wait_ge(bias_ready, 1)
                    for j in range(5):
                        rope(G[:, j, 0:S])
                    mod_store("1_0_1")
                    mod_store("1_0_2")
                    attend(ATT["global"])
                    attend(ATT["near"])
                else:
                    begin(LIN["od_k"], ahead)
                    products("od_k")
                    products("od_v")
                    products("od_q")
                    mod_store("1_1_1")
                    for j in range(9):
                        rope(G[:, j, 0:S])
                    mod_store("1_1_2")
                    attend(ATT["window"])
                low(lambda c: OH[:, 8 + c, :], lambda c: O[:, c, :], lambda c: OH[:, c, :], KC, w)
                begin(LIN[f"mix1_{l}"], ahead)
                residual(f"mix1_{l}", w)
                layer_norm(w)
                modulate(l, l, 1, 24, ns, False)
                L = LIN[f"up1_{l}"]
                begin(L, ahead)

                def product_last(u, count):
                    dve.wait_ge(sig_ready, count)
                    v.tensor_tensor(SC[:, u, 0:w], SC[:, u, 0:w], SC[:, u + 1, 0:w], ALU.mult).then_inc(prod_ready, 1)

                def low_last(f, u, count):
                    dve.wait_ge(fh_ready, count)
                    v.tensor_tensor(FL[:, bass.ds(f - 1, 1), 0:w], SC[:, u:u + 1, 0:w],
                                    FH[:, bass.ds(f - 1, 1), 0:w].bitcast(F32), ALU.subtract).then_inc(hid_ready, 1)

                def conv3(at):
                    f, first = at.over(2), isinstance(at.g, int) and at.g < 2
                    dve.wait_ge(tap_ready, at.g + (n["tap"] + 1))
                    y, u = streams(SC[:, at.u, 0:w], ns), streams(bank[at.u % 2][:, 0:w], ns)
                    v.scalar_tensor_tensor(y[:, :, 1:S], u[:, :, 0:S - 1], vcol(l, at.g + V1["conv_w"]),
                                           y[:, :, 1:S], ALU.mult, ALU.add).then_inc(tap_left, 1)
                    dve.wait_ge(tap_left, at.g + (n["tap"] + 1))
                    v.scalar_tensor_tensor(y[:, :, 0:S - 1], u[:, :, 1:S], vcol(l, at.g + (V1["conv_w"] + 4 * FC)),
                                           y[:, :, 0:S - 1], ALU.mult, ALU.add).then_inc(emptied["vector"], 1)
                    if first:
                        return
                    if at.u % 2 == 0:
                        product_last((at.u + 2) % 4, f + n["sig"])
                    else:
                        low_last(f, (at.u + 1) % 4, f + n["fh"])

                products(f"up1_{l}", conv3)
                product_last(2, n["sig"] + FC)
                low_last(FC, 2, n["fh"] + FC)
                n["tap"] += 2 * FC
                n["sig"] += FC
                n["fh"] += FC
                mod_store(("1_1_0", "2_0_0")[l])
                residual(f"down1_{l}", w)
                layer_norm(w)
                if l == 0:
                    modulate(1, 1, 0, 0, 2, False)
            for l in range(2):
                w, ns = (TOK, 2) if l == 0 else (S, 1)
                minus_lam = small[:, 10 + l:11 + l]
                own.link(v.tensor_scalar(small[:, 12:13], vcol(l, V2["subln_g"]), 1.0 - LAM_INIT[l], None, ALU.mult))
                if l == 0:
                    dve.wait_ge(ctx_in, 16)
                inverse(TOK)
                modulate(l, 2 + l, 0, 0, 2, True)
                begin(LIN[f"glu_{l}"], ahead)
                own.link(v.memset(BIG[:, 0:8 * UW], 0.0))

                def unit(at):
                    if at.u % 2:
                        i = at.g // 2
                        dve.wait_ge(slab_done, at.full())
                        dve.wait_ge(*At(at.L, at.g - 1, (at.g - 1) % 4, None).emptied())
                        v.tensor_tensor(U[:, i, 0:ns, CONV_PAD:CONV_PAD + S], streams(bank[1][:, 0:w], ns),
                                        streams(TMP[:, i % 2, 0:w], ns), ALU.mult).then_inc(emptied["vector"], 1)

                products(f"glu_{l}", unit)
                dve.wait_ge(emptied["vector"], LIN[f"glu_{l}"].empty0["vector"] + 4)
                mod_store(("2_0_1", "2_1_1")[l])

                def cvs(c):
                    return streams(CV[:, c, 0:w], ns)

                for c in range(4):
                    v.tensor_scalar(cvs(c), U[:, c, 0:ns, 0:S], vcol(l, V2["conv_w"] + c * CONV_TAPS),
                                    vcol(l, V2["conv_b"] + c), ALU.mult, ALU.add).then_inc(tap_done, 1)
                base = n["taps"]
                n["taps"] += 4 * (CONV_TAPS - 1)
                todo = list(enumerate(TAPS))

                def taps(count):
                    for i, (k, c) in todo[:count]:
                        dve.wait_ge(tap_done, base + i + 1)
                        ins = v.scalar_tensor_tensor(cvs(c), U[:, c, 0:ns, k:k + S], vcol(l, V2["conv_w"] + c * CONV_TAPS + k),
                                                     cvs(c), ALU.mult, ALU.add)
                        ins.then_inc(tap_done if k < CONV_TAPS - 1 else conv_ready, 1)
                    del todo[:count]

                products(f"p_{l}")
                products(f"q_{l}", lambda at: taps(TAP_SHARE[l]["q"]))

                def beside(share, first):
                    def one(at):
                        taps(TAP_SHARE[l][share])
                        rope(QK[:, first + at.g, 0:S])
                    return one

                products(f"k_{l}", beside("k", 0))
                products(f"v_{l}", beside("v", 8))
                assert not todo
                dve.wait_ge(conv_ready, 4 * (l + 1))
                centre(CV, 4, w, 1.0 / 512)
                products(f"gate_{l}_0")
                inverse(w)
                normed(CV, 4, w)
                products(f"gate_{l}_1")
                dve.wait_ge(rope_done, n["rope"])
                attend(ATT[f"diff_{l}"], minus_lam)
                for h in range(8):
                    inverse(w, h % 2)
                    v.scalar_tensor_tensor(O[:, h, 0:w], O[:, h, 0:w], small[:, 12:13], ROOT[h % 2][:, 0:w],
                                           ALU.mult, ALU.mult).then_inc(norm_ready, 1)
                    if h >= 3:
                        low(lambda c: OH[:, 8 + h - 3, :], lambda c: O[:, h - 3, :], lambda c: OH[:, h - 3, :], 1, w)
                for h in range(8, 11):
                    low(lambda c: OH[:, 8 + h - 3, :], lambda c: O[:, h - 3, :], lambda c: OH[:, h - 3, :], 1, w)
                n["norm"] += 8
                mod_store(f"2_{l}_2")
                begin(LIN[f"merge_{l}"], ahead)

                def low_merged(c):
                    low(lambda _: HL[:, c, :], lambda _: G[:, c, :], lambda _: HH[:, c, :], 1, w)

                def merge(at):
                    c, part = at.g // 3, at.g % 3
                    dve.wait_ge(slab_done, at.full())
                    m, t = G[:, c, 0:w], G[:, c + (0, 16, 8)[part], 0:w]
                    v.tensor_tensor(t, bank[at.u % 2][:, 0:w], t, ALU.mult).then_inc(emptied["vector"], 1)
                    if part == 0:
                        if c:
                            low_merged(c - 1)
                        return
                    dve.wait_ge(*at.emptied())
                    if part == 2:
                        dve.wait_ge(merge_step, c * 2 + (n["merge"] + 1))
                    v.tensor_tensor(m, m, t, ALU.add).then_inc(merge_step, 1)

                products(f"merge_{l}", merge)
                low_merged(7)
                n["merge"] += 16

                def post_norm(k, y):
                    inverse(w)
                    for c in range(KC):
                        own.inc(v.tensor_tensor(y[:, c, 0:w], y[:, c, 0:w], RS_[:, 0:w], ALU.mult))
                    for c in range(KC):
                        own.wait(own.n - KC + 1 + c)
                        for s in range(ns):
                            cols = slice(s * S, s * S + S)
                            ins = v.scalar_tensor_tensor(X[:, c, cols], y[:, c, cols], MDS[:, l, k, c, s:s + 1], X[:, c, cols],
                                                         ALU.mult, ALU.add)
                        ins.then_inc(x_ready, 1)
                    n["x"] += KC
                    dve.wait_ge(x_ready, n["x"])

                products(f"out_{l}")
                post_norm(2, QK)
                inverse(w)
                modulate(l, 2 + l, 1, 24, ns, True)
                L = LIN[f"up2_{l}"]
                if l == 0:
                    begin(L, ahead)

                def low_last(f, u, count):
                    dve.wait_ge(fh_ready, count)
                    v.tensor_tensor(FL[:, bass.ds(f - 1, 1), 0:w], SC[:, u:u + 1, 0:w],
                                    FH[:, bass.ds(f - 1, 1), 0:w].bitcast(F32), ALU.subtract).then_inc(hid_ready, 1)

                def hidden(at):
                    f = at.over(2)
                    if at.u % 2:
                        if not (isinstance(at.g, int) and at.g < 2):
                            low_last(f, (at.u + 1) % 4, f + n["fh"])
                        dve.wait_ge(slab_done, at.full())
                        dve.wait_ge(emptied["scalar"], f + (at.L.empty0["scalar"] + 1))
                        v.tensor_tensor(SC[:, at.u - 1, 0:w], bank[1][:, 0:w], SC[:, at.u - 1, 0:w],
                                        ALU.mult).then_inc(emptied["vector"], 1)

                products(f"up2_{l}", hidden)
                low_last(FC, 2, n["fh"] + FC)
                n["fh"] += FC
                if l == 0:
                    mod_store("2_1_0")
                products(f"down2_{l}")
                post_norm(3, HS)

        @block.gpsimd
        def _(pool):
            g = nc.gpsimd
            own = Own(pool, pool_step)
            pool.dma_start(con[:, :], T["consts"]).then_inc(const_in, 16)
            pool.dma_start(TMP_[:, 0:8 * HD], T["lam"]).then_inc(lam_in, 16)
            pool.dma_start(vec[:, 0:NV1], T["vecs1"][0]).then_inc(vec_in, 16)
            pool.dma_start(vec[:, NV:NV + NV1], T["vecs1"][1]).then_inc(vec_in, 16)
            pool.dma_start(X[:, :, :], T["x"]).then_inc(x_in, 16)
            pool.dma_start(MASKB, T["masks"][0]).then_inc(mask_in, 16)
            pool.dma_start(MASKC, T["masks"][1]).then_inc(mask_in, 16)
            rpb = T["rpb"]
            wide = rpb.shape[2] // GRID_W
            for h in range(8):
                for qt in range(2):
                    for r in range(2):
                        row = 2 * qt + r
                        src = bass.AP(rpb.tensor, (h * 15 + 7 - row) * GRID_W * wide + wide // 2,
                                      [[wide - 1, GRID_W], [GRID_W * wide, 4], [1, GRID_W]])
                        dst = BIAS[GRID_W * r:GRID_W * r + GRID_W, h, qt, :].rearrange("p (k c) -> p k c", k=4)
                        pool.dma_start(dst, src).then_inc(bias_in, 16)

            def sum_rows(l, first):
                w = TOK if l == 0 else S
                acc = HS[:, 0, 0:w]
                pool.wait_ge(row_ready, first + 2)
                own.link(g.tensor_tensor(acc, X[:, 0, 0:w], X[:, 1, 0:w], ALU.add))
                for c in range(2, KC):
                    pool.wait_ge(row_ready, first + c + 1)
                    ins = g.tensor_tensor(acc, acc, X[:, c, 0:w], ALU.add)
                    if c < KC - 1:
                        own.link(ins)
                ins.then_inc(presum, 1)

            def sum_squares(name, sq):
                L = LIN[name]
                acc = sq[:, 0, 0:L.n]
                for c in range(1, KC):
                    pool.wait_ge(emptied["scalar"], L.empty0["scalar"] + c + 1)
                    ins = g.tensor_tensor(acc, acc, sq[:, c, 0:L.n], ALU.add)
                    if c < KC - 1:
                        own.link(ins)
                ins.then_inc(presum, 1)

            for l in range(2):
                sum_rows(l, 16 * l)
                sum_rows(l, 16 * l + 8)
                pool.wait_ge(x_ready, 16 * (l + 1))
                pool.dma_start(vec[:, l * NV:l * NV + NV2], T["vecs2"][l]).then_inc(vec_in, 16)
                if l == 1:
                    pool.dma_start(X[:, :, S:TOK], T["ctx2"]).then_inc(ctx_in, 16)
            for l in range(2):
                ns = 2 - l
                pool.wait_ge(h_ready, 2 * 3 * KC + KC + 4 * KC * l)
                g.memset(PADS, 0.0).then_inc(pad_ready, 1)
                L = LIN[f"p_{l}"]
                for i in range(4):
                    pool.wait_ge(emptied["scalar"], L.empty0["scalar"] + i + 1)
                    src, width, last = PP[:, i, 0:ns, :], PW, 1
                    for d in range(i + 1):
                        dst = (PT0, PT1)[d % 2][:, 0:ns, :]
                        width -= last
                        own.link(g.tensor_tensor(dst[:, :, 0:width], src[:, :, 0:width], src[:, :, last:last + width], ALU.add))
                        src, last = dst, 2 * last
                    half = POOL_WINDOWS[i] // 2
                    win = src[:, :, POOL_PAD - half:POOL_PAD - half + S]
                    out = streams(PM[:, i, 0:ns * S], ns)
                    own.link(g.tensor_scalar(out, win, 1.0 / POOL_WINDOWS[i], None, ALU.mult))
                    for e in range(2):
                        cols = slice(0, POOL_PAD) if e == 0 else slice(S - POOL_PAD, S)
                        at = C_EDGE + (2 * i + e) * POOL_PAD
                        for s in range(ns):
                            own.inc(g.tensor_tensor(out[:, s, cols], out[:, s, cols], con[:, at:at + POOL_PAD], ALU.mult))
                    own.wait(own.n)
                    g.tensor_tensor(out, out, PP[:, i, 0:ns, POOL_PAD:POOL_PAD + S], ALU.subtract).then_inc(pool_ready, 1)
                sum_squares(f"out_{l}", QK[:, 8:16, :])
                sum_squares(f"down2_{l}", O)


def kernel(**inputs):
    import concourse.bacc as bacc
    from concourse.bass_utils import run_bass_kernel_spmd

    a = {k: np.asarray(v) for k, v in inputs.items()}

    def by_feature(x):
        return x.T.reshape(-1, P, x.shape[0]).transpose(1, 0, 2)

    def cols(x):
        return x.reshape(-1, P).T

    def pack(w, order=None):
        k, m = w.shape
        t = w.reshape(k // P, P, m // P, P).transpose(2, 1, 0, 3)
        if order is not None:
            t = t[order]
        return t.reshape(t.shape[0], P, k)

    def zip_groups(n):
        return [i + n * j for i in range(n) for j in range(2)]

    def paired(w, heads, axis):
        shape = w.shape
        t = w.reshape(shape[:axis] + (heads, HD) + shape[axis + 1:])
        order = [i + heads // 2 * j for i in range(heads // 2) for j in range(2)]
        return np.take(t, order, axis).reshape(shape)

    arrays = {}
    x = np.concatenate([by_feature(a["x"][0]), by_feature(a["ctx"][0])], 2)
    arrays["x"] = x
    arrays["ctx2"] = by_feature(a["ctx_2"][0])
    arrays["cvecs"] = np.concatenate([np.stack([cols(a["c" + s][0]), cols(a["c_ctx" + s])], 2).reshape(P, 16)
                                      for s in ("", "_2")], 1)
    ew, eo = a["ev_w_in"][0], a["ev_w_out"][0]
    ev = np.concatenate([paired(ew[:, 0:512], 8, 1), ew[:, 512:]], 1)
    arrays["w_ev_qk"] = pack(ev, [0, 1, 2, 3, 4, 6, 7, 8, 9, 10, 11, 12, 13])
    arrays["w_ev_v"] = pack(ev, [5, 14, 15, 16, 17])
    arrays["w_mix1_0"] = pack(np.concatenate([paired(eo[0:512], 8, 0), eo[512:]], 0))
    ow = a["od_w_in"][0]
    arrays["w_od_q"] = pack(paired(ow[:, 0:D], 16, 1))
    arrays["w_od_k"] = pack(ow[:, D:D + P])
    arrays["w_od_v"] = pack(ow[:, D + P:])
    arrays["w_mix1_1"] = pack(paired(a["od_w_out"][0], 16, 0))
    vecs1, vecs2 = [], []
    two = zip_groups(FC)
    for l in range(2):
        for b, w in ((1, a["ada_w"][l]), (2, a["w_mod_2"][l])):
            t = w.reshape(4, 2, P, 12, 512).transpose(3, 0, 2, 1, 4).reshape(12, 4, P, 2 * 512)
            for i in range(3):
                arrays[f"w_mod{b}_{l}_{i}"] = t[4 * i:4 * i + 4]
        arrays[f"w_up1_{l}"] = pack(a["ffn_w_up"][l], two)
        arrays[f"w_down1_{l}"] = pack(a["ffn_w_down"][l])
        wide = lambda v: np.broadcast_to(v, (P, v.shape[-1]))
        vecs1.append(np.concatenate(
            [cols(a["ada_b"][l]), cols(a["ln_g"][l]), cols(a["ln_b"][l])]
            + [cols(a["ffn_conv_w"][l, j])[:, two] for j in range(3)]
            + [cols(a["ffn_conv_b"][l])[:, two]]
            + [np.concatenate([a[k][0], a[k][0]])[:, None] for k in ("ev_q_gain", "ev_k_gain")]
            + [wide(a["od_sink"][0])], 1))
        w = a["w_in_2"][l]
        arrays[f"w_glu_{l}"] = pack(w[:, 0:1024], [i + 4 * j for i in range(4) for j in (1, 0)])
        for k, (lo, hi) in dict(q=(1024, 2048), k=(2048, 3072), v=(3072, 4096), p=(4096, 4608), gate=(4608, 7680)).items():
            arrays[f"w_{k}_{l}"] = pack(w[:, lo:hi])
        gates = arrays.pop(f"w_gate_{l}")
        arrays[f"w_gate_{l}_0"], arrays[f"w_gate_{l}_1"] = gates[:12], gates[12:]
        arrays[f"w_group_{l}"] = a["w_pool_group_2"][l]
        conv, att, pool = (pack(a[k][l]) for k in ("w_conv_out_2", "w_attn_out_2", "w_pool_out_2"))
        short = lambda t: np.concatenate([t, t], 2)
        arrays[f"w_merge_{l}"] = np.stack([short(conv), short(pool), att], 1).reshape(24, P, D)
        arrays[f"w_out_{l}"] = pack(a["w_out_2"][l])
        arrays[f"w_up2_{l}"] = pack(a["w_ffn_in_2"][l], two)
        arrays[f"w_down2_{l}"] = pack(a["w_ffn_out_2"][l])
        vecs2.append(np.concatenate(
            [cols(a["b_mod_2"][l])] + [cols(a[k + "_2"][l]) for k in ("g_pre_mix", "g_post_mix", "g_pre_ffn", "g_post_ffn")]
            + [cols(a["b_gate_2"][l]), a["conv_w_2"][l].T.reshape(4, P, CONV_TAPS).transpose(1, 0, 2).reshape(P, -1)]
            + [cols(a[k + "_2"][l]) for k in ("conv_b", "conv_ln_g", "conv_ln_b", "subln_g", "pool_scale")], 1))
    arrays["vecs1"], arrays["vecs2"] = np.stack(vecs1), np.stack(vecs2)
    arrays["lam"] = np.broadcast_to(
        np.concatenate([a[k + "_2"][l] for l in range(2) for k in ("lam_q1", "lam_q2", "lam_k1", "lam_k2")]), (P, 8 * HD))
    pad = GRID_W - 16
    arrays["rpb"] = np.tile(np.pad(a["ev_rpb"][0], ((0, 0), (0, 0), (pad, pad))), (1, 1, GRID_W))

    t = np.arange(S)
    half = HD // 2
    freq = (10000.0 ** (-np.arange(0, half, 2, dtype=np.float32) / np.float32(half))).astype(np.float32)
    by_row = (t // GRID_W).astype(np.float32)[:, None] * freq
    by_col = (t % GRID_W).astype(np.float32)[:, None] * freq
    ang = np.concatenate([by_row, by_row, by_col, by_col], 1).T
    rot = np.zeros((P, P), np.float32)
    for i in range(P):
        low = i % half < half // 2
        rot[i + half // 2 if low else i - half // 2, i] = -1.0 if low else 1.0
    head = np.kron(np.eye(2), np.ones((HD, HD)))
    edge = []
    for w in POOL_WINDOWS:
        count = np.clip(t + w // 2, 0, S) - np.clip(t - w // 2, 0, S)
        edge += [w / count[:POOL_PAD], w / count[-POOL_PAD:]]
    arrays["consts"] = np.concatenate(
        [np.tile(np.cos(ang), (2, 1)), np.tile(np.sin(ang), (2, 1)), np.ones((P, P)), np.eye(P), rot, head,
         np.broadcast_to(np.concatenate(edge), (P, 8 * POOL_PAD))], 1).astype(np.float32)
    col = t % GRID_W
    first = np.clip(col - 8, 0, GRID_W - 16)
    near = (col[None, :] >= first[:, None]) & (col[None, :] < first[:, None] + 16)
    window = np.abs(t[None, :] - t[:, None]) <= 128
    arrays["masks"] = np.stack([np.where(m, 0.0, NEG).astype(np.float32).reshape(2, P, S).transpose(1, 0, 2)
                                for m in (near, window)])

    nc = bacc.Bacc("TRN2", target_bir_lowering=False, num_devices=1)
    tensors, fed = {}, {}
    for k, v in arrays.items():
        v = np.ascontiguousarray(v)
        fed["in_" + k] = v
        tensors[k] = nc.dram_tensor("in_" + k, v.shape, F32, kind="ExternalInput").ap()
    tensors["out"] = nc.dram_tensor("out", (P, KC, S), F32, kind="ExternalOutput").ap()
    build(nc, tensors)
    r = run_bass_kernel_spmd(nc, [fed], core_ids=[0])
    y = r.results[0]["out"]
    return np.ascontiguousarray(y.transpose(2, 1, 0).reshape(1, S, D))
```

```python
from contextlib import ExitStack
import math

import numpy as np

import concourse.bass as bass
from concourse import mybir

F32 = mybir.dt.float32
F32R = mybir.dt.float32r
ALU = mybir.AluOpType
ACT = mybir.ActivationFunctionType
AX_X = mybir.AxisListType.X

P = 128
D = 1024
KC = D // P
S = 256
TOK = 2 * S
TT = TOK // P
HD = 64
FF = 2816
FC = FF // P
GRID_W = 64
ALPHA = 4.0 ** 0.25
LN_EPS = 1e-5
RMS_EPS = 1e-6
SCALE = HD ** -0.5
NEG = -1e30
CONV_TAPS = 31
CONV_PAD = CONV_TAPS // 2
POOL_PAD = 8
POOL_WINDOWS = (2, 4, 8, 16)
LAM_INIT = [0.8 - 0.6 * math.exp(-0.3 * l) for l in range(2)]

GATES = (8, 0, 16)
RING = 4
AHEAD_SLABS = 2
BUSY = {TOK: (5, 3, 16, 14), S: (3, 1, 8, 8)}
BEGIN = 3
SLAB = 8
DOWN = [6, 5, 6, 5]

def columns(spec):
    at, out = 0, {}
    for name, n in spec:
        out[name] = at
        at += n
    return out, at


V1, NV1 = columns([("mod_b", 48), ("ln_g", 16), ("ln_b", 16), ("conv_w", 3 * 2 * FC), ("conv_b", 2 * FC),
                   ("q_gain", 1), ("k_gain", 1), ("sink", 16)])
V2, NV2 = columns([("mod_b", 48), ("g_pre_mix", 8), ("g_post_mix", 8), ("g_pre_ffn", 8), ("g_post_ffn", 8),
                   ("b_gate", 24), ("conv_w", 4 * CONV_TAPS), ("conv_b", 4), ("conv_ln_g", 4), ("conv_ln_b", 4),
                   ("subln_g", 1), ("pool_scale", 4)])
NV = max(NV1, NV2)
C_COS, C_SIN, C_ONE, C_ID, C_ROT, C_HEAD, C_EDGE = 0, S, 2 * S, 2 * S + P, 2 * S + 2 * P, 2 * S + 3 * P, 2 * S + 4 * P
NCONST = C_EDGE + 4 * 2 * POOL_PAD


ROOTS, X_READS = 4, 4 * KC


class Linear:

    def __init__(self, name, groups, tiles, n, emptied, kind="features", halved=True):
        self.name, self.groups, self.tiles, self.n, self.kind, self.halved = name, groups, tiles, n, kind, halved
        self.emptied = emptied if isinstance(emptied, tuple) else (emptied, emptied)
        self.per = len(tiles)
        self.step = 8 if name.startswith("branch") else RING if self.per == 1 else 2

    def tiles_of(self, g, j):
        return self.tiles[j]

    def halved_at(self, g):
        return self.halved


def plan_linears():
    plan = []

    def modulation(b, l, *parts):
        plan.extend(Linear(f"mod{b}_{l}_{i}", 4, [8] * 4, 2, "vector", "rows", False) for i in parts)

    modulation(1, 0, 0)
    for l in range(2):
        n = TOK if l == 0 else S
        if l == 0:
            plan += [Linear("ev_qk", 13, [8], TOK, "scalar"), Linear("ev_v", 5, [8], TOK, "scalar")]
            modulation(1, 0, 1, 2)
            modulation(1, 1, 0, 1)
        else:
            plan += [Linear("od_k", 1, [8], TOK, "scalar"), Linear("od_v", 1, [8], TOK, "scalar"),
                     Linear("od_q", 8, [8], S, "scalar")]
            modulation(1, 1, 2)
            modulation(2, 0, 0)
        plan.append(Linear(f"mix1_{l}", 8, [8], n, "scalar"))
        plan += [Linear(f"up1_{l}", 2 * FC, [8], n, "vector"), Linear(f"down1_{l}", 8, DOWN, n, "scalar")]
        if l == 1:
            modulation(2, 0, 1)
    for l in range(2):
        n = TOK if l == 0 else S
        plan += [Linear(f"glu_{l}", 8, [8], n, ("scalar", "vector")), Linear(f"p_{l}", 4, [8], n, "scalar"),
                 Linear(f"q_{l}", 8, [8], n, "scalar"), Linear(f"k_{l}", 8, [8], TOK, "scalar"),
                 Linear(f"v_{l}", 8, [8], TOK, "scalar")]
        plan += [Linear(f"gate_{l}_{i}", 8, [8], n, "scalar") for i in range(3)]
        plan += [
                 Linear(f"group_{l}", 4, [1], n, "scalar", halved=False)]
        modulation(2, l, 2 - l)
        plan += [
                 Linear(f"branch_{l}", 16, [4], n, "vector", halved=False),
                 Linear(f"merge_{l}", 8, [8], n, "vector"), Linear(f"out_{l}", 8, [8], n, "scalar")]
        if l == 1:
            modulation(2, 1, 2)
        plan += [Linear(f"up2_{l}", 2 * FC, [8], n, ("scalar", "vector")),
                 Linear(f"down2_{l}", 8, DOWN, n, "scalar")]
        if l == 0:
            modulation(2, 1, 0)
    slab, emptied, last, half = 0, {"scalar": 0, "vector": 0}, {0: None, 1: None}, 0
    for i, L in enumerate(plan):
        L.next = plan[i + 1] if i + 1 < len(plan) else None
        L.slab0, L.half0 = slab, half
        L.empty0 = dict(emptied)
        L.before = dict(last)
        slab += L.groups * L.per
        half += sum(L.halved_at(g) for g in range(L.groups)) * L.per
        if L.kind == "rows":
            continue
        for g in range(L.groups):
            emptied[L.emptied[g % 2]] += 1
            last[g % 2] = (L.emptied[g % 2], emptied[L.emptied[g % 2]])
    return {L.name: L for L in plan}, plan


def build(nc, T):
    LIN, ORDER = plan_linears()
    ctx = ExitStack()
    with ctx:
        def sem(name):
            return ctx.enter_context(nc.semaphore(name))

        bank = [ctx.enter_context(nc.psum_tensor(f"bank{i}", [P, 512], F32)) for i in range(8)]
        where = [-(-nc.sbuf_base // 32) * 32]

        def region(words):
            at = where[0]
            where[0] += -(-4 * words // 32) * 32
            return at

        def view(name, at, words, dt=F32):
            return nc.alloc_sbuf_tensor_at(name, [P, words], dt, offset=at)

        def sb(name, words):
            return view(name, region(words), words)

        R_H, R_L = region(KC * TOK), region(KC * TOK)
        R_1, R_2, R_C = region(24 * TOK), region(24 * TOK), region(8 * TOK)
        R_W, R_WH = region(RING * SLAB * P), region(RING * SLAB * P)
        X_ = sb("x", KC * TOK)
        BIG = view("big", R_1, 24 * TOK)
        QK_ = view("qk", R_2, 16 * TOK)
        VT_ = view("v_tokens", R_2 + 4 * 16 * TOK, TT * D)
        HF = view("h_space", R_H, KC * TOK)
        LF = view("l_space", R_L, KC * TOK)
        SC_ = view("conv_space", R_C, 8 * TOK)
        TMP_ = sb("tmp", 2 * TOK)
        RS_ = sb("rstd", TOK)
        raw = view("ring", R_W, RING * SLAB * P)
        vec = sb("vec", 2 * NV)
        con = sb("con", NCONST)
        mod = sb("mod", 4 * 96)
        mods = sb("mod_derived", 2 * 4 * 16)
        cvec = sb("cvec", 32)
        small = sb("small", 16)
        nsink = sb("minus_sink", 16)
        NS = 32
        smax = sb("smax", NS)
        ssum = sb("ssum", NS)
        srec = sb("srec", NS)
        ssink = sb("ssink", NS)
        assert where[0] <= nc.sbuf_usable_end
        HH_, HL_ = view("h_high", R_H, KC * TOK, F32R), view("h_low", R_L, KC * TOK, F32R)
        FH_, FL_ = view("f_high", R_1, FC * TOK, F32R), view("f_low", R_2, FC * TOK, F32R)
        OHL = view("o_halves", R_2, 16 * TOK, F32R)
        wh, wl = view("w_high", R_WH, RING * SLAB * P, F32R), view("w_low", R_W, RING * SLAB * P, F32R)

        def chunks(t, c):
            return t[:, :].rearrange("p (c n) -> p c n", c=c)

        X, QK, G, SC = chunks(X_, KC), chunks(QK_, 16), chunks(BIG, 24), chunks(SC_, 8)
        HH, HL, FH, FL, OH = chunks(HH_, KC), chunks(HL_, KC), chunks(FH_, FC), chunks(FL_, FC), chunks(OHL, 16)
        HS, O = chunks(HF, KC), chunks(LF, KC)
        CV, PM = SC[:, 0:4, :], SC[:, 4:8, :]
        TMP = chunks(TMP_, 2)
        VALUES1, VALUES2 = [SC[:, i, :] for i in range(2)], [G[:, 22 + i, :] for i in range(2)]
        ROOT = [RS_[:, :], TMP_[:, 0:TOK]]
        VT = VT_[:, :].rearrange("p (t d) -> p t d", t=TT)
        MOD = mod[:, :].rearrange("p (k j s) -> p k j s", k=4, s=2)
        MDS = mods[:, :].rearrange("p (l k c s) -> p l k c s", l=2, k=4, s=2)
        UW = S + 2 * CONV_PAD
        U_ = BIG[:, 16 * TOK:16 * TOK + 4 * 2 * UW]
        U = U_.rearrange("p (c s n) -> p c s n", c=4, s=2)
        PW = S + 2 * POOL_PAD
        PADS = BIG[:, 0:12 * PW]
        PP = PADS[:, 0:8 * PW].rearrange("p (c s n) -> p c s n", c=4, s=2)
        PT0 = PADS[:, 8 * PW:10 * PW].rearrange("p (s n) -> p s n", s=2)
        PT1 = PADS[:, 10 * PW:12 * PW].rearrange("p (s n) -> p s n", s=2)
        LAM = TMP_[:, 0:8 * HD].rearrange("p (l j d) -> p l j d", l=2, j=4)
        BIAS = BIG[:, 13 * TOK:13 * TOK + 8 * 2 * S].rearrange("p (h q t) -> p h q t", h=8, q=2)
        MASKB = BIG[:, 22 * TOK:22 * TOK + 2 * S].rearrange("p (q t) -> p q t", q=2)
        MASKC = BIG[:, 23 * TOK:23 * TOK + 2 * S].rearrange("p (q t) -> p q t", q=2)
        COS, SIN = con[:, C_COS:C_COS + S], con[:, C_SIN:C_SIN + S]
        ONES, IDENT = con[:, C_ONE:C_ONE + P], con[:, C_ID:C_ID + P]
        ROT, HEADS = con[:, C_ROT:C_ROT + P], con[:, C_HEAD:C_HEAD + P]
        PROB = [HS[:, i, :] for i in range(6)]
        PROBT = [HS[:, 6 + i, :] for i in range(2)]
        SCORES = [bank[i] for i in (2, 3, 4, 0)]
        OUTB = [bank[7], bank[1]]

        def vcol(layer, at, n=1):
            return vec[:, bass.ds(at + NV * (layer % 2), n)]

        landed = [sem(f"slab_landed{i}") for i in range(RING)]
        slab_done = sem("slab_done")
        emptied = {"scalar": sem("banks_emptied_by_scalar"), "vector": sem("banks_emptied_by_vector")}
        pool_step = sem("pool_step")
        const_in, cvec_in, vec_in, mask_in, x_in, ctx_in = sem("const_in"), sem("cvec_in"), sem("vec_in"), sem("mask_in"), sem("x_in"), sem("ctx_in")
        bias_in, lam_in = sem("bias_in"), sem("lam_in")
        silu_c = sem("silu_c_ready")
        high_ready, low_ready = sem("weights_high_ready"), sem("weights_low_ready")
        t_ready, hh_ready = sem("values_to_halve"), sem("high_half_ready")
        half_ready = sem("scalar_streams_ready")
        h_ready = sem("both_halves_ready")
        rows_copied, mod_turned, mod_stored = sem("mod_rows_copied"), sem("mod_turned"), sem("mod_stored")
        row_ready = sem("residual_chunk_ready")
        cent_ready = sem("centred_chunk_ready")
        sq_ready = sem("square_chunk_ready")
        presum = sem("presum_ready")
        stat_done = sem("stat_done")
        root_ready = sem("root_ready")
        norm_ready = sem("normed_chunk_ready")
        x_ready = sem("x_chunk_ready")
        prod_ready, fh_ready = sem("hidden_product"), sem("hidden_high")
        rope_mm = sem("rope_product_done")
        rope_done = sem("rope_chunk_done")
        hsq_ready, hsum_done, hroot_ready, hnorm_done = sem("head_square"), sem("head_sum"), sem("head_root"), sem("head_norm")
        sc_done, nm_ready, ex_ready, pr_ready = sem("scores_done"), sem("max_ready"), sem("exp_ready"), sem("probs_ready")
        tr_done, pt_ready, pv_done, o_ready = sem("probs_turned"), sem("turned_copied"), sem("pv_done"), sem("o_ready")
        sig_ready, tap_ready = sem("sigmoid_ready"), sem("conv_centre_ready")
        hid_ready = sem("hidden_ready")
        conv_ready = sem("conv_ready")
        pad_ready, pool_ready = sem("pads_ready"), sem("pooled_ready")
        bias_ready = sem("bias_ready")
        lam_ready, lam_exp = sem("lam_ready"), sem("lam_exp")
        sub_sq = sem("subln_square")
        out_sem = sem("out_stored")

        dve_own = sem("dve_own")
        tap_left = sem("conv_left_tap_done")
        tap_done = sem("filter_tap_done")
        value_turned, value_copied = sem("values_turned"), sem("values_copied")
        merge_step = sem("merge_sum_done")
        small_ready = sem("small_ready")

        class Own:

            def __init__(self, eng, s):
                self.eng, self.s, self.n = eng, s, 0

            def inc(self, ins):
                ins.then_inc(self.s, 1)
                self.n += 1
                return self.n

            def wait(self, n):
                self.eng.wait_ge(self.s, n)

            def link(self, ins):
                self.wait(self.inc(ins))

        class Tally(dict):

            def __missing__(self, k):
                return 0

        class At:

            def __init__(self, L, g, u, turn):
                self.L, self.g, self.u, self.turn = L, g, u, turn

            def over(self, k):
                return self.g // k if self.turn is None else self.turn * (self.L.step // k) + self.u // k

            def full(self):
                return self.g * self.L.per + (self.L.per + self.L.slab0)

            def emptied(self, back=0):
                L, who = self.L, self.L.emptied[self.u % 2]
                if L.emptied[0] == L.emptied[1]:
                    return emptied[who], self.g + (L.empty0[who] + 1 - back)
                return emptied[who], self.over(2) + (L.empty0[who] + 1 - back // 2)

            def slot(self, j):
                return (self.L.slab0 + self.u * self.L.per + j) % RING * SLAB * P

            def landed(self, j):
                L = self.L
                n = L.slab0 + (self.g if self.turn is None else self.u) * L.per + j
                use = n // RING + 1
                if self.turn is not None:
                    use = self.turn * (L.step * L.per // RING) + use
                s = landed[(L.slab0 + self.u * L.per + j) % RING]
                return s, use * 16

            def halved(self, j):
                L = self.L
                return self.g * L.per + (L.half0 + j + 1)

            def later(self, k):
                L = self.L
                j = k % L.per
                if self.turn is not None:
                    u = self.u + k // L.per
                    return At(L, self.turn * L.step + u, u, self.turn), j
                g = self.g + k // L.per
                if g < L.groups:
                    return At(L, g, g % L.step, None), j
                if L.next is None or L.next.kind == "rows":
                    return None
                k -= (L.groups - self.g) * L.per
                N = L.next
                return At(N, k // N.per, k // N.per, None), k % N.per

        def turns(eng, L, body, ahead=None):
            def group(at):
                if ahead is not None:
                    for j in range(L.per):
                        ahead(at.later(j + AHEAD_SLABS))
                if body is not None:
                    body(at)

            whole = L.groups // L.step
            whole = whole if whole > 3 else 0
            for g in range(L.step if whole else L.groups):
                group(At(L, g, g % L.step, None))
            if whole:
                with eng.Fori(1, whole - 1) as turn:
                    for u in range(L.step):
                        group(At(L, turn * L.step + u, u, turn))
                for g in range((whole - 1) * L.step, L.groups):
                    group(At(L, g, g % L.step, None))

        def begin(L, ahead):
            for k in range(AHEAD_SLABS):
                ahead((At(L, k // L.per, k // L.per, None), k % L.per))

        def streams(ap, ns):
            return ap.rearrange("p (s n) -> p s n", s=ns)

        def units_pair(qchunk, kchunk, chunk0, vcols, tiles, mask, sink, shared):
            out = []
            for c in range(8 if sink else 4):
                for half in range(2):
                    rows = slice(HD * half, HD * half + HD)
                    for qt in tiles:
                        keys = slice(0, TOK) if qt < 2 else slice(S, TOK)
                        k0 = keys.start // P
                        m = None if qt >= 2 or mask is None else mask(2 * c + half, qt)
                        q = G[rows, qchunk + c, qt * P:(qt + 1) * P]
                        k = G[rows, kchunk + (0 if shared else c), keys]
                        v0 = vcols + (0 if shared else c * P) + HD * half
                        out.append(dict(
                            subs=[(q, k)], T=keys.stop - keys.start, mask=m, diff=False,
                            sink=(c + 8 * half) if sink else None,
                            v=[VT[:, k0 + t, v0:v0 + HD] for t in range((keys.stop - keys.start) // P)],
                            rows=rows, out=O[rows, chunk0 + c, qt * P:(qt + 1) * P]))
            return out

        def units_diff(tiles):
            out = []
            for h in range(8):
                for qt in tiles:
                    keys = slice(0, TOK) if qt < 2 else slice(S, TOK)
                    k0 = keys.start // P
                    subs = [(QK[HD * i:HD * i + HD, h, qt * P:(qt + 1) * P], QK[HD * i:HD * i + HD, 8 + h, keys])
                            for i in range(2)]
                    out.append(dict(subs=subs, T=keys.stop - keys.start, mask=None, diff=True, sink=None,
                                    v=[VT[:, k0 + t, h * P:(h + 1) * P] for t in range((keys.stop - keys.start) // P)],
                                    rows=slice(0, P), out=O[:, h, qt * P:(qt + 1) * P]))
            return out

        ATT = {
            "global": units_pair(0, 4, 0, 0, range(4), None, False, True),
            "near": units_pair(5, 9, 4, P, range(4), lambda h, qt: BIAS[:, h, qt, :], False, False),
            "window": units_pair(1, 0, 0, 0, range(2), lambda h, qt: MASKC[:, qt, :], True, True),
            "diff_0": units_diff(range(4)),
            "diff_1": units_diff(range(2)),
        }
        AHEAD = 2


        MODS = {"2_0_2": (1, TMP[:, 1, :]), "2_1_1": (1, TMP[:, 1, :])}
        for name in ("1_0_1", "1_1_0", "1_1_2"):
            MODS[name] = (0, SC[:, 7, :])
        for name in ("1_0_2", "1_1_1", "2_0_0"):
            MODS[name] = (0, SC[:, 6, :])
        for name in ("1_0_0", "2_0_1", "2_1_0", "2_1_2"):
            MODS[name] = (6, SC[:, 7, :])
        BESIDE = {"global": ("1_0_1", "1_0_2"), "near": ("1_1_0", "1_1_1"), "window": ("1_1_2", "2_0_0"),
                  "diff_0": ("2_0_2",), "diff_1": ("2_1_1",)}

        def columns_bank(name):
            return bank[6 if MODS[name][0] == 1 else MODS[name][0]]

        CHUNKS = {"global": (8, 0), "near": (8, 4), "window": (4, 0), "diff_0": (4, 0), "diff_1": (2, 0)}

        def chunk_over(name, u):
            per, first = CHUNKS[name]
            return first + u // per - 1 if u >= 0 and u % per == 0 and first + u // per else None

        TAPS = [(k, c) for k in range(1, CONV_TAPS) for c in range(4)]
        TAP_SHARE = [{"q": 4, "k": 3, "v": 3, "gate": 5}, {"q": 3, "k": 6, "v": 5, "gate": 1}]
        for l in range(2):
            assert 8 * sum(TAP_SHARE[l].values()) >= len(TAPS)

        block = ctx.enter_context(nc.Block())

        @block.sync
        def _(sp):
            sp.dma_start(cvec[:, :], T["cvecs"]).then_inc(cvec_in, 16)
            for L in ORDER:
                w = T["w_" + L.name]

                def load(at):
                    for j in range(L.per):
                        n = at.g * L.per + (L.slab0 + j)
                        if not (isinstance(n, int) and n < RING):
                            sp.wait_ge(slab_done, n - (RING - 1))
                        words = L.tiles_of(at.u, j) * P
                        if L.kind == "rows":
                            src = w[at.g, j]
                        elif L.per == 1:
                            src = w[at.g]
                        else:
                            first = sum(L.tiles[:j]) * P
                            src = w[at.g, :, first:first + words]
                        sp.dma_start(raw[:, at.slot(j):at.slot(j) + words], src[:, 0:words]).then_inc(at.landed(j)[0], 16)

                turns(sp, L, load)
            sp.wait_ge(x_ready, X_READS + 32)
            sp.dma_start(T["out"], X[:, :, 0:S]).then_inc(out_sem, 16)
            sp.wait_ge(out_sem, 16)

        @block.tensor
        def _(pe):
            n = Tally()

            def linear(name, rhs, waits=(), extra=None, arriving=None):
                L = LIN[name]
                for s, v in waits:
                    pe.wait_ge(s, v)

                def free(at):
                    if isinstance(at.g, int) and at.g < 2:
                        if L.before[at.u % 2] is not None:
                            who, count = L.before[at.u % 2]
                            pe.wait_ge(emptied[who], count)
                    else:
                        pe.wait_ge(*at.emptied(back=2))

                def slab(at, j):
                    if L.halved_at(at.u):
                        pe.wait_ge(low_ready, at.halved(j))
                    else:
                        pe.wait_ge(*at.landed(j))

                def tile(at, j, i, kc):
                    out = bank[at.u % 2][:, 0:L.n]
                    tiles = L.tiles_of(at.u, j)
                    cols = slice(at.slot(j) + i * P, at.slot(j) + (i + 1) * P)
                    first, last = kc == 0, j == L.per - 1 and i == tiles - 1
                    if L.halved_at(at.u):
                        high, low = rhs(kc, at)
                        pe.matmul(out, wh[:, cols], high, start=first, stop=False)
                        pe.matmul(out, wh[:, cols], low, start=False, stop=False)
                        ins = pe.matmul(out, wl[:, cols], high, start=False, stop=last)
                    else:
                        ins = pe.matmul(out, raw[:, cols], rhs(kc, at), start=first, stop=last)
                    if i == tiles - 1:
                        ins.then_inc(slab_done, 1)

                def arrived(kc):
                    pe.wait_ge(arriving[0], arriving[1] + kc + 1)

                def group(at):
                    opening = arriving is not None and isinstance(at.g, int) and at.g < 2
                    if opening and L.per == 1 and L.groups > 1:
                        if at.g == 1:
                            return
                        pair = [At(L, g, g, None) for g in range(2)]
                        for one in pair:
                            free(one)
                            slab(one, 0)
                        for kc in range(KC):
                            arrived(kc)
                            for one in pair:
                                tile(one, 0, kc, kc)
                        return
                    free(at)
                    kc = 0
                    for j in range(L.per):
                        slab(at, j)
                        for i in range(L.tiles_of(at.u, j)):
                            if opening and at.g == 0:
                                arrived(kc)
                            tile(at, j, i, kc)
                            kc += 1
                    if extra is not None:
                        extra(at.g)

                turns(pe, L, group)

            def mod_slab(name, k):
                L, (b, _) = LIN["mod" + name], MODS[name]
                g, j = divmod(k, L.per)
                at = At(L, g, g % L.step, None)
                pe.wait_ge(*at.landed(j))
                for i in range(2):
                    kc = 2 * j + i
                    vec0 = 16 * (int(name[0]) - 1) + 2 * kc
                    ins = pe.matmul(bank[b][32 * g:32 * g + 2, :], cvec[:, vec0:vec0 + 2],
                                    raw[:, at.slot(j) + 512 * i:at.slot(j) + 512 * (i + 1)],
                                    start=(kc == 0), stop=(kc == KC - 1))
                ins.then_inc(slab_done, 1)

            def mod_rows(name, groups=range(4)):
                for k in range(4 * groups.start, 4 * groups.stop):
                    mod_slab(name, k)

            def mod_turn(name):
                b, space = MODS[name]
                n["rows"] += 4
                pe.wait_ge(rows_copied, n["rows"])
                for g in range(4):
                    q = slice(32 * g, 32 * g + 2)
                    if g:
                        pe.wait_ge(mod_turned, n["rows"] - 4 + g)
                    for i in range(4):
                        col = (4 * g + i) * 2
                        ins = pe.transpose(columns_bank(name)[:, col:col + 2], space[q, i * P:(i + 1) * P], IDENT[q, q])
                    ins.then_inc(mod_turned, 1)

            def stat(src, chunks, width, ready, b):
                for c in range(chunks):
                    n[ready] += 1
                    pe.wait_ge(ready, n[ready])
                    ins = pe.matmul(bank[b][:, 0:width], ONES, src(c), start=(c == 0), stop=(c == chunks - 1))
                ins.then_inc(stat_done, 1)

            def rope(chunk, after):
                n["rope"] += 1
                pe.wait_ge(*after)
                if n["rope"] > 2:
                    pe.wait_ge(rope_done, n["rope"] - 2)
                pe.matmul(bank[2 + n["rope"] % 2][:, 0:S], ROT, chunk, start=True, stop=True).then_inc(rope_mm, 1)

            def value_turn(src, last):
                n["value"] += 1
                j = n["value"]
                pe.wait_ge(emptied["scalar"], last)
                if j > 2:
                    pe.wait_ge(value_copied, j - 2)
                for t in range(TT):
                    ins = pe.transpose(bank[4 + j % 2][:, t * P:(t + 1) * P], src[:, t * P:(t + 1) * P], IDENT)
                ins.then_inc(value_turned, 1)

            def values_by_token(name, spaces, beside=None):
                at = LIN[name].empty0["scalar"]

                def extra(g):
                    if g:
                        value_turn(spaces[(g - 1) % 2], at + g)
                    if beside is not None:
                        beside(g)

                linear(name, of_h(TOK), extra=extra)
                value_turn(spaces[(LIN[name].groups - 1) % 2], at + LIN[name].groups)

            def attend(name):
                units, beside = ATT[name], BESIDE[name]
                outs = OUTB[0:1] if units[0]["diff"] else OUTB
                pace = len(units) // (16 * len(beside))
                spu = len(units[0]["subs"])
                j0, u0 = n["sub"], n["unit"]
                score_banks = 2 + spu

                def scores(u):
                    for i, (q, k) in enumerate(units[u]["subs"]):
                        j = u * spu + i
                        if j >= score_banks:
                            pe.wait_ge(ex_ready, j0 + j - score_banks + 1)
                        pe.matmul(SCORES[j % score_banks][:, 0:units[u]["T"]], q, k, start=True, stop=True).then_inc(sc_done, 1)

                def turn(u):
                    pe.wait_ge(pr_ready, u0 + u + 1)
                    if u >= 2:
                        pe.wait_ge(pt_ready, u0 + u - 1)
                    src = PROB[(u * spu + spu - 1) % 6]
                    for t in range(units[u]["T"] // P):
                        ins = pe.transpose(bank[5 + u % 2][:, t * P:(t + 1) * P], src[:, t * P:(t + 1) * P], IDENT)
                    ins.then_inc(tr_done, 1)

                def values(u):
                    pe.wait_ge(pt_ready, u0 + u + 1)
                    if u0 + u >= 2:
                        pe.wait_ge(o_ready, u0 + u + 1 - len(outs))
                    unit = units[u]
                    for t, v in enumerate(unit["v"]):
                        ins = pe.matmul(outs[u % len(outs)][unit["rows"], 0:P], v,
                                        PROBT[u % 2][:, t * P:(t + 1) * P], start=(t == 0), stop=(t == len(unit["v"]) - 1))
                    ins.then_inc(pv_done, 1)

                for u in range(AHEAD):
                    scores(u)
                for u in range(len(units)):
                    if u + AHEAD < len(units):
                        scores(u + AHEAD)
                    if u % pace == 0:
                        k = u // pace
                        if k >= 16 and k % 4 == 0:
                            pe.wait_ge(rows_copied, n["rows"] + (k - 16) // 4 + 1)
                        mod_slab(beside[k // 16], k % 16)
                    turn(u)
                    if u:
                        values(u - 1)
                values(len(units) - 1)
                if len(beside) == 2:
                    pe.wait_ge(rows_copied, n["rows"] + 8)
                    for part in beside:
                        mod_turn(part)
                        stored()
                n["sub"] += len(units) * spu
                n["unit"] += len(units)

            def coming():
                n["h"] += KC
                return h_ready, n["h"] - KC

            def of_h(w):
                return lambda kc, at: (HH[:, kc, 0:w], HL[:, kc, 0:w])

            def of_f(w):
                return lambda kc, at: (FH[:, kc, 0:w], FL[:, kc, 0:w])

            def stored():
                n["mod"] += 1
                pe.wait_ge(mod_stored, n["mod"])

            def keep_busy(count):
                for _ in range(count):
                    pe.matmul(bank[4][:, 0:S], ONES, COS, start=True, stop=True)

            def layer_norm(w, name=None):
                for k in range(3 if name else 0):
                    mod_slab(name, k)
                if not name:
                    keep_busy(BUSY[w][0])
                stat(lambda c: HS[:, 0, 0:w], 1, w, presum, 2)
                if name:
                    mod_slab(name, 3)
                else:
                    keep_busy(BUSY[w][1])
                stat(lambda c: O[:, c, 0:w], KC, w, sq_ready, 3)
                if not name:
                    keep_busy(BUSY[w][2])

            pe.wait_ge(silu_c, 1)
            pe.wait_ge(const_in, 16)
            mod_rows("1_0_0")
            mod_turn("1_0_0")
            for l in range(2):
                w = TOK if l == 0 else S
                if l == 0:
                    linear("ev_qk", of_h(TOK), arriving=coming())

                    def head_norm(g):
                        pe.wait_ge(hsq_ready, g + 1)
                        if g >= 2:
                            pe.wait_ge(hroot_ready, g - 1)
                        pe.matmul(bank[6 + g % 2][:, :], HEADS, QK[:, 8 + g, :], start=True, stop=True).then_inc(hsum_done, 1)
                        if g:
                            rope(G[:, g - 1, 0:S], (hnorm_done, g))

                    values_by_token("ev_v", VALUES1, head_norm)
                    rope(G[:, 4, 0:S], (hnorm_done, 5))
                    pe.wait_ge(value_copied, n["value"])
                    pe.wait_ge(rope_done, n["rope"])
                    stored()
                    attend("global")
                    pe.wait_ge(bias_ready, 8)
                    attend("near")
                else:
                    linear("od_k", of_h(TOK), arriving=coming())
                    values_by_token("od_v", VALUES1)
                    linear("od_q", of_h(S))
                    for j in range(9):
                        at = LIN["od_q"].empty0["scalar"]
                        rope(G[:, j, 0:S], (emptied["scalar"], at + max(j, 1)))
                    pe.wait_ge(rope_done, n["rope"])
                    pe.wait_ge(emptied["scalar"], LIN["od_q"].empty0["scalar"] + 8)
                    attend("window")
                linear(f"mix1_{l}", lambda kc, at: (OH[:, kc, 0:w], OH[:, 8 + kc, 0:w]), arriving=coming())
                layer_norm(w)
                linear(f"up1_{l}", of_h(w), arriving=coming())
                linear(f"down1_{l}", of_f(w), arriving=(hid_ready, n["hid"]))
                n["hid"] += FC
                if l == 0:
                    layer_norm(w)
                else:
                    layer_norm(w, "2_0_1")
            for l in range(2):
                w = TOK if l == 0 else S
                stat(lambda c: QK[:, 8 + c, :], KC, TOK, sq_ready, 3)
                if l == 0:
                    mod_rows("2_0_1", range(1, 4))
                else:
                    mod_rows("2_1_0", range(3, 4))
                    mod_turn("2_1_0")
                    stored()
                linear(f"glu_{l}", of_h(w), arriving=coming())
                if l == 0:
                    mod_turn("2_0_1")
                linear(f"p_{l}", of_h(w))
                linear(f"q_{l}", of_h(w))
                eq, ek = (LIN[f"{k}_{l}"].empty0["scalar"] for k in ("q", "k"))
                linear(f"k_{l}", of_h(TOK), extra=lambda g: rope(QK[:, g, 0:S], (emptied["scalar"], eq + g + 1)))
                values_by_token(f"v_{l}", VALUES2,
                                lambda g: rope(QK[:, 8 + g, 0:S], (emptied["scalar"], ek + g + 1)))
                linear(f"gate_{l}_0", of_h(w))
                pe.wait_ge(rope_done, n["rope"])
                stat(lambda c: CV[:, c, 0:w], 4, w, conv_ready, 2)
                linear(f"gate_{l}_1", of_h(w))
                stat(lambda c: G[:, 20 + c, 0:w], 4, w, sq_ready, 3)
                linear(f"gate_{l}_2", of_h(w))
                n["pool"] += 4
                linear(f"group_{l}", lambda kc, at: PM[:, at.g, 0:w], [(pool_ready, n["pool"])])
                g4 = LIN[f"group_{l}"]
                if l == 0:
                    stored()
                pe.wait_ge(root_ready, ROOTS + 13 * l + 2)
                pe.wait_ge(emptied["scalar"], g4.empty0["scalar"] + 4)
                attend(f"diff_{l}")

                def head_sum(h):
                    pe.wait_ge(sub_sq, 8 * l + h + 1)
                    if h >= 2:
                        pe.wait_ge(root_ready, ROOTS + 13 * l + 2 + h - 1)
                    pe.matmul(bank[2 + h % 2][:, 0:w], ONES, QK[:, h, 0:w], start=True, stop=True).then_inc(stat_done, 1)

                head_sum(0)
                pe.wait_ge(o_ready, n["unit"])
                pe.wait_ge(rows_copied, n["rows"] + 4)
                linear(f"branch_{l}", lambda kc, at: (CV, PM)[at.g % 2][:, kc, 0:w],
                       [(silu_c, 1 + 4 * (l + 1)), (emptied["scalar"], g4.empty0["scalar"] + 4)],
                       extra=lambda g: head_sum((g + 1) // 2) if g % 2 and g < 15 else None)
                mod_turn(BESIDE[f"diff_{l}"][0])
                stored()
                linear(f"merge_{l}", lambda kc, at: (OH[:, kc, 0:w], OH[:, 8 + kc, 0:w]), arriving=coming())
                linear(f"out_{l}", of_h(w), arriving=coming())
                if l == 1:
                    for k in range(3):
                        mod_slab("2_1_2", k)
                if l == 0:
                    keep_busy(BUSY[w][0])
                stat(lambda c: QK[:, 8, 0:w], 1, w, presum, 3)
                if l == 1:
                    for k in range(3, 12):
                        mod_slab("2_1_2", k)
                else:
                    keep_busy(BUSY[w][3])
                stat(lambda c: QK[:, 8 + c, 0:w], KC, w, sq_ready, 3)
                if l == 0:
                    keep_busy(BUSY[w][2])
                if l == 1:
                    mod_rows("2_1_2", range(3, 4))
                    mod_turn("2_1_2")
                linear(f"up2_{l}", of_h(w), arriving=coming())
                if l == 1:
                    stored()
                linear(f"down2_{l}", of_f(w), arriving=(hid_ready, n["hid"]))
                n["hid"] += FC
                if l == 0:
                    for k in range(3):
                        mod_slab("2_1_0", k)
                stat(lambda c: O[:, 0, 0:w], 1, w, presum, 3)
                if l == 0:
                    for k in range(3, 12):
                        mod_slab("2_1_0", k)

        @block.scalar
        def _(act):
            n = Tally()

            def ahead(what):
                if what is None or not what[0].L.halved_at(what[0].u):
                    return
                at, j = what
                act.wait_ge(*at.landed(j))
                cols = slice(at.slot(j), at.slot(j) + at.L.tiles_of(at.u, j) * P)
                nc.scalar.copy(wh[:, cols], raw[:, cols]).then_inc(high_ready, 1)

            def products(name, body):
                turns(act, LIN[name], body, ahead)

            def copies(name, dst, scale=lambda g: False, after=None):
                L = LIN[name]

                def one(at):
                    act.wait_ge(slab_done, at.full())
                    src = bank[at.u % 2][:, 0:L.n]
                    if name.startswith("p_"):
                        src = streams(src, L.n // S)
                    if scale(at.g):
                        ins = nc.scalar.activation(dst(at), src, ACT.Copy, scale=SCALE)
                    else:
                        ins = nc.scalar.copy(dst(at), src)
                    ins.then_inc(emptied["scalar"], 1)
                    if after is not None:
                        after(at.g)

                products(name, one)

            def values_by_token(name, spaces, beside=None):
                L = LIN[name]

                def turned(c):
                    n["value"] += 1
                    act.wait_ge(value_turned, n["value"])
                    src = bank[4 + n["value"] % 2][:, :].rearrange("p (t d) -> p t d", t=TT)
                    nc.scalar.copy(VT[:, :, c * P:(c + 1) * P], src).then_inc(value_copied, 1)

                def one(at):
                    act.wait_ge(slab_done, at.full())
                    nc.scalar.copy(spaces[at.g % 2], bank[at.u % 2][:, :]).then_inc(emptied["scalar"], 1)
                    if beside is not None:
                        beside(at.g)
                    if at.g:
                        turned(at.g - 1)

                products(name, one)
                turned(L.groups - 1)

            def mod_copy(name, groups=range(4)):
                L, (b, space) = LIN["mod" + name], MODS[name]
                for g in groups:
                    act.wait_ge(slab_done, At(L, g, g % L.step, None).full())
                    q = slice(32 * g, 32 * g + 2)
                    nc.scalar.copy(space[q, :], bank[b][q, :]).then_inc(rows_copied, 1)

            def gated(name, k, gate, ns):
                def one(at):
                    act.wait_ge(slab_done, at.full())
                    if not (isinstance(at.g, int) and at.g < 2):
                        act.wait_ge(row_ready, at.g + (n["row"] - 1))
                    for s in range(ns):
                        cols = slice(s * S, s * S + S)
                        ins = nc.scalar.activation(TMP[:, at.u % 2, cols], bank[at.u % 2][:, cols], ACT.Copy,
                                                   scale=MOD[:, k, bass.ds(at.g + gate, 1), s])
                    ins.then_inc(emptied["scalar"], 1)

                products(name, one)
                n["row"] += KC

            def squares(src, dst, count, ready, done=sq_ready):
                for c in range(count):
                    n[ready] += 1
                    act.wait_ge(ready, n[ready])
                    nc.scalar.activation(dst(c), src(c), ACT.Square).then_inc(done, 1)

            def root(b, w, scale, eps, slot=0):
                n["stat"] += 1
                act.wait_ge(stat_done, n["stat"])
                nc.scalar.activation(ROOT[slot][:, 0:w], bank[b][:, 0:w], ACT.Sqrt, scale=scale,
                                     bias=small[:, eps:eps + 1]).then_inc(root_ready, 1)

            def high_out(c):
                w = TOK if n["layer"] == 0 else S
                nc.scalar.copy(OH[:, c, 0:w], O[:, c, 0:w]).then_inc(hh_ready, 1)

            def modulate(l, k, kind, shift, ns, rooted, L=None, before=None):
                mine = range(ns) if rooted else range(ns - 1)
                for step in range(KC + 2):
                    if before is not None and step < KC:
                        before(step)
                    c = step - 1
                    if 0 <= c < KC and len(mine):
                        if rooted:
                            n["t"] += 1
                            act.wait_ge(t_ready, n["t"])
                        elif before is not None:
                            act.wait_ge(x_ready, n["x"] + c + 1)
                        else:
                            act.wait_ge(t_ready, 1)
                        for s in mine:
                            cols = slice(s * S, s * S + S)
                            src = O[:, c, cols] if rooted else X[:, c, cols]
                            ins = nc.scalar.activation(O[:, c, cols], src, ACT.Identity, scale=MDS[:, l, kind, c, s:s + 1],
                                                       bias=MOD[:, k, shift + c, s:s + 1])
                        ins.then_inc(half_ready, 1)
                    c = step - 2
                    if c >= 0:
                        if len(mine):
                            n["half"] += 1
                            act.wait_ge(half_ready, n["half"])
                        if not rooted:
                            n["t"] += 1
                            act.wait_ge(t_ready, n["t"])
                        nc.scalar.copy(HH[:, c, 0:ns * S], O[:, c, 0:ns * S]).then_inc(hh_ready, 1)
                    if step == BEGIN and L is not None:
                        begin(L, ahead)

            def layer_norm(ln, vl, w, name, modulation=None):
                n["stat"] += 1
                squares(lambda c: X[:, c, 0:w], lambda c: O[:, c, 0:w], KC, cent_ready)
                if name is not None:
                    mod_copy(name, range(1))
                root(3, w, 1.0 / D, 0)

                def gains(c):
                    n["norm"] += 1
                    act.wait_ge(norm_ready, n["norm"])
                    nc.scalar.activation(X[:, c, 0:w], X[:, c, 0:w], ACT.Identity,
                                         scale=vcol(vl, V1["ln_g"] + 8 * ln + c),
                                         bias=vcol(vl, V1["ln_b"] + 8 * ln + c)).then_inc(x_ready, 1)

                if modulation is None:
                    act.wait_ge(ctx_in, 16)
                    for c in range(KC + 1):
                        if c < KC:
                            gains(c)
                        if c:
                            act.wait_ge(x_ready, n["x"] + c)
                            nc.scalar.activation(QK[:, 7 + c, :], X[:, c - 1, :], ACT.Square).then_inc(sq_ready, 1)
                else:
                    modulate(*modulation, before=gains)
                n["x"] += KC

            def attend(name, finish, vl=0):
                units, beside = ATT[name], BESIDE[name]
                pace = len(units) // (16 * len(beside))
                spu = len(units[0]["subs"])
                j0, u0 = n["sub"], n["unit"]
                score_banks = 2 + spu

                def exps(u):
                    unit = units[u]
                    for i in range(spu):
                        j = u * spu + i
                        act.wait_ge(nm_ready, j0 + j + 1)
                        if j >= 6:
                            act.wait_ge(tr_done, u0 + (j - 6) // spu + 1)
                        m = smax[:, j % NS:j % NS + 1]
                        if unit["sink"] is not None:
                            nc.scalar.activation(ssink[:, j % NS:j % NS + 1], vcol(vl, V1["sink"] + unit["sink"]),
                                                 ACT.Exp, bias=m)
                        nc.scalar.activation(PROB[j % 6][:, 0:unit["T"]], SCORES[j % score_banks][:, 0:unit["T"]], ACT.Exp,
                                             bias=m,
                                             accum_out=ssum[:, j % NS:j % NS + 1]).then_inc(ex_ready, 1)

                def copy(u):
                    act.wait_ge(tr_done, u0 + u + 1)
                    if u0 + u >= 2:
                        act.wait_ge(pv_done, u0 + u - 1)
                    w = units[u]["T"]
                    nc.scalar.copy(PROBT[u % 2][:, 0:w], bank[5 + u % 2][:, 0:w]).then_inc(pt_ready, 1)

                for u in range(AHEAD):
                    exps(u)
                for u in range(len(units)):
                    if u + AHEAD < len(units):
                        exps(u + AHEAD)
                    copy(u)
                    c = chunk_over(name, u - 2)
                    if c is not None:
                        act.wait_ge(o_ready, u0 + u - 2)
                        finish(c)
                    g, rest = divmod(u - 1, 4 * pace)
                    if g > 0 and rest == 0:
                        mod_copy(beside[(g - 1) // 4], range((g - 1) % 4, (g - 1) % 4 + 1))
                mod_copy(beside[-1], range(3, 4))
                n["sub"] += len(units) * spu
                n["unit"] += len(units)

            act.wait_ge(cvec_in, 16)
            nc.scalar.activation(cvec[:, :], cvec[:, :], ACT.Silu).then_inc(silu_c, 1)
            mod_copy("1_0_0")
            act.wait_ge(vec_in, 32)
            act.wait_ge(small_ready, 3)
            for l in range(2):
                act.wait_ge(lam_ready, l + 1)
                nc.scalar.activation(small[:, 6 + 2 * l:8 + 2 * l], small[:, 2 + 2 * l:4 + 2 * l], ACT.Exp).then_inc(lam_exp, 1)
            for l in range(2):
                w, ns = (TOK, 2) if l == 0 else (S, 1)
                n["layer"] = l
                if l == 0:
                    act.wait_ge(x_in, 16)
                    modulate(0, 0, 0, 0, 2, False, LIN["ev_qk"])

                    def square(g):
                        if g >= 8:
                            nc.scalar.activation(QK[:, g, :], G[:, g - 8, :], ACT.Square).then_inc(hsq_ready, 1)

                    def head_root(g):
                        act.wait_ge(hsum_done, g + 1)
                        if g:
                            act.wait_ge(hnorm_done, g)
                        nc.scalar.activation(RS_[:, :], bank[6 + g % 2][:, :], ACT.Sqrt, scale=1.0 / HD,
                                             bias=small[:, 1:2]).then_inc(hroot_ready, 1)

                    copies("ev_qk", lambda at: G[:, at.g, :], lambda g: 5 <= g < 9, after=square)
                    values_by_token("ev_v", VALUES1, head_root)
                    attend("global", high_out)
                    attend("near", high_out)
                else:
                    copies("od_k", lambda at: G[:, at.g, :])
                    values_by_token("od_v", VALUES1)
                    copies("od_q", lambda at: G[:, at.g + 1, 0:S], lambda g: True)
                    attend("window", high_out, l)
                begin(LIN[f"mix1_{l}"], ahead)
                act.wait_ge(o_ready, n["unit"])
                high_out(KC - 1)
                gated(f"mix1_{l}", l, 16, ns)
                L = LIN[f"up1_{l}"]
                layer_norm(0, l, w, None, (l, l, 1, 24, ns, False))

                def silu_last(u, count):
                    act.wait_ge(emptied["vector"], count)
                    nc.scalar.activation(SC[:, u, 0:w], SC[:, u, 0:w], ACT.Silu).then_inc(sig_ready, 1)

                def high_last(f, u, count):
                    act.wait_ge(prod_ready, count)
                    nc.scalar.copy(FH[:, bass.ds(f - 1, 1), 0:w], SC[:, u:u + 1, 0:w]).then_inc(fh_ready, 1)

                def conv3(at):
                    f, first = at.over(2), isinstance(at.g, int) and at.g < 2
                    act.wait_ge(slab_done, at.full())
                    if not (isinstance(at.g, int) and at.g < 4):
                        act.wait_ge(hid_ready, f + (n["hid"] - 1))
                    nc.scalar.activation(SC[:, at.u, 0:w], bank[at.u % 2][:, 0:w], ACT.Identity,
                                         scale=vcol(l, at.g + (V1["conv_w"] + 2 * FC)),
                                         bias=vcol(l, at.g + V1["conv_b"])).then_inc(tap_ready, 1)
                    if first:
                        return
                    if at.u % 2 == 0:
                        silu_last((at.u + 3) % 4, at.g + at.L.empty0["vector"])
                    else:
                        high_last(f, (at.u + 1) % 4, f + n["hid"])

                products(f"up1_{l}", conv3)
                silu_last(3, L.empty0["vector"] + 2 * FC)
                high_last(FC, 2, n["hid"] + FC)
                n["hid"] += FC
                gated(f"down1_{l}", l, 40, ns)
                if l == 0:
                    layer_norm(1, l, w, None, (1, 1, 0, 0, 2, False))
                else:
                    layer_norm(1, l, w, "2_0_1")
            for l in range(2):
                w, ns = (TOK, 2) if l == 0 else (S, 1)
                if l == 1:
                    act.wait_ge(x_ready, X_READS + 16 * l)
                    for c in range(KC):
                        nc.scalar.activation(QK[:, 8 + c, :], X[:, c, :], ACT.Square).then_inc(sq_ready, 1)
                root(3, TOK, 1.0 / D, 1)
                if l == 1:
                    mod_copy("2_1_0", range(3, 4))
                modulate(l, 2 + l, 0, 0, 2, True, LIN[f"glu_{l}"])
                if l == 0:
                    mod_copy("2_0_1", range(1, 4))

                def gate_half(at):
                    if at.u % 2 == 0:
                        act.wait_ge(slab_done, at.full())
                        if at.g >= 4:
                            act.wait_ge(*At(at.L, at.g - 3, (at.g - 3) % 4, None).emptied())
                        nc.scalar.activation(TMP[:, at.g // 2 % 2, 0:w], bank[0][:, 0:w],
                                             ACT.Sigmoid).then_inc(emptied["scalar"], 1)

                products(f"glu_{l}", gate_half)
                act.wait_ge(pad_ready, l + 1)
                copies(f"p_{l}", lambda at: PP[:, at.g, 0:ns, POOL_PAD:POOL_PAD + S])
                copies(f"q_{l}", lambda at: QK[:, at.g, 0:w], lambda g: True)
                copies(f"k_{l}", lambda at: QK[:, at.g + 8, :])
                values_by_token(f"v_{l}", VALUES2)

                def gate(first):
                    def one(at):
                        act.wait_ge(slab_done, at.full())
                        nc.scalar.activation(G[:, at.g + first, 0:w], bank[at.u % 2][:, 0:w], ACT.Sigmoid,
                                             bias=vcol(l, at.g + (V2["b_gate"] + first))).then_inc(emptied["scalar"], 1)
                    return one

                products(f"gate_{l}_0", gate(GATES[0]))
                n["stat"] += 1
                squares(lambda c: CV[:, c, 0:w], lambda c: G[:, 20 + c, 0:w], 4, cent_ready)
                act.wait_ge(pool_ready, 4 * (l + 1))
                products(f"gate_{l}_1", gate(GATES[1]))
                root(3, w, 1.0 / 512, 1)
                for c in range(4):
                    n["norm"] += 1
                    act.wait_ge(norm_ready, n["norm"])
                    nc.scalar.activation(CV[:, c, 0:w], CV[:, c, 0:w], ACT.Silu, scale=vcol(l, V2["conv_ln_g"] + c),
                                         bias=vcol(l, V2["conv_ln_b"] + c)).then_inc(silu_c, 1)
                products(f"gate_{l}_2", gate(GATES[2]))

                def scaled(at):
                    act.wait_ge(slab_done, at.full())
                    nc.scalar.activation(PM[:, at.g, 0:w], bank[at.u % 2][:, 0:w], ACT.Copy,
                                         scale=vcol(l, at.g + V2["pool_scale"])).then_inc(emptied["scalar"], 1)

                products(f"group_{l}", scaled)

                def square_out(h):
                    nc.scalar.activation(QK[:, h, 0:w], O[:, h, 0:w], ACT.Square).then_inc(sub_sq, 1)

                attend(f"diff_{l}", square_out)
                act.wait_ge(o_ready, n["unit"])
                for h in range(7 - l, 8):
                    square_out(h)
                for h in range(8):
                    root(2 + h % 2, w, 1.0 / P, 1)
                    n["norm"] += 1
                    act.wait_ge(norm_ready, n["norm"])
                    nc.scalar.copy(OH[:, h, 0:w], O[:, h, 0:w]).then_inc(hh_ready, 1)
                begin(LIN[f"merge_{l}"], ahead)

                def merged(at):
                    act.wait_ge(merge_step, n["merge"] + 8 + at.g + 1)
                    nc.scalar.copy(HH[:, at.g, 0:w], G[:, at.g, 0:w]).then_inc(hh_ready, 1)

                products(f"merge_{l}", merged)
                n["merge"] += 16

                def plain(name, y, sq):
                    def one(at):
                        act.wait_ge(slab_done, at.full())
                        src = bank[at.u % 2][:, 0:w]
                        nc.scalar.copy(y[:, at.g, 0:w], src)
                        nc.scalar.activation(sq[:, at.g, 0:w], src, ACT.Square).then_inc(emptied["scalar"], 1)

                    products(name, one)
                    root(3, w, 1.0 / D, 1)

                plain(f"out_{l}", QK[:, 0:8, :], QK[:, 8:16, :])
                for c in range(KC):
                    act.wait_ge(x_ready, X_READS + 16 * l + c + 1)
                    nc.scalar.activation(QK[:, 8 + c, 0:w], X[:, c, 0:w], ACT.Square).then_inc(sq_ready, 1)
                L = LIN[f"up2_{l}"]
                if l == 1:
                    mod_copy("2_1_2", range(3))
                root(3, w, 1.0 / D, 1)
                if l == 1:
                    mod_copy("2_1_2", range(3, 4))
                modulate(l, 2 + l, 1, 24, ns, True, L if l == 1 else None)

                def high_hidden(f, u, count):
                    act.wait_ge(emptied["vector"], count)
                    nc.scalar.copy(FH[:, bass.ds(f - 1, 1), 0:w], SC[:, u:u + 1, 0:w]).then_inc(fh_ready, 1)

                def silu_half(at):
                    f = at.over(2)
                    if at.u % 2 == 0:
                        act.wait_ge(slab_done, at.full())
                        if not (isinstance(at.g, int) and at.g < 4):
                            act.wait_ge(hid_ready, f + (n["hid"] - 1))
                        nc.scalar.activation(SC[:, at.u, 0:w], bank[0][:, 0:w], ACT.Silu).then_inc(emptied["scalar"], 1)
                        if not (isinstance(at.g, int) and at.g < 2):
                            high_hidden(f, (at.u + 2) % 4, f + at.L.empty0["vector"])

                products(f"up2_{l}", silu_half)
                high_hidden(FC, 2, L.empty0["vector"] + FC)
                n["hid"] += FC
                plain(f"down2_{l}", HS, O)
                if l == 0:
                    mod_copy("2_1_0", range(3))

        @block.vector
        def _(dve):
            v = nc.vector
            n = Tally()
            own = Own(dve, dve_own)

            def ahead(what):
                if what is None or not what[0].L.halved_at(what[0].u):
                    return
                at, j = what
                dve.wait_ge(high_ready, at.halved(j))
                cols = slice(at.slot(j), at.slot(j) + at.L.tiles_of(at.u, j) * P)
                v.tensor_tensor(wl[:, cols], raw[:, cols], wh[:, cols].bitcast(F32), ALU.subtract).then_inc(low_ready, 1)

            def products(name, body=None):
                turns(dve, LIN[name], body, ahead)

            def mod_store(name):
                b, _ = MODS[name]
                block, l, i = (int(x) for x in name.split("_"))
                k = 2 * (block - 1) + l
                V = (V1, V2)[block - 1]
                n["mod"] += 1
                dve.wait_ge(mod_turned, 4 * n["mod"])
                if block == 2 and i == 0:
                    dve.wait_ge(vec_in, 16 * (3 + l))
                rows = slice(16 * i, 16 * i + 16)
                for s in range(2):
                    src = columns_bank(name)[:, 0:32].rearrange("p (j s) -> p j s", s=2)[:, :, s]
                    ins = v.tensor_tensor(MOD[:, k, rows, s], src, vcol(l, V["mod_b"] + 16 * i, 16), ALU.add)
                ins.then_inc(mod_stored, 1)
                dve.wait_ge(mod_stored, n["mod"])
                MD = MDS[:, l]
                for kind, j, gain in ((0, 8, "g_pre_mix"), (2, 16, "g_post_mix"), (1, 32, "g_pre_ffn"), (3, 40, "g_post_ffn")):
                    if not rows.start <= j < rows.stop:
                        continue
                    for s in range(2):
                        src, dst = MOD[:, k, j:j + 8, s], MD[:, kind, :, s]
                        if block == 1:
                            if kind < 2:
                                own.inc(v.tensor_scalar(dst, src, 1.0, None, ALU.add))
                        elif kind < 2:
                            own.inc(v.scalar_tensor_tensor(dst, src, 1.0, vcol(l, V[gain], 8), ALU.add, ALU.mult))
                        else:
                            own.inc(v.tensor_tensor(dst, src, vcol(l, V[gain], 8), ALU.mult))
                own.wait(own.n)

            def low(dst, src, highs, count, w):
                for c in range(count):
                    n["hh"] += 1
                    dve.wait_ge(hh_ready, n["hh"])
                    v.tensor_tensor(dst(c)[:, 0:w], src(c)[:, 0:w], highs(c)[:, 0:w].bitcast(F32),
                                    ALU.subtract).then_inc(h_ready, 1)

            def modulate(l, k, kind, shift, ns, rooted, L=None, before=None):
                lag = 2 if before is not None else 0
                w = ns * S
                for step in range(KC + lag + 2):
                    if before is not None and step < KC:
                        before(step)
                    c = step - lag
                    if 0 <= c < KC:
                        if rooted:
                            ins = v.tensor_tensor(O[:, c, 0:w], X[:, c, 0:w], RS_[:, 0:w], ALU.mult)
                        else:
                            if before is not None:
                                dve.wait_ge(x_ready, n["x"] + c + 1)
                            cols = slice((ns - 1) * S, ns * S)
                            ins = v.tensor_scalar(O[:, c, cols], X[:, c, cols], MDS[:, l, kind, c, ns - 1:ns],
                                                  MOD[:, k, shift + c, ns - 1:ns], ALU.mult, ALU.add)
                        ins.then_inc(t_ready, 1)
                    if step == BEGIN + lag and L is not None:
                        begin(L, ahead)
                    c = step - lag - 2
                    if c >= 0:
                        n["hh"] += 1
                        dve.wait_ge(hh_ready, n["hh"])
                        v.tensor_tensor(HL[:, c, 0:w], O[:, c, 0:w], HH[:, c, 0:w].bitcast(F32),
                                        ALU.subtract).then_inc(h_ready, 1)

            def residual(name, w):
                def one(at):
                    dve.wait_ge(*at.emptied())
                    xs = X[:, at.g, 0:w]
                    v.scalar_tensor_tensor(xs, xs, ALPHA, TMP[:, at.u % 2, 0:w], ALU.mult, ALU.add).then_inc(row_ready, 1)

                products(name, one)
                n["row"] += KC
                dve.wait_ge(row_ready, n["row"])

            def centre(buf, chunks, w, scale):
                n["stat"] += 1
                dve.wait_ge(stat_done, n["stat"])
                for c in range(chunks):
                    v.scalar_tensor_tensor(buf[:, c, 0:w], bank[2][:, 0:w], -scale, buf[:, c, 0:w], ALU.mult,
                                           ALU.add).then_inc(cent_ready, 1)
                n["cent"] += chunks
                dve.wait_ge(cent_ready, n["cent"])

            def inverse(w, slot=0):
                n["root"] += 1
                n["stat"] += 1
                dve.wait_ge(root_ready, n["root"])
                own.link(v.reciprocal(ROOT[slot][:, 0:w], ROOT[slot][:, 0:w]))

            def normed(buf, chunks, w):
                for c in range(chunks):
                    v.tensor_tensor(buf[:, c, 0:w], buf[:, c, 0:w], RS_[:, 0:w], ALU.mult).then_inc(norm_ready, 1)
                n["norm"] += chunks

            def layer_norm(w, modulation=None):
                centre(X, KC, w, 1.0 / D)
                inverse(w)
                if modulation is None:
                    normed(X, KC, w)
                else:
                    modulate(*modulation, before=lambda c: v.tensor_tensor(
                        X[:, c, 0:w], X[:, c, 0:w], RS_[:, 0:w], ALU.mult).then_inc(norm_ready, 1))
                    n["norm"] += KC
                n["x"] += KC
                dve.wait_ge(x_ready, n["x"])

            def rope(chunk):
                n["rope"] += 1
                dve.wait_ge(rope_mm, n["rope"])
                t = TMP[:, n["rope"] % 2, 0:S]
                own.inc(v.tensor_tensor(t, bank[2 + n["rope"] % 2][:, 0:S], SIN, ALU.mult))
                own.link(v.tensor_tensor(chunk, chunk, COS, ALU.mult))
                v.tensor_tensor(chunk, chunk, t, ALU.add).then_inc(rope_done, 1)

            def low_out(c):
                w = TOK if n["layer"] == 0 else S
                low(lambda _: OH[:, 8 + c, :], lambda _: O[:, c, :], lambda _: OH[:, c, :], 1, w)

            def attend(name, lam=None, finish=None, opens=None):
                units = ATT[name]
                outs = OUTB[0:1] if units[0]["diff"] else OUTB
                spu = len(units[0]["subs"])
                j0, u0 = n["sub"], n["unit"]
                score_banks = 2 + spu

                def maxima(u):
                    unit = units[u]
                    w = unit["T"]
                    for i in range(spu):
                        j = u * spu + i
                        dve.wait_ge(sc_done, j0 + j + 1)
                        sc = SCORES[j % score_banks]
                        if unit["mask"] is not None:
                            own.link(v.tensor_tensor(sc[:, 0:S], sc[:, 0:S], unit["mask"], ALU.add))
                        m = smax[:, j % NS:j % NS + 1]
                        ins = v.reduce_max(m, sc[:, 0:w], AX_X, negate=True)
                        if unit["sink"] is not None:
                            own.link(ins)
                            k = unit["sink"]
                            ins = v.tensor_scalar(m, m, nsink[:, k:k + 1], None, ALU.min)
                        ins.then_inc(nm_ready, 1)

                def normalise(u):
                    unit = units[u]
                    w, j = unit["T"], u * spu
                    dve.wait_ge(ex_ready, j0 + j + spu)
                    cols = slice(j % NS, j % NS + spu)
                    if unit["sink"] is not None:
                        own.link(v.tensor_tensor(ssum[:, cols], ssum[:, cols], ssink[:, cols], ALU.add))
                    own.link(v.reciprocal(srec[:, cols], ssum[:, cols]))
                    p0, r0 = PROB[j % 6][:, 0:w], srec[:, j % NS:j % NS + 1]
                    if not unit["diff"]:
                        v.tensor_scalar(p0, p0, r0, None, ALU.mult).then_inc(pr_ready, 1)
                        return
                    p1, r1 = PROB[(j + 1) % 6][:, 0:w], srec[:, j % NS + 1:j % NS + 2]
                    own.inc(v.tensor_tensor(r1, r1, lam, ALU.mult))
                    own.link(v.tensor_scalar(p0, p0, r0, None, ALU.mult))
                    v.scalar_tensor_tensor(p1, p1, r1, p0, ALU.mult, ALU.add).then_inc(pr_ready, 1)

                def store(u):
                    dve.wait_ge(pv_done, u0 + u + 1)
                    v.tensor_copy(units[u]["out"], outs[u % len(outs)][units[u]["rows"], 0:P]).then_inc(o_ready, 1)

                for u in range(AHEAD):
                    maxima(u)
                normalise(0)
                for u in range(len(units)):
                    if u + AHEAD < len(units):
                        maxima(u + AHEAD)
                    if u + 1 < len(units):
                        normalise(u + 1)
                    if u:
                        store(u - 1)
                    c = chunk_over(name, u - 3)
                    if finish is not None and c is not None:
                        finish(c)
                store(len(units) - 1)
                n["sub"] += len(units) * spu
                n["unit"] += len(units)
                if opens is not None:
                    begin(LIN[opens], ahead)
                if not units[0]["diff"]:
                    for part in BESIDE[name]:
                        mod_store(part)
                dve.wait_ge(o_ready, n["unit"])

            v.memset(small[:, 0:1], LN_EPS).then_inc(small_ready, 1)
            v.memset(small[:, 1:2], RMS_EPS).then_inc(small_ready, 1)
            dve.wait_ge(vec_in, 32)
            v.tensor_scalar(nsink[:, :], vcol(1, V1["sink"], 16), -1.0, None, ALU.mult).then_inc(small_ready, 1)
            v.tensor_scalar(small[:, 13:14], vcol(0, V1["q_gain"]), SCALE, None, ALU.mult).then_inc(small_ready, 1)
            dve.wait_ge(small_ready, 4)
            dve.wait_ge(lam_in, 16)
            for l in range(2):
                own.link(v.tensor_tensor(LAM[:, l, 0:2, :], LAM[:, l, 0:2, :], LAM[:, l, 2:4, :], ALU.mult))
                v.tensor_reduce(small[:, 2 + 2 * l:4 + 2 * l], LAM[:, l, 0:2, :], AX_X, ALU.add).then_inc(lam_ready, 1)
            for l in range(2):
                dve.wait_ge(lam_exp, l + 1)
                e = 6 + 2 * l
                own.link(v.tensor_tensor(small[:, 10 + l:11 + l], small[:, e + 1:e + 2], small[:, e:e + 1], ALU.subtract))
                own.link(v.tensor_scalar(small[:, 10 + l:11 + l], small[:, 10 + l:11 + l], -LAM_INIT[l], None, ALU.add))
            mod_store("1_0_0")
            for l in range(2):
                w, ns = (TOK, 2) if l == 0 else (S, 1)
                n["layer"] = l
                if l == 0:
                    dve.wait_ge(x_in, 16)
                    modulate(0, 0, 0, 0, 2, False, LIN["ev_qk"])
                    products("ev_qk")
                    dve.wait_ge(bias_in, 16 * (8 * 4))
                    dve.wait_ge(mask_in, 32)

                    def head_norm(at):
                        g = at.g
                        for h in range(2 * g, min(2 * g + 2, 8)):
                            v.tensor_tensor(BIAS[:, h, :, :], BIAS[:, h, :, :], MASKB, ALU.add).then_inc(bias_ready, 1)
                        if g >= 2:
                            rope(G[:, g - 2, 0:S])
                        gain = small[:, 13:14] if g < 4 else vcol(0, V1["k_gain"])
                        dve.wait_ge(hroot_ready, g + 1)
                        own.link(v.reciprocal(RS_[:, :], RS_[:, :]))
                        v.scalar_tensor_tensor(G[:, g, :], G[:, g, :], gain, RS_[:, :], ALU.mult,
                                               ALU.mult).then_inc(hnorm_done, 1)

                    products("ev_v", head_norm)
                    rope(G[:, 3, 0:S])
                    rope(G[:, 4, 0:S])
                    dve.wait_ge(bias_ready, 8)
                    attend("global", finish=low_out)
                    attend("near", finish=low_out, opens="mix1_0")
                else:
                    products("od_k")
                    products("od_v")
                    products("od_q")
                    for j in range(9):
                        rope(G[:, j, 0:S])
                    attend("window", finish=low_out, opens="mix1_1")
                low_out(KC - 1)
                residual(f"mix1_{l}", w)
                L = LIN[f"up1_{l}"]
                layer_norm(w, (l, l, 1, 24, ns, False))

                def product_last(u, count):
                    dve.wait_ge(sig_ready, count)
                    v.tensor_tensor(SC[:, u, 0:w], SC[:, u, 0:w], SC[:, u + 1, 0:w], ALU.mult).then_inc(prod_ready, 1)

                def low_last(f, u, count):
                    dve.wait_ge(fh_ready, count)
                    v.tensor_tensor(FL[:, bass.ds(f - 1, 1), 0:w], SC[:, u:u + 1, 0:w],
                                    FH[:, bass.ds(f - 1, 1), 0:w].bitcast(F32), ALU.subtract).then_inc(hid_ready, 1)

                def conv3(at):
                    f, first = at.over(2), isinstance(at.g, int) and at.g < 2
                    dve.wait_ge(tap_ready, at.g + (n["tap"] + 1))
                    y, u = streams(SC[:, at.u, 0:w], ns), streams(bank[at.u % 2][:, 0:w], ns)
                    v.scalar_tensor_tensor(y[:, :, 1:S], u[:, :, 0:S - 1], vcol(l, at.g + V1["conv_w"]),
                                           y[:, :, 1:S], ALU.mult, ALU.add).then_inc(tap_left, 1)
                    dve.wait_ge(tap_left, at.g + (n["tap"] + 1))
                    v.scalar_tensor_tensor(y[:, :, 0:S - 1], u[:, :, 1:S], vcol(l, at.g + (V1["conv_w"] + 4 * FC)),
                                           y[:, :, 0:S - 1], ALU.mult, ALU.add).then_inc(emptied["vector"], 1)
                    if first:
                        return
                    if at.u % 2 == 0:
                        product_last((at.u + 2) % 4, f + n["sig"])
                    else:
                        low_last(f, (at.u + 1) % 4, f + n["fh"])

                products(f"up1_{l}", conv3)
                product_last(2, n["sig"] + FC)
                low_last(FC, 2, n["fh"] + FC)
                n["tap"] += 2 * FC
                n["sig"] += FC
                n["fh"] += FC
                residual(f"down1_{l}", w)
                layer_norm(w, (1, 1, 0, 0, 2, False) if l == 0 else None)
            for l in range(2):
                w, ns = (TOK, 2) if l == 0 else (S, 1)
                minus_lam = small[:, 10 + l:11 + l]
                dve.wait_ge(vec_in, 16 * (3 + l))
                own.link(v.tensor_scalar(small[:, 12:13], vcol(l, V2["subln_g"]), 1.0 - LAM_INIT[l], None, ALU.mult))
                if l == 0:
                    dve.wait_ge(ctx_in, 16)
                own.link(v.memset(U_, 0.0))
                inverse(TOK)
                if l == 1:
                    mod_store("2_1_0")
                modulate(l, 2 + l, 0, 0, 2, True, LIN[f"glu_{l}"])
                def unit(at):
                    if at.u % 2:
                        i = at.g // 2
                        dve.wait_ge(slab_done, at.full())
                        dve.wait_ge(*At(at.L, at.g - 1, (at.g - 1) % 4, None).emptied())
                        v.tensor_tensor(U[:, i, 0:ns, CONV_PAD:CONV_PAD + S], streams(bank[1][:, 0:w], ns),
                                        streams(TMP[:, i % 2, 0:w], ns), ALU.mult).then_inc(emptied["vector"], 1)

                products(f"glu_{l}", unit)
                dve.wait_ge(emptied["vector"], LIN[f"glu_{l}"].empty0["vector"] + 4)
                if l == 0:
                    mod_store("2_0_1")

                def cvs(c):
                    return streams(CV[:, c, 0:w], ns)

                for c in range(4):
                    v.tensor_scalar(cvs(c), U[:, c, 0:ns, 0:S], vcol(l, V2["conv_w"] + c * CONV_TAPS),
                                    vcol(l, V2["conv_b"] + c), ALU.mult, ALU.add).then_inc(tap_done, 1)
                base = n["taps"]
                n["taps"] += 4 * (CONV_TAPS - 1)
                todo = list(enumerate(TAPS))

                def taps(count):
                    for i, (k, c) in todo[:count]:
                        dve.wait_ge(tap_done, base + i + 1)
                        ins = v.scalar_tensor_tensor(cvs(c), U[:, c, 0:ns, k:k + S], vcol(l, V2["conv_w"] + c * CONV_TAPS + k),
                                                     cvs(c), ALU.mult, ALU.add)
                        ins.then_inc(tap_done if k < CONV_TAPS - 1 else conv_ready, 1)
                    del todo[:count]

                products(f"p_{l}")
                products(f"q_{l}", lambda at: taps(TAP_SHARE[l]["q"]))

                def beside(share, first):
                    def one(at):
                        taps(TAP_SHARE[l][share])
                        rope(QK[:, first + at.g, 0:S])
                    return one

                products(f"k_{l}", beside("k", 0))
                products(f"v_{l}", beside("v", 8))
                dve.wait_ge(rope_done, n["rope"])
                products(f"gate_{l}_0", lambda at: taps(TAP_SHARE[l]["gate"]))
                assert not todo
                dve.wait_ge(conv_ready, 4 * (l + 1))
                centre(CV, 4, w, 1.0 / 512)
                products(f"gate_{l}_1")
                inverse(w)
                normed(CV, 4, w)
                products(f"gate_{l}_2")
                attend(f"diff_{l}", minus_lam)

                def low_merged(c):
                    low(lambda _: HL[:, c, :], lambda _: G[:, c, :], lambda _: HH[:, c, :], 1, w)

                def gate_product(at, c, space):
                    dve.wait_ge(slab_done, at.full())
                    t = G[:, space, 0:w]
                    v.tensor_tensor(t, bank[at.u % 2][:, 0:w], t, ALU.mult).then_inc(emptied["vector"], 1)
                    if space == c:
                        return
                    dve.wait_ge(*at.emptied())
                    m = G[:, c, 0:w]
                    v.tensor_tensor(m, m, t, ALU.add).then_inc(merge_step, 1)

                def branch(at):
                    h = at.g // 2
                    gate_product(at, h, h + 16 * (at.g % 2))
                    if at.g % 2 == 0:
                        inverse(w)
                        v.scalar_tensor_tensor(O[:, h, 0:w], O[:, h, 0:w], small[:, 12:13], RS_[:, 0:w],
                                               ALU.mult, ALU.mult).then_inc(norm_ready, 1)
                    else:
                        low(lambda _: OH[:, 8 + h, :], lambda _: O[:, h, :], lambda _: OH[:, h, :], 1, w)

                turns(dve, LIN[f"branch_{l}"], branch)
                n["norm"] += 8
                begin(LIN[f"merge_{l}"], ahead)
                mod_store(BESIDE[f"diff_{l}"][0])
                dve.wait_ge(merge_step, n["merge"] + 8)

                def merge(at):
                    gate_product(at, at.g, at.g + 8)
                    if at.g:
                        low_merged(at.g - 1)

                products(f"merge_{l}", merge)
                low_merged(7)
                n["merge"] += 16

                def post_norm(k, y):
                    inverse(w)
                    for c in range(KC):
                        own.inc(v.tensor_tensor(y[:, c, 0:w], y[:, c, 0:w], RS_[:, 0:w], ALU.mult))
                    for c in range(KC):
                        own.wait(own.n - KC + 1 + c)
                        for s in range(ns):
                            cols = slice(s * S, s * S + S)
                            ins = v.scalar_tensor_tensor(X[:, c, cols], y[:, c, cols], MDS[:, l, k, c, s:s + 1], X[:, c, cols],
                                                         ALU.mult, ALU.add)
                        ins.then_inc(x_ready, 1)
                    n["x"] += KC
                    dve.wait_ge(x_ready, n["x"])

                products(f"out_{l}")
                post_norm(2, QK)
                inverse(w)
                L = LIN[f"up2_{l}"]
                if l == 1:
                    mod_store("2_1_2")
                modulate(l, 2 + l, 1, 24, ns, True, L if l == 1 else None)

                def low_last(f, u, count):
                    dve.wait_ge(fh_ready, count)
                    v.tensor_tensor(FL[:, bass.ds(f - 1, 1), 0:w], SC[:, u:u + 1, 0:w],
                                    FH[:, bass.ds(f - 1, 1), 0:w].bitcast(F32), ALU.subtract).then_inc(hid_ready, 1)

                def hidden(at):
                    f = at.over(2)
                    if at.u % 2:
                        if not (isinstance(at.g, int) and at.g < 2):
                            low_last(f, (at.u + 1) % 4, f + n["fh"])
                        dve.wait_ge(slab_done, at.full())
                        dve.wait_ge(emptied["scalar"], f + (at.L.empty0["scalar"] + 1))
                        v.tensor_tensor(SC[:, at.u - 1, 0:w], bank[1][:, 0:w], SC[:, at.u - 1, 0:w],
                                        ALU.mult).then_inc(emptied["vector"], 1)

                products(f"up2_{l}", hidden)
                low_last(FC, 2, n["fh"] + FC)
                n["fh"] += FC
                products(f"down2_{l}")
                post_norm(3, HS)

        @block.gpsimd
        def _(pool):
            g = nc.gpsimd
            n = Tally()
            own = Own(pool, pool_step)
            pool.dma_start(con[:, :], T["consts"]).then_inc(const_in, 16)
            pool.dma_start(TMP_[:, 0:8 * HD], T["lam"]).then_inc(lam_in, 16)
            pool.dma_start(vec[:, 0:NV1], T["vecs1"][0]).then_inc(vec_in, 16)
            pool.dma_start(vec[:, NV:NV + NV1], T["vecs1"][1]).then_inc(vec_in, 16)
            pool.dma_start(X[:, :, :], T["x"]).then_inc(x_in, 16)
            pool.wait_ge(h_ready, 1)
            pool.dma_start(MASKB, T["masks"][0]).then_inc(mask_in, 16)
            pool.dma_start(MASKC, T["masks"][1]).then_inc(mask_in, 16)
            rpb = T["rpb"]
            wide = rpb.shape[2] // GRID_W
            for h in range(8):
                for qt in range(2):
                    for r in range(2):
                        row = 2 * qt + r
                        src = bass.AP(rpb.tensor, (h * 15 + 7 - row) * GRID_W * wide + wide // 2,
                                      [[wide - 1, GRID_W], [GRID_W * wide, 4], [1, GRID_W]])
                        dst = BIAS[GRID_W * r:GRID_W * r + GRID_W, h, qt, :].rearrange("p (k c) -> p k c", k=4)
                        pool.dma_start(dst, src).then_inc(bias_in, 16)

            def sum_rows(l, first):
                w = TOK if l == 0 else S
                acc = HS[:, 0, 0:w]
                pool.wait_ge(row_ready, first + 2)
                own.link(g.tensor_tensor(acc, X[:, 0, 0:w], X[:, 1, 0:w], ALU.add))
                for c in range(2, KC):
                    pool.wait_ge(row_ready, first + c + 1)
                    ins = g.tensor_tensor(acc, acc, X[:, c, 0:w], ALU.add)
                    if c < KC - 1:
                        own.link(ins)
                ins.then_inc(presum, 1)

            def sum_squares(name, sq):
                L = LIN[name]
                acc = sq[:, 0, 0:L.n]
                for c in range(1, KC):
                    pool.wait_ge(emptied["scalar"], L.empty0["scalar"] + c + 1)
                    ins = g.tensor_tensor(acc, acc, sq[:, c, 0:L.n], ALU.add)
                    if c < KC - 1:
                        own.link(ins)
                ins.then_inc(presum, 1)

            for l in range(2):
                if l == 1:
                    pool.wait_ge(h_ready, 4 * KC)
                    pool.dma_start(X[:, :, S:TOK], T["ctx2"]).then_inc(ctx_in, 16)
                sum_rows(l, 16 * l)
                sum_rows(l, 16 * l + 8)
                pool.wait_ge(x_ready, 16 * (l + 1))
                pool.dma_start(vec[:, l * NV:l * NV + NV2], T["vecs2"][l]).then_inc(vec_in, 16)
            for l in range(2):
                ns = 2 - l
                pool.wait_ge(h_ready, 2 * 3 * KC + KC + 4 * KC * l)
                g.memset(PADS, 0.0).then_inc(pad_ready, 1)
                L = LIN[f"p_{l}"]
                for i in range(4):
                    pool.wait_ge(emptied["scalar"], L.empty0["scalar"] + i + 1)
                    src, width, last = PP[:, i, 0:ns, :], PW, 1
                    for d in range(i + 1):
                        dst = (PT0, PT1)[d % 2][:, 0:ns, :]
                        width -= last
                        own.link(g.tensor_tensor(dst[:, :, 0:width], src[:, :, 0:width], src[:, :, last:last + width], ALU.add))
                        src, last = dst, 2 * last
                    half = POOL_WINDOWS[i] // 2
                    win = src[:, :, POOL_PAD - half:POOL_PAD - half + S]
                    out = streams(PM[:, i, 0:ns * S], ns)
                    own.link(g.tensor_scalar(out, win, 1.0 / POOL_WINDOWS[i], None, ALU.mult))
                    for e in range(2):
                        cols = slice(0, POOL_PAD) if e == 0 else slice(S - POOL_PAD, S)
                        at = C_EDGE + (2 * i + e) * POOL_PAD
                        for s in range(ns):
                            own.inc(g.tensor_tensor(out[:, s, cols], out[:, s, cols], con[:, at:at + POOL_PAD], ALU.mult))
                    own.wait(own.n)
                    g.tensor_tensor(out, out, PP[:, i, 0:ns, POOL_PAD:POOL_PAD + S], ALU.subtract).then_inc(pool_ready, 1)
                sum_squares(f"out_{l}", QK[:, 8:16, :])
                sum_squares(f"down2_{l}", O)


def kernel(**inputs):
    import concourse.bacc as bacc
    from concourse.bass_utils import run_bass_kernel_spmd

    a = {k: np.asarray(v) for k, v in inputs.items()}

    def by_feature(x):
        return x.T.reshape(-1, P, x.shape[0]).transpose(1, 0, 2)

    def cols(x):
        return x.reshape(-1, P).T

    def pack(w, order=None):
        k, m = w.shape
        t = w.reshape(k // P, P, m // P, P).transpose(2, 1, 0, 3)
        if order is not None:
            t = t[order]
        return t.reshape(t.shape[0], P, k)

    def zip_groups(n):
        return [i + n * j for i in range(n) for j in range(2)]

    def paired(w, heads, axis):
        shape = w.shape
        t = w.reshape(shape[:axis] + (heads, HD) + shape[axis + 1:])
        order = [i + heads // 2 * j for i in range(heads // 2) for j in range(2)]
        return np.take(t, order, axis).reshape(shape)

    arrays = {}
    x = np.concatenate([by_feature(a["x"][0]), by_feature(a["ctx"][0])], 2)
    arrays["x"] = x
    arrays["ctx2"] = by_feature(a["ctx_2"][0])
    arrays["cvecs"] = np.concatenate([np.stack([cols(a["c" + s][0]), cols(a["c_ctx" + s])], 2).reshape(P, 16)
                                      for s in ("", "_2")], 1)
    ew, eo = a["ev_w_in"][0], a["ev_w_out"][0]
    ev = np.concatenate([paired(ew[:, 0:512], 8, 1), ew[:, 512:]], 1)
    arrays["w_ev_qk"] = pack(ev, [0, 1, 2, 3, 4, 6, 7, 8, 9, 10, 11, 12, 13])
    arrays["w_ev_v"] = pack(ev, [5, 14, 15, 16, 17])
    arrays["w_mix1_0"] = pack(np.concatenate([paired(eo[0:512], 8, 0), eo[512:]], 0))
    ow = a["od_w_in"][0]
    arrays["w_od_q"] = pack(paired(ow[:, 0:D], 16, 1))
    arrays["w_od_k"] = pack(ow[:, D:D + P])
    arrays["w_od_v"] = pack(ow[:, D + P:])
    arrays["w_mix1_1"] = pack(paired(a["od_w_out"][0], 16, 0))
    vecs1, vecs2 = [], []
    two = zip_groups(FC)
    for l in range(2):
        for b, w in ((1, a["ada_w"][l]), (2, a["w_mod_2"][l])):
            t = w.reshape(4, 2, P, 12, 512).transpose(3, 0, 2, 1, 4).reshape(12, 4, P, 2 * 512)
            for i in range(3):
                arrays[f"w_mod{b}_{l}_{i}"] = t[4 * i:4 * i + 4]
        arrays[f"w_up1_{l}"] = pack(a["ffn_w_up"][l], two)
        arrays[f"w_down1_{l}"] = pack(a["ffn_w_down"][l])
        wide = lambda v: np.broadcast_to(v, (P, v.shape[-1]))
        vecs1.append(np.concatenate(
            [cols(a["ada_b"][l]), cols(a["ln_g"][l]), cols(a["ln_b"][l])]
            + [cols(a["ffn_conv_w"][l, j])[:, two] for j in range(3)]
            + [cols(a["ffn_conv_b"][l])[:, two]]
            + [np.concatenate([a[k][0], a[k][0]])[:, None] for k in ("ev_q_gain", "ev_k_gain")]
            + [wide(a["od_sink"][0])], 1))
        w = a["w_in_2"][l]
        arrays[f"w_glu_{l}"] = pack(w[:, 0:1024], [i + 4 * j for i in range(4) for j in (1, 0)])
        for k, (lo, hi) in dict(q=(1024, 2048), k=(2048, 3072), v=(3072, 4096), p=(4096, 4608), gate=(4608, 7680)).items():
            arrays[f"w_{k}_{l}"] = pack(w[:, lo:hi])
        gates = arrays.pop(f"w_gate_{l}")
        for i, first in enumerate(GATES):
            arrays[f"w_gate_{l}_{i}"] = gates[first:first + 8]
        arrays[f"w_group_{l}"] = a["w_pool_group_2"][l]
        conv, att, pool = (pack(a[k][l]) for k in ("w_conv_out_2", "w_attn_out_2", "w_pool_out_2"))
        arrays[f"w_branch_{l}"] = np.stack([conv, pool], 1).reshape(16, P, D // 2)
        arrays[f"w_merge_{l}"] = att
        arrays[f"w_out_{l}"] = pack(a["w_out_2"][l])
        arrays[f"w_up2_{l}"] = pack(a["w_ffn_in_2"][l], two)
        arrays[f"w_down2_{l}"] = pack(a["w_ffn_out_2"][l])
        vecs2.append(np.concatenate(
            [cols(a["b_mod_2"][l])] + [cols(a[k + "_2"][l]) for k in ("g_pre_mix", "g_post_mix", "g_pre_ffn", "g_post_ffn")]
            + [cols(a["b_gate_2"][l]), a["conv_w_2"][l].T.reshape(4, P, CONV_TAPS).transpose(1, 0, 2).reshape(P, -1)]
            + [cols(a[k + "_2"][l]) for k in ("conv_b", "conv_ln_g", "conv_ln_b", "subln_g", "pool_scale")], 1))
    arrays["vecs1"], arrays["vecs2"] = np.stack(vecs1), np.stack(vecs2)
    arrays["lam"] = np.broadcast_to(
        np.concatenate([a[k + "_2"][l] for l in range(2) for k in ("lam_q1", "lam_q2", "lam_k1", "lam_k2")]), (P, 8 * HD))
    pad = GRID_W - 16
    arrays["rpb"] = np.tile(np.pad(a["ev_rpb"][0], ((0, 0), (0, 0), (pad, pad))), (1, 1, GRID_W))

    t = np.arange(S)
    half = HD // 2
    freq = (10000.0 ** (-np.arange(0, half, 2, dtype=np.float32) / np.float32(half))).astype(np.float32)
    by_row = (t // GRID_W).astype(np.float32)[:, None] * freq
    by_col = (t % GRID_W).astype(np.float32)[:, None] * freq
    ang = np.concatenate([by_row, by_row, by_col, by_col], 1).T
    rot = np.zeros((P, P), np.float32)
    for i in range(P):
        low = i % half < half // 2
        rot[i + half // 2 if low else i - half // 2, i] = -1.0 if low else 1.0
    head = np.kron(np.eye(2), np.ones((HD, HD)))
    edge = []
    for w in POOL_WINDOWS:
        count = np.clip(t + w // 2, 0, S) - np.clip(t - w // 2, 0, S)
        edge += [w / count[:POOL_PAD], w / count[-POOL_PAD:]]
    arrays["consts"] = np.concatenate(
        [np.tile(np.cos(ang), (2, 1)), np.tile(np.sin(ang), (2, 1)), np.ones((P, P)), np.eye(P), rot, head,
         np.broadcast_to(np.concatenate(edge), (P, 8 * POOL_PAD))], 1).astype(np.float32)
    col = t % GRID_W
    first = np.clip(col - 8, 0, GRID_W - 16)
    near = (col[None, :] >= first[:, None]) & (col[None, :] < first[:, None] + 16)
    window = np.abs(t[None, :] - t[:, None]) <= 128
    arrays["masks"] = np.stack([np.where(m, 0.0, NEG).astype(np.float32).reshape(2, P, S).transpose(1, 0, 2)
                                for m in (near, window)])

    nc = bacc.Bacc("TRN2", target_bir_lowering=False, num_devices=1)
    tensors, fed = {}, {}
    for k, v in arrays.items():
        v = np.ascontiguousarray(v)
        fed["in_" + k] = v
        tensors[k] = nc.dram_tensor("in_" + k, v.shape, F32, kind="ExternalInput").ap()
    tensors["out"] = nc.dram_tensor("out", (P, KC, S), F32, kind="ExternalOutput").ap()
    build(nc, tensors)
    r = run_bass_kernel_spmd(nc, [fed], core_ids=[0])
    y = r.results[0]["out"]
    return np.ascontiguousarray(y.transpose(2, 1, 0).reshape(1, S, D))
```
